# Optimizing a Trainium2 kernel written in Bass

```python
import math
import jax, jax.numpy as jnp
from jax import lax
import numpy as np

D_MODEL = 1024
BATCH = 1
SEQ = 256
DEPTH = 2

N_MIXERS = 3
N_HEADS = 8
HEAD_DIM = D_MODEL // N_HEADS
ROT_DIM = HEAD_DIM // 4
ROPE_THETA = 500000.0
MOBA_BLOCK = 256
MOBA_TOPK = 3
Q_CHUNK = 16
POOL_WINDOWS = (2, 4, 8, 16)
N_POOL_GROUPS = len(POOL_WINDOWS)
POOL_GROUP_DIM = D_MODEL // N_POOL_GROUPS
CONV_WIDTH = 3
D_FF = 4 * D_MODEL
NORM_EPS = 1e-6
NEG_INF = -1e30


def rms_norm(x, g):
    xf = x.astype(jnp.float32)
    y = xf * lax.rsqrt(jnp.mean(xf * xf, axis=-1, keepdims=True) + NORM_EPS)
    return (y * g.astype(jnp.float32)).astype(x.dtype)

def rope_tables(positions):
    inv_freq = ROPE_THETA ** (-jnp.arange(0, ROT_DIM, 2, dtype=jnp.float32) / ROT_DIM)
    ang = positions.astype(jnp.float32)[..., None] * inv_freq
    return jnp.cos(ang)[:, None], jnp.sin(ang)[:, None]

def apply_partial_rope(t, cos, sin):
    half = ROT_DIM // 2
    rot = t[..., :ROT_DIM].astype(jnp.float32)
    x1, x2 = rot[..., :half], rot[..., half:]
    rotated = jnp.concatenate([x1 * cos - x2 * sin, x2 * cos + x1 * sin], axis=-1)
    return jnp.concatenate([rotated.astype(t.dtype), t[..., ROT_DIM:]], axis=-1)

def moba_attention(xn, w_qkv, w_o, cos, sin):
    b, s, _ = xn.shape
    qkv = (xn @ w_qkv).reshape(b, s, 3, N_HEADS, HEAD_DIM)
    q, k, v = [jnp.transpose(qkv[:, :, i], (0, 2, 1, 3)) for i in range(3)]
    q = apply_partial_rope(q, cos, sin)
    k = apply_partial_rope(k, cos, sin)

    n_blocks = -(-s // MOBA_BLOCK)
    top_k = min(MOBA_TOPK, n_blocks)
    pad = n_blocks * MOBA_BLOCK - s
    kp = jnp.pad(k, ((0, 0), (0, 0), (0, pad), (0, 0)))
    vp = jnp.pad(v, ((0, 0), (0, 0), (0, pad), (0, 0)))
    kb = kp.reshape(b, N_HEADS, n_blocks, MOBA_BLOCK, HEAD_DIM)
    vb = vp.reshape(b, N_HEADS, n_blocks, MOBA_BLOCK, HEAD_DIM)
    k_mean = jnp.mean(kb.astype(jnp.float32), axis=3)

    scale = 1.0 / math.sqrt(HEAD_DIM)
    bi = jnp.arange(b)[:, None, None, None]
    hi = jnp.arange(N_HEADS)[None, :, None, None]
    blk_ids = jnp.arange(n_blocks)

    def chunk(c):
        start = c * Q_CHUNK
        qc = lax.dynamic_slice_in_dim(q, start, Q_CHUNK, axis=2)
        qpos = start + jnp.arange(Q_CHUNK)
        qblk = start // MOBA_BLOCK
        gate = jnp.einsum('bhqd,bhnd->bhqn', qc.astype(jnp.float32), k_mean)
        gate = jnp.where(blk_ids < qblk, gate, NEG_INF)
        _, sel = lax.top_k(gate, top_k)
        sel_valid = sel < qblk
        k_sel = kb[bi, hi, sel]
        v_sel = vb[bi, hi, sel]
        s_sel = jnp.einsum('bhqd,bhqnkd->bhqnk', qc, k_sel).astype(jnp.float32) * scale
        s_sel = jnp.where(sel_valid[..., None], s_sel, NEG_INF)
        s_sel = s_sel.reshape(b, N_HEADS, Q_CHUNK, top_k * MOBA_BLOCK)
        k_own = lax.dynamic_slice_in_dim(kp, qblk * MOBA_BLOCK, MOBA_BLOCK, axis=2)
        v_own = lax.dynamic_slice_in_dim(vp, qblk * MOBA_BLOCK, MOBA_BLOCK, axis=2)
        s_own = jnp.einsum('bhqd,bhkd->bhqk', qc, k_own).astype(jnp.float32) * scale
        kpos = qblk * MOBA_BLOCK + jnp.arange(MOBA_BLOCK)
        s_own = jnp.where(kpos[None, :] <= qpos[:, None], s_own, NEG_INF)
        p = jax.nn.softmax(jnp.concatenate([s_sel, s_own], axis=-1), axis=-1)
        p_sel = p[..., :top_k * MOBA_BLOCK].reshape(
            b, N_HEADS, Q_CHUNK, top_k, MOBA_BLOCK).astype(v.dtype)
        p_own = p[..., top_k * MOBA_BLOCK:].astype(v.dtype)
        return (jnp.einsum('bhqnk,bhqnkd->bhqd', p_sel, v_sel)
                + jnp.einsum('bhqk,bhkd->bhqd', p_own, v_own))

    outs = lax.map(chunk, jnp.arange(s // Q_CHUNK))
    out = jnp.transpose(outs, (1, 0, 3, 2, 4)).reshape(b, s, D_MODEL)
    return out @ w_o

def pool_mixer(xn, w_groups, ls_scale):
    b, s, _ = xn.shape
    xf = xn.astype(jnp.float32).reshape(b, s, N_POOL_GROUPS, POOL_GROUP_DIM)
    cs = jnp.concatenate([jnp.zeros((b, 1, N_POOL_GROUPS, POOL_GROUP_DIM), jnp.float32),
                          jnp.cumsum(xf, axis=1)], axis=1)
    t = jnp.arange(s)
    pooled = []
    for g, w in enumerate(POOL_WINDOWS):
        c = cs[:, :, g]
        lower = jnp.pad(c[:, :s - w + 1], ((0, 0), (w - 1, 0), (0, 0)))
        count = jnp.minimum(t + 1, w).astype(jnp.float32)[None, :, None]
        pooled.append((c[:, 1:] - lower) / count)
    pooled = jnp.stack(pooled, axis=2) - xf
    y = jnp.einsum('bsgc,gcd->bsgd', pooled.astype(xn.dtype), w_groups)
    return y.reshape(b, s, D_MODEL) * ls_scale

def short_conv_mixer(xn, w_in, conv_w, w_out):
    u = xn @ w_in
    gate_b, gate_c, h = jnp.split(u, 3, axis=-1)
    z = gate_c * h
    zc = lax.conv_general_dilated(
        z, conv_w[:, None, :].astype(z.dtype), window_strides=(1,),
        padding=[(CONV_WIDTH - 1, 0)], dimension_numbers=('NWC', 'WIO', 'NWC'),
        feature_group_count=D_MODEL)
    return (gate_b * zc) @ w_out

def squared_relu_mlp(x, w_up, w_down):
    h = jax.nn.relu(x @ w_up)
    return (h * h) @ w_down

def first_inputs(seed: int = 0) -> dict:
    key = jax.random.key(seed)
    ks = jax.random.split(key, 16)
    n_attn = len(range(0, DEPTH, N_MIXERS))
    n_pool = len(range(1, DEPTH, N_MIXERS))
    n_conv = len(range(2, DEPTH, N_MIXERS))
    f32 = jnp.float32

    def nrm(k, shape, fan_in):
        return jax.random.normal(k, shape, f32) * (fan_in ** -0.5)

    x = jax.random.normal(ks[0], (BATCH, SEQ, D_MODEL), f32)
    positions = jnp.broadcast_to(jnp.arange(SEQ, dtype=jnp.int32), (BATCH, SEQ))
    norm_mix = 1.0 + 0.02 * jax.random.normal(ks[1], (DEPTH, D_MODEL), f32)
    norm_mlp = 1.0 + 0.02 * jax.random.normal(ks[2], (DEPTH, D_MODEL), f32)
    attn_w_qkv = nrm(ks[3], (n_attn, D_MODEL, 3 * D_MODEL), D_MODEL)
    attn_w_o = nrm(ks[4], (n_attn, D_MODEL, D_MODEL), D_MODEL)
    pool_w = nrm(ks[5], (n_pool, N_POOL_GROUPS, POOL_GROUP_DIM, POOL_GROUP_DIM), POOL_GROUP_DIM)
    pool_scale = 1.0 + 0.1 * jax.random.normal(ks[6], (n_pool, D_MODEL), f32)
    conv_w_in = nrm(ks[7], (n_conv, D_MODEL, 3 * D_MODEL), D_MODEL)
    conv_w = nrm(ks[8], (n_conv, CONV_WIDTH, D_MODEL), CONV_WIDTH)
    conv_w_out = nrm(ks[9], (n_conv, D_MODEL, D_MODEL), D_MODEL)
    mlp_w_up = nrm(ks[10], (DEPTH, D_MODEL, D_FF), D_MODEL)
    mlp_w_down = nrm(ks[11], (DEPTH, D_FF, D_MODEL), D_FF)
    norm_final = 1.0 + 0.02 * jax.random.normal(ks[12], (D_MODEL,), f32)
    return {"x": x, "positions": positions, "norm_mix": norm_mix, "norm_mlp": norm_mlp,
            "attn_w_qkv": attn_w_qkv, "attn_w_o": attn_w_o,
            "pool_w": pool_w, "pool_scale": pool_scale,
            "conv_w_in": conv_w_in, "conv_w": conv_w, "conv_w_out": conv_w_out,
            "mlp_w_up": mlp_w_up, "mlp_w_down": mlp_w_down, "norm_final": norm_final}

def first_block(x, positions, norm_mix, norm_mlp, attn_w_qkv, attn_w_o, pool_w, pool_scale,
              conv_w_in, conv_w, conv_w_out, mlp_w_up, mlp_w_down, norm_final):
    cos, sin = rope_tables(positions)
    i_attn = i_pool = i_conv = 0
    for i in range(DEPTH):
        xn = rms_norm(x, norm_mix[i])
        kind = i % N_MIXERS
        if kind == 0:
            y = moba_attention(xn, attn_w_qkv[i_attn], attn_w_o[i_attn], cos, sin)
            i_attn += 1
        elif kind == 1:
            y = pool_mixer(xn, pool_w[i_pool], pool_scale[i_pool])
            i_pool += 1
        else:
            y = short_conv_mixer(xn, conv_w_in[i_conv], conv_w[i_conv], conv_w_out[i_conv])
            i_conv += 1
        x = x + y
        x = x + squared_relu_mlp(rms_norm(x, norm_mlp[i]), mlp_w_up[i], mlp_w_down[i])
    return rms_norm(x, norm_final)


CHUNK = 64
N_A_LAYERS = DEPTH // 2
N_B_LAYERS = DEPTH - N_A_LAYERS
MLA_HEADS = 8
Q_LORA = 384
KV_LORA = 256
NOPE_DIM = 128
ROPE_DIM = 64
V_DIM = 128
ROPE_THETA_2 = 10000.0
Q_BLOCK = 128
B_HEADS = 16
B_HEAD_DIM = 64
LEFT_CHUNKS = 8
BAND = (LEFT_CHUNKS + 1) * CHUNK
MAX_REL = 256
REL_TABLE = MAX_REL + CHUNK
D_FF_2 = -(-8 * D_MODEL // (3 * 256)) * 256
EPS = 1e-6


def rms_norm_2(x, g):
    xf = x.astype(jnp.float32)
    y = xf * lax.rsqrt(jnp.mean(xf * xf, axis=-1, keepdims=True) + EPS)
    return (y * g.astype(jnp.float32)).astype(x.dtype)

def rope_tables_2(positions, dtype):
    inv = 1.0 / (ROPE_THETA_2 ** (jnp.arange(0, ROPE_DIM, 2, dtype=jnp.float32) / ROPE_DIM))
    ang = positions.astype(jnp.float32)[..., None] * inv
    return jnp.cos(ang).astype(dtype), jnp.sin(ang).astype(dtype)

def apply_rope(t, cos, sin):
    t1, t2 = jnp.split(t, 2, axis=-1)
    return jnp.concatenate([t1 * cos - t2 * sin, t2 * cos + t1 * sin], axis=-1)

def swiglu(h, w_gate, w_up, w_down):
    return (jax.nn.silu(h @ w_gate) * (h @ w_up)) @ w_down

def mla_mixer(h, cos, sin, w_a, g_q, w_uq, g_kv, w_ukv, w_o):
    B, S, _ = h.shape
    a = h @ w_a
    cq, ckv, kr = jnp.split(a, [Q_LORA, Q_LORA + KV_LORA], axis=-1)
    q = (rms_norm_2(cq, g_q) @ w_uq).reshape(B, S, MLA_HEADS, NOPE_DIM + ROPE_DIM)
    q_nope = q[..., :NOPE_DIM]
    q_rope = apply_rope(q[..., NOPE_DIM:], cos[:, :, None], sin[:, :, None])
    kv = (rms_norm_2(ckv, g_kv) @ w_ukv).reshape(B, S, MLA_HEADS, NOPE_DIM + V_DIM)
    k_nope, v = kv[..., :NOPE_DIM], kv[..., NOPE_DIM:]
    k_rope = apply_rope(kr, cos, sin)
    scale = (NOPE_DIM + ROPE_DIM) ** -0.5
    n_blk = S // Q_BLOCK
    key_chunk = jnp.arange(S) // CHUNK

    def to_blocks(t):
        return jnp.moveaxis(t.reshape(B, n_blk, Q_BLOCK, *t.shape[2:]), 1, 0)

    def block_attn(args):
        qn, qr, blk = args
        s = (jnp.einsum('bqhd,bkhd->bhqk', qn, k_nope, preferred_element_type=jnp.float32)
             + jnp.einsum('bqhr,bkr->bhqk', qr, k_rope, preferred_element_type=jnp.float32)) * scale
        q_chunk = (blk * Q_BLOCK + jnp.arange(Q_BLOCK)) // CHUNK
        mask = key_chunk[None, :] <= q_chunk[:, None]
        s = jnp.where(mask[None, None], s, -jnp.inf)
        p = jax.nn.softmax(s, axis=-1).astype(v.dtype)
        return jnp.einsum('bhqk,bkhd->bqhd', p, v)

    o = lax.map(block_attn, (to_blocks(q_nope), to_blocks(q_rope), jnp.arange(n_blk)))
    o = jnp.moveaxis(o, 0, 1).reshape(B, S, MLA_HEADS * V_DIM)
    return o @ w_o

def gather_band(t):
    B, S = t.shape[:2]
    n_c = S // CHUNK
    tp = jnp.pad(t, ((0, 0), (LEFT_CHUNKS * CHUNK, 0), (0, 0), (0, 0)))
    tp = tp.reshape(B, n_c + LEFT_CHUNKS, CHUNK, *t.shape[2:])
    band = jnp.stack([tp[:, j:j + n_c] for j in range(LEFT_CHUNKS + 1)], axis=2)
    return band.reshape(B, n_c, BAND, *t.shape[2:])

def shared_kv(x, g_src, w_kv):
    B, S, _ = x.shape
    kv = (rms_norm_2(x, g_src) @ w_kv).reshape(B, S, 2, B_HEADS, B_HEAD_DIM)
    return gather_band(kv[:, :, 0]), gather_band(kv[:, :, 1])

def chunked_mixer(h, k_band, v_band, w_q, rel_table, w_o):
    B, S, _ = h.shape
    n_c = S // CHUNK
    q = (h @ w_q).reshape(B, n_c, CHUNK, B_HEADS, B_HEAD_DIM)
    dist = LEFT_CHUNKS * CHUNK + jnp.arange(CHUNK)[:, None] - jnp.arange(BAND)[None, :]
    idx = jnp.clip(dist, -(CHUNK - 1), MAX_REL) + (CHUNK - 1)
    bias = rel_table.astype(jnp.float32)[:, idx]
    valid = (jnp.arange(n_c)[:, None] - LEFT_CHUNKS + jnp.arange(BAND)[None, :] // CHUNK) >= 0
    s = jnp.einsum('bnqhd,bnkhd->bnhqk', q, k_band, preferred_element_type=jnp.float32)
    s = s * (B_HEAD_DIM ** -0.5) + bias[None, None]
    s = jnp.where(valid[None, :, None, None, :], s, -jnp.inf)
    p = jax.nn.softmax(s, axis=-1).astype(v_band.dtype)
    o = jnp.einsum('bnhqk,bnkhd->bnqhd', p, v_band).reshape(B, S, B_HEADS * B_HEAD_DIM)
    return o @ w_o

def second_inputs(seed: int = 0) -> dict:
    key = jax.random.key(seed)
    ks = iter(jax.random.split(key, 32))
    f32 = jnp.float32

    def w(shape, fan_in):
        return jax.random.normal(next(ks), shape, f32) * (fan_in ** -0.5)

    def gain(shape):
        return 1.0 + 0.05 * jax.random.normal(next(ks), shape, f32)

    x = jax.random.normal(next(ks), (BATCH, SEQ, D_MODEL), f32)
    offsets = jax.random.randint(next(ks), (BATCH, 1), 0, 4096, dtype=jnp.int32)
    positions = (jnp.arange(SEQ, dtype=jnp.int32)[None, :] + offsets).astype(jnp.int32)
    return {
        "x": x,
        "positions": positions,
        "attn_pre_g": gain((DEPTH, D_MODEL)),
        "attn_post_g": gain((DEPTH, D_MODEL)),
        "ffn_pre_g": gain((DEPTH, D_MODEL)),
        "ffn_post_g": gain((DEPTH, D_MODEL)),
        "ffn_w_gate": w((DEPTH, D_MODEL, D_FF_2), D_MODEL),
        "ffn_w_up": w((DEPTH, D_MODEL, D_FF_2), D_MODEL),
        "ffn_w_down": w((DEPTH, D_FF_2, D_MODEL), D_FF_2),
        "mla_w_a": w((N_A_LAYERS, D_MODEL, Q_LORA + KV_LORA + ROPE_DIM), D_MODEL),
        "mla_g_q": gain((N_A_LAYERS, Q_LORA)),
        "mla_w_uq": w((N_A_LAYERS, Q_LORA, MLA_HEADS * (NOPE_DIM + ROPE_DIM)), Q_LORA),
        "mla_g_kv": gain((N_A_LAYERS, KV_LORA)),
        "mla_w_ukv": w((N_A_LAYERS, KV_LORA, MLA_HEADS * (NOPE_DIM + V_DIM)), KV_LORA),
        "mla_w_o": w((N_A_LAYERS, MLA_HEADS * V_DIM, D_MODEL), MLA_HEADS * V_DIM),
        "kv_src_g": gain((D_MODEL,)),
        "w_kv_shared": w((D_MODEL, 2 * B_HEADS * B_HEAD_DIM), D_MODEL),
        "b_w_q": w((N_B_LAYERS, D_MODEL, B_HEADS * B_HEAD_DIM), D_MODEL),
        "b_rel_table": 0.2 * jax.random.normal(next(ks), (N_B_LAYERS, B_HEADS, REL_TABLE), f32),
        "b_w_o": w((N_B_LAYERS, B_HEADS * B_HEAD_DIM, D_MODEL), B_HEADS * B_HEAD_DIM),
    }

def second_block(x, positions, attn_pre_g, attn_post_g, ffn_pre_g, ffn_post_g,
              ffn_w_gate, ffn_w_up, ffn_w_down,
              mla_w_a, mla_g_q, mla_w_uq, mla_g_kv, mla_w_ukv, mla_w_o,
              kv_src_g, w_kv_shared, b_w_q, b_rel_table, b_w_o):
    cos, sin = rope_tables_2(positions, x.dtype)
    k_band = v_band = None
    for layer in range(DEPTH):
        h = rms_norm_2(x, attn_pre_g[layer])
        if layer < N_A_LAYERS:
            a = layer
            y = mla_mixer(h, cos, sin, mla_w_a[a], mla_g_q[a], mla_w_uq[a],
                          mla_g_kv[a], mla_w_ukv[a], mla_w_o[a])
        else:
            b = layer - N_A_LAYERS
            y = chunked_mixer(h, k_band, v_band, b_w_q[b], b_rel_table[b], b_w_o[b])
        x = x + rms_norm_2(y, attn_post_g[layer])
        h = rms_norm_2(x, ffn_pre_g[layer])
        f = swiglu(h, ffn_w_gate[layer], ffn_w_up[layer], ffn_w_down[layer])
        x = x + rms_norm_2(f, ffn_post_g[layer])
        if layer == N_A_LAYERS - 1:
            k_band, v_band = shared_kv(x, kv_src_g, w_kv_shared)
    return x


def setup_inputs(seed=0):
    out = dict(first_inputs(seed))
    for name, value in second_inputs(seed + 1).items():
        if name != "x":
            out[name + "_2"] = value
    return out


def reference(
    x, positions, norm_mix, norm_mlp, attn_w_qkv, attn_w_o, pool_w, pool_scale, conv_w_in,
    conv_w, conv_w_out, mlp_w_up, mlp_w_down, norm_final, positions_2, attn_pre_g_2,
    attn_post_g_2, ffn_pre_g_2, ffn_post_g_2, ffn_w_gate_2, ffn_w_up_2, ffn_w_down_2, mla_w_a_2,
    mla_g_q_2, mla_w_uq_2, mla_g_kv_2, mla_w_ukv_2, mla_w_o_2, kv_src_g_2, w_kv_shared_2,
    b_w_q_2, b_rel_table_2, b_w_o_2,
):
    x = first_block(
        x, positions, norm_mix, norm_mlp, attn_w_qkv, attn_w_o, pool_w, pool_scale, conv_w_in,
        conv_w, conv_w_out, mlp_w_up, mlp_w_down, norm_final,
    )
    return second_block(
        x, positions_2, attn_pre_g_2, attn_post_g_2, ffn_pre_g_2, ffn_post_g_2, ffn_w_gate_2,
        ffn_w_up_2, ffn_w_down_2, mla_w_a_2, mla_g_q_2, mla_w_uq_2, mla_g_kv_2, mla_w_ukv_2,
        mla_w_o_2, kv_src_g_2, w_kv_shared_2, b_w_q_2, b_rel_table_2, b_w_o_2,
    )


_drawn_inputs = setup_inputs


def setup_inputs(seed=0):
    import zlib

    import numpy as np

    out = dict(_drawn_inputs(seed))
    spreads = {}
    factors = {'norm_mix': 4.478, 'mla_g_q_2': 4.225, 'b_rel_table_2': 3.767}
    for name, (base, spread) in spreads.items():
        noise = np.random.default_rng([zlib.crc32(name.encode()), seed]).standard_normal(out[name].shape)
        drawn = base * np.exp(spread * noise) if base else spread * noise
        out[name] = __import__('jax').numpy.asarray(drawn.astype(out[name].dtype))
    for name, factor in factors.items():
        out[name] = (out[name] * factor).astype(out[name].dtype)
    return out
```

```python
from contextlib import ExitStack

import concourse.bass as bass
from concourse import mybir

F32 = mybir.dt.float32
F32R = mybir.dt.float32r
I32 = mybir.dt.int32
ALU = mybir.AluOpType
ACT = mybir.ActivationFunctionType

P = 128
T = 256
TT = T // P
D = 1024
KT = D // P
DFF1 = 4 * D
DFF2 = 2816
W = 2048
SLOTS = 4
HALF = 512
FC = 256
EPS = 1e-6
NEG = -1e30
MIN32 = -3.0e38
MAGIC = 12582912.0
INV_2PI = 0.15915494309189535
PI_A = 6.28125
PI_B = 0.0019350051879882812
PI_C = 2 * 3.141592653589793 - PI_A - PI_B
PI_SAFE = 3.1415925
HALF_PI = 1.5707963267948966
H1, HD1, ROT1 = 8, 128, 16
QL, KVL, ROT2 = 384, 256, 32
H2 = 16
REL = 320

C_IDENT, C_CAUSAL, C_CHUNKED, C_BAND, C_INV = 0, 128, 384, 640, 2176
NCONST = C_INV + ROT1 + ROT2

CHUNKS = []


def plan():
    def add(kind, n, width=W):
        first = len(CHUNKS)
        CHUNKS.extend((kind, i, width) for i in range(n))
        return first

    def mlp(layer):
        first = len(CHUNKS)
        n = DFF1 // FC
        CHUNKS.append(("up", (layer, 0), W))
        for i in range(1, n):
            CHUNKS.extend([("up", (layer, i), W), ("down", (layer, i - 1), W)])
        CHUNKS.append(("down", (layer, n - 1), W))
        return first

    def ffn(layer):
        first = len(CHUNKS)
        n = DFF2 // FC
        CHUNKS.extend([("gate2", (layer, 0), W), ("up2", (layer, 0), W)])
        for i in range(1, n):
            CHUNKS.extend([("gate2", (layer, i), W), ("up2", (layer, i), W), ("down2", (layer, i - 1), W)])
        CHUNKS.append(("down2", (layer, n - 1), W))
        return first

    at = {}
    at["qkv"] = add("qkv", 12)
    at["wo"] = add("wo", 4)
    at["mlp0"] = mlp(0)
    at["pool"] = add("pool", 1)
    at["mlp1"] = mlp(1)
    at["wa"] = add("wa", 4, 2 * 704)
    at["uq"] = add("uq", 4, 3 * 384)
    at["ukv"] = add("ukv", 2)
    at["mwo"] = add("mwo", 4)
    at["ffn0"] = ffn(0)
    at["kvk"] = add("kvk", 4)
    at["kvv"] = add("kvv", 4)
    at["bq"] = add("bq", 4)
    at["bwo"] = add("bwo", 4)
    at["ffn1"] = ffn(1)
    return at


AT = plan()
NCH = len(CHUNKS)
NM = DFF1 // FC
NF = DFF2 // FC


def place():
    ffn = {AT["ffn0"] + m for m in range(2, 3 * NF)} | {AT["ffn1"] + m for m in range(2, 3 * NF)}
    slot, prev, nth = [], [], []
    last = [-SLOTS + s for s in range(SLOTS)]
    count = [0] * SLOTS
    for c in range(NCH):
        s = slot[c - 3] if c in ffn else min(range(SLOTS), key=lambda q: last[q])
        slot.append(s)
        prev.append(max(last[s], -1))
        last[s] = c
        count[s] += 1
        nth.append(count[s])
    return slot, prev, nth


SLOT, PREV, NTH = place()

ROWS = ["mix0", "mlp0", "mix1", "pool_scale", "mlp1", "final", "pre0", "lora", "post0", "fpre0",
        "fpost0", "kvsrc", "pre1", "post1", "fpre1", "fpost1"]
ROW = {name: i for i, name in enumerate(ROWS)}
ROW_SLOTS = 3
NORMS = ["mix0", "mlp0", "mix1", "mlp1", "final", "pre0", "lora", "post0", "fpre0", "fpost0",
         "kvsrc", "post1", "fpre1", "fpost1"]
NORM = {name: i for i, name in enumerate(NORMS)}


def two_blocks(nc, a, out):
    with ExitStack() as ctx:
        def sb(name, shape, dt=F32):
            return ctx.enter_context(nc.sbuf_tensor(name, shape, dt))

        def sem(name):
            return ctx.enter_context(nc.semaphore(name))

        raw = sb("raw", [P, SLOTS, W])
        whi = sb("whi", [P, SLOTS, W], F32R)
        wlo = sb("wlo", [P, SLOTS, W], F32R)
        x = sb("x", [P, TT, D])
        xs = sb("xs", [P, TT, D])
        junk = sb("junk", [P, D])
        act_hi = sb("act_hi", [P, KT, T], F32R)
        act_lo = sb("act_lo", [P, KT, T], F32R)
        rows = sb("rows", [P, ROW_SLOTS, D])
        const = sb("const", [P, NCONST])
        arena = sb("arena", [P, 8192])
        hhi = sb("hhi", [P, 2, T], F32R)
        hlo = sb("hlo", [P, 2, T], F32R)
        pos_i = sb("pos_i", [P, 2, TT], I32)
        pos_f = sb("pos_f", [P, 2, TT])
        NA = ROT1 + ROT2
        ang = sb("ang", [P, TT, NA])
        turns = sb("turns", [P, TT, NA])
        red = sb("red", [P, TT, NA])
        red2 = sb("red2", [P, TT, NA])
        cos = sb("cos", [P, TT, NA])
        sin = sb("sin", [P, TT, NA])
        stat = sb("stat", [P, 7, 2 * len(NORMS), 2])
        soft = sb("soft", [P, 4, 2 * (8 + 8 + 16)])

        qk_tok = arena[:, 0:4096].rearrange("p (t n) -> p t n", t=TT)
        qT = arena[:, 4096:6144].rearrange("p (h t) -> p h t", t=T)
        kT = arena[:, 6144:8192].rearrange("p (h t) -> p h t", t=T)
        rope_tmp = junk[:, 0:1024].rearrange("p (a n) -> p a n", a=4)
        lora = arena[:, 0:1408].rearrange("p (t n) -> p t n", t=TT)
        qr_tok = arena[:, 1408:2432].rearrange("p (t n) -> p t n", t=TT)
        qrT = arena[:, 2432:3456].rearrange("p (h t) -> p h t", t=T)
        krT = arena[:, 3456:3712]
        relu = arena[:, 0:512]
        hf = arena[:, 512:1024]
        bias = arena[:, 0:2048].rearrange("p (a n) -> p a n", a=8)
        probs = sb("probs", [P, 3, 3 * P])
        probsT = sb("probsT", [P, 2, 3 * P])
        V = xs
        V2 = arena[:, 2048:4096].rearrange("p (t n) -> p t n", t=TT)

        ident = const[:, C_IDENT:C_IDENT + P]
        causal = const[:, C_CAUSAL:C_CAUSAL + T]
        chunked = const[:, C_CHUNKED:C_CHUNKED + T]
        inv = const[:, C_INV:C_INV + NA]

        ps = ctx.enter_context(nc.psum_tensor("ps", [P, 8 * HALF], F32))

        def bank(b, lo=0, hi=HALF):
            return ps[:, b * HALF + lo:b * HALF + hi]

        w_loaded = [sem(f"w_loaded{s}") for s in range(SLOTS)]
        hi_ready = sem("hi_ready")
        lo_ready_v = sem("lo_ready_v")
        lo_ready_g = sem("lo_ready_g")
        w_used = sem("w_used")
        row_loaded = [sem(f"row_loaded{s}") for s in range(ROW_SLOTS)]
        row_used = sem("row_used")
        x_loaded = sem("x_loaded")
        const_loaded = sem("const_loaded")
        pos_loaded = sem("pos_loaded")
        bias_loaded = [sem(f"bias_loaded{s}") for s in range(8)]
        bias_free = sem("bias_free")
        bias_edge = sem("bias_edge")
        bias_ready = sem("bias_ready")
        out_stored = sem("out_stored")
        chain = sem("chain")
        angle_ready = sem("angle_ready")
        trig_ready = sem("trig_ready")
        x_ready = sem("x_ready")
        squares = sem("squares")
        var_ready = sem("var_ready")
        root_ready = sem("root_ready")
        xs_ready = sem("xs_ready")
        turned = sem("turned")
        act_hi_ready = sem("act_hi_ready")
        act_lo_ready = sem("act_lo_ready")
        acc_t0 = sem("acc_t0")
        qkv_a = sem("qkv_copied_act")
        qkv_v = sem("qkv_copied_dve")
        roped = sem("roped")
        heads_turned = sem("heads_turned")
        heads_copied = sem("heads_copied")
        pooled = sem("pooled")
        acc_wa = sem("acc_wa")
        lora_a = sem("lora_copied_act")
        lora_v = sem("lora_copied_dve")
        kr_copied = sem("kr_copied")
        kr_roped = sem("kr_roped")
        qn_copied = sem("qn_copied")
        qr_copied = sem("qr_copied")
        qr_turned = sem("qr_turned")
        qr_roped = sem("qr_roped")
        qrT_copied = sem("qrT_copied")
        kn_copied = sem("kn_copied")
        v_copied = sem("v_copied")
        kT_copied = sem("kT_copied")
        vs_copied = sem("vs_copied")
        qT_copied = sem("qT_copied")

        class Ffn:
            def __init__(self, name, first):
                self.first = first
                self.act_done = sem(name + "_act_done")
                self.h_done = sem(name + "_h_done")
                self.hi_done = sem(name + "_hi_done")
                self.lo_done = sem(name + "_lo_done")

        class Attn:
            def __init__(self, name, heads, scale, first_col):
                self.heads, self.scale, self.col = heads, scale, first_col
                self.scored = sem(name + "_scored")
                self.maxed = sem(name + "_maxed")
                self.exped = sem(name + "_exped")
                self.normed = sem(name + "_normed")
                self.p_turned = sem(name + "_p_turned")
                self.p_copied = sem(name + "_p_copied")
                self.mixed = sem(name + "_mixed")
                self.o_hi = sem(name + "_o_hi")
                self.o_lo = sem(name + "_o_lo")

        mlp = [Ffn("mlp0", AT["mlp0"]), Ffn("mlp1", AT["mlp1"])]
        ffn = [Ffn("ffn0", AT["ffn0"]), Ffn("ffn1", AT["ffn1"])]
        moba = Attn("moba", 8, 128.0 ** -0.5, 0)
        mla = Attn("mla", 8, 192.0 ** -0.5, 16)
        chk = Attn("chk", 16, 64.0 ** -0.5, 32)

        XR = {"mix0": 0, "mlp0": 1, "mix1": 2, "mlp1": 3, "final": 4, "pre0": 5, "fpre0": 6,
              "kvsrc": 7, "fpre1": 8}
        TURN = {"mix0": 0, "mlp0": 1, "mlp1": 2, "pre0": 3, "lora": 4, "fpre0": 5, "kvsrc": 6,
                "pre1": 7, "fpre1": 8}
        XSR = {"mix0": 0, "mlp0": 1, "mix1": 2, "mlp1": 3, "pre0": 4, "lora": 5, "fpre0": 6,
               "kvsrc": 7, "pre1": 8, "fpre1": 9}
        ACTN = {"mix0": 0, "mlp0": 1, "mix1": 2, "mlp1": 3, "pre0": 4, "lora": 5, "fpre0": 6,
                "kvsrc": 7, "pre1": 8, "fpre1": 9}
        ACC = {"wo": 0, "mlp0": 1, "mlp1": 2, "mwo": 3, "ffn0": 4, "bwo": 5, "ffn1": 6}

        block = ctx.enter_context(nc.Block())

        w_qkv = a["attn_w_qkv"][0].rearrange("(h k p) (n f) -> h n p k f", h=2, p=P, f=HALF)
        w_up1 = a["mlp_w_up"].rearrange("l (k p) (n f) -> l n p k f", p=P, f=FC)
        w_down1 = a["mlp_w_down"].rearrange("l (n k p) f -> l n p k f", p=P, k=2)
        w_gate2 = a["ffn_w_gate_2"].rearrange("l (k p) (n f) -> l n p k f", p=P, f=FC)
        w_up2 = a["ffn_w_up_2"].rearrange("l (k p) (n f) -> l n p k f", p=P, f=FC)
        w_down2 = a["ffn_w_down_2"].rearrange("l (n k p) f -> l n p k f", p=P, k=2)

        def two_rows(w):
            return w.rearrange("(n k p) f -> n p k f", p=P, k=2)

        def source(kind, i):
            if kind == "qkv":
                return w_qkv[i % 2, i // 2]
            if kind == "wo":
                return two_rows(a["attn_w_o"][0])[i]
            if kind == "pool":
                return a["pool_w"][0].rearrange("g (k p) f -> p (g k) f", p=P)
            if kind == "wa":
                return two_rows(a["mla_w_a_2"][0])[i]
            if kind == "uq":
                return a["mla_w_uq_2"][0].rearrange("(k p) (n f) -> n p k f", p=P, f=384)[i]
            if kind == "ukv":
                return a["mla_w_ukv_2"][0].rearrange("(k p) (n f) -> n p k f", p=P, f=1024)[i]
            if kind == "mwo":
                return two_rows(a["mla_w_o_2"][0])[i]
            if kind == "kvk":
                return a["w_kv_shared_2"].rearrange("(k p) (n f) -> n p k f", p=P, f=FC)[i]
            if kind == "kvv":
                return a["w_kv_shared_2"].rearrange("(h k p) (n f) -> h n p k f", h=2, p=P, f=HALF)[i % 2, 2 + i // 2]
            if kind == "bq":
                return a["b_w_q_2"][0].rearrange("(k p) (n f) -> n p k f", p=P, f=FC)[i]
            if kind == "bwo":
                return two_rows(a["b_w_o_2"][0])[i]
            return {"up": w_up1, "down": w_down1, "gate2": w_gate2, "up2": w_up2,
                    "down2": w_down2}[kind][i[0], i[1]]

        row_source = {
            "mix0": a["norm_mix"][0:1, :], "mlp0": a["norm_mlp"][0:1, :], "mix1": a["norm_mix"][1:2, :],
            "pool_scale": a["pool_scale"][0:1, :], "mlp1": a["norm_mlp"][1:2, :],
            "final": a["norm_final"].rearrange("(a n) -> a n", a=1),
            "pre0": a["attn_pre_g_2"][0:1, :], "post0": a["attn_post_g_2"][0:1, :],
            "fpre0": a["ffn_pre_g_2"][0:1, :], "fpost0": a["ffn_post_g_2"][0:1, :],
            "kvsrc": a["kv_src_g_2"].rearrange("(a n) -> a n", a=1),
            "pre1": a["attn_pre_g_2"][1:2, :], "post1": a["attn_post_g_2"][1:2, :],
            "fpre1": a["ffn_pre_g_2"][1:2, :], "fpost1": a["ffn_post_g_2"][1:2, :],
        }
        ROW_BYTES_DONE = {}
        seen = [0] * ROW_SLOTS
        for r, name in enumerate(ROWS):
            seen[r % ROW_SLOTS] += 32 if name == "lora" else 16
            ROW_BYTES_DONE[name] = seen[r % ROW_SLOTS]

        def row(name, lo=0, hi=D):
            return rows[:, ROW[name] % ROW_SLOTS, lo:hi]

        def wait_row(eng, name):
            eng.wait_ge(row_loaded[ROW[name] % ROW_SLOTS], ROW_BYTES_DONE[name])

        @block.sync
        def _(sp):
            def load_row(name):
                r = ROW[name]
                s = r % ROW_SLOTS
                if r >= ROW_SLOTS:
                    sp.wait_ge(row_used, r - ROW_SLOTS + 1)
                if name == "lora":
                    sp.dma_start(rows[:, s, 0:QL], a["mla_g_q_2"][0:1, :].partition_broadcast(P)
                                 .rearrange("q a n -> q (a n)")).then_inc(row_loaded[s], 16)
                    sp.dma_start(rows[:, s, QL:QL + KVL], a["mla_g_kv_2"][0:1, :].partition_broadcast(P)
                                 .rearrange("q a n -> q (a n)")).then_inc(row_loaded[s], 16)
                else:
                    sp.dma_start(rows[:, s, :], row_source[name].partition_broadcast(P)
                                 .rearrange("q a n -> q (a n)")).then_inc(row_loaded[s], 16)

            def load(c, s, src, width, freed):
                if freed is not None:
                    sp.wait_ge(lo_ready_v, freed)
                    sp.wait_ge(lo_ready_g, freed)
                sp.dma_start(raw[:, s, 0:width].rearrange("p (k f) -> p k f", f=src.shape[-1]), src)\
                  .then_inc(w_loaded[s], 16)

            def load_one(c):
                kind, i, width = CHUNKS[c]
                load(c, SLOT[c], source(kind, i), width, PREV[c] + 1 if PREV[c] >= 0 else None)

            def load_bias(h):
                if h >= 8:
                    sp.wait_ge(chk.maxed, h - 7)
                table = a["b_rel_table_2"]
                sp.dma_start(bias[0:64, h % 8, 64:T],
                             bass.AP(table.tensor, h * REL, [[1, 64], [1, T - 64]]))\
                  .then_inc(bias_loaded[h % 8], 16)
                sp.dma_start(bias[64:128, h % 8, :],
                             bass.AP(table.tensor, h * REL, [[1, 64], [1, T]]))\
                  .then_inc(bias_loaded[h % 8], 16)

            sp.dma_start(x[:, :, :], a["x"][0].rearrange("(t p) n -> p t n", p=P)).then_inc(x_loaded, 16)
            load_one(0)
            sp.dma_start(const[:, :], a["const"]).then_inc(const_loaded, 16)
            for n, name in enumerate(("positions", "positions_2")):
                sp.dma_start(pos_i[:, n, :], a[name].rearrange("a (t p) -> p (a t)", p=P),
                             allow_slow_non_contiguous=True).then_inc(pos_loaded, 16)
            load_row("mix0")
            for c in range(1, AT["mlp0"]):
                load_one(c)
                if c == 4:
                    load_row("mlp0")
                    load_row("mix1")
                    load_row("pool_scale")
            for layer in range(2):
                n0 = AT[f"mlp{layer}"]
                for m in range(3):
                    load_one(n0 + m)
                if layer == 1:
                    load_row("final")
                    load_row("pre0")
                    load_row("lora")
                with sp.Fori(0, (NM - 2) // 2) as i:
                    for j in range(4):
                        c = n0 + 3 + j
                        src = w_up1[layer, i * 2 + 2 + j // 2] if j % 2 == 0 else w_down1[layer, i * 2 + 1 + j // 2]
                        sp.wait_ge(lo_ready_v, i * 4 + (c - 3))
                        sp.wait_ge(lo_ready_g, i * 4 + (c - 3))
                        sp.dma_start(raw[:, SLOT[c], :].rearrange("p (k f) -> p k f", f=src.shape[-1]), src)\
                          .then_inc(w_loaded[SLOT[c]], 16)
                load_one(n0 + 31)
                if layer == 0:
                    load_one(AT["pool"])
                    load_row("mlp1")
            for c in range(AT["wa"], AT["ffn0"]):
                load_one(c)
                if c == AT["uq"]:
                    load_row("post0")
                    load_row("fpre0")
                if c == AT["mwo"] + 1:
                    load_row("fpost0")
            for layer in range(2):
                n0 = AT[f"ffn{layer}"]
                for m in range(4):
                    load_one(n0 + m)
                if layer == 0:
                    load_row("kvsrc")
                    load_row("pre1")
                with sp.Fori(1, NF - 1) as i:
                    for j, src in enumerate((w_down2[layer, i - 1], w_gate2[layer, i + 1], w_up2[layer, i + 1])):
                        c = n0 + 4 + j
                        sp.wait_ge(lo_ready_v, i * 3 + (c - 3 + 1 - 3))
                        sp.wait_ge(lo_ready_g, i * 3 + (c - 3 + 1 - 3))
                        sp.dma_start(raw[:, SLOT[c], :].rearrange("p (k f) -> p k f", f=src.shape[-1]), src)\
                          .then_inc(w_loaded[SLOT[c]], 16)
                load_one(n0 + 31)
                load_one(n0 + 32)
                if layer == 0:
                    for c in range(AT["kvk"], AT["ffn1"]):
                        load_one(c)
                        if c == AT["kvk"] + 3:
                            load_row("post1")
                            sp.wait_ge(ffn[0].lo_done, NF)
                            sp.wait_ge(bias_edge, 1)
                            for h in range(8):
                                load_bias(h)
                            load_row("fpre1")
                        if c == AT["bwo"] + 3:
                            load_row("fpost1")
                            for h in range(8, 16):
                                load_bias(h)
            for t in range(TT):
                sp.wait_ge(x_ready, 2 * 9 + t + 1)
                sp.dma_start(out[0, t * P:(t + 1) * P, :], x[:, t, :]).then_inc(out_stored, 16)
            sp.wait_ge(out_stored, 16 * TT)

        DV = 5

        def cut(width):
            return width * DV // 8

        def scale_bias(pool, h):
            pool.wait_ge(bias_loaded[h % 8], 32 * (h // 8 + 1))
            if h == 0:
                pool.wait_ge(bias_edge, 1)
            nc.gpsimd.tensor_scalar(bias[:, h % 8, :], bias[:, h % 8, :], 8.0, None, ALU.mult)\
                .then_inc(bias_ready, 1)

        @block.gpsimd
        def _(pool):
            def lo_part(s, width, value):
                pool.wait_ge(hi_ready, value)
                w = cut(width)
                nc.gpsimd.tensor_tensor(wlo[:, s, w:width], raw[:, s, w:width],
                                        whi[:, s, w:width].bitcast(F32), ALU.subtract)\
                    .then_inc(lo_ready_g, 1)

            def lo_one(c):
                lo_part(SLOT[c], CHUNKS[c][2], c + 1)

            for c in range(AT["mlp0"]):
                lo_one(c)
            for layer in range(2):
                n0 = AT[f"mlp{layer}"]
                for m in range(3):
                    lo_one(n0 + m)
                with pool.Fori(0, (NM - 2) // 2) as i:
                    for j in range(4):
                        lo_part(SLOT[n0 + 3 + j], W, i * 4 + (n0 + 4 + j))
                lo_one(n0 + 31)
                if layer == 0:
                    lo_one(AT["pool"])
            for c in range(AT["wa"], AT["ffn0"]):
                lo_one(c)
            for layer in range(2):
                n0 = AT[f"ffn{layer}"]
                for m in range(4):
                    lo_one(n0 + m)
                with pool.Fori(1, NF - 1) as i:
                    for j in range(3):
                        lo_part(SLOT[n0 + 4 + j], W, i * 3 + (n0 + 5 + j - 3))
                lo_one(n0 + 31)
                lo_one(n0 + 32)
                if layer == 0:
                    pool.wait_ge(ffn[0].lo_done, NF)
                    nc.gpsimd.memset(bias[:, :, 0:64], NEG).then_inc(bias_edge, 1)
                    for c in range(AT["kvk"], AT["ffn1"]):
                        lo_one(c)
                        if c == AT["bq"]:
                            for h in range(8):
                                scale_bias(pool, h)
                    for h in range(8, 16):
                        scale_bias(pool, h)

        def norm_stat(name, t, what, lo=0, hi=1):
            return stat[:, what, 2 * NORM[name] + t, lo:hi]

        def squares_after(name, t):
            n = 2 * NORM[name] + t + 1
            if NORM[name] > NORM["lora"]:
                n += 2
            elif name == "lora":
                n += t + 1
            return n

        def post_stats(act, sum_squares, root, name, done, acc):
            act.wait_ge(acc_t0, acc + 1)
            sum_squares(name, 0, ps[:, 0:D], D)
            root(name, 0)
            act.wait_ge(w_used, done)
            sum_squares(name, 1, ps[:, D:2 * D], D)
            root(name, 1)

        def copy_heads(act, n):
            dst = qT if n < 2 else kT
            for b in range(2):
                act.wait_ge(heads_turned, 2 * n + b + 1)
                h = 4 * (n % 2) + 2 * b
                nc.scalar.activation(dst[:, h:h + 2, :].rearrange("p h t -> p (h t)"),
                                     bank(4 + 2 * (n % 2) + b), ACT.Copy).then_inc(heads_copied, 1)

        def copy_qr(act, j):
            act.wait_ge(qr_turned, j + 1)
            nc.scalar.activation(qrT[:, j, :], bank(4 + j % 2, 0, T), ACT.Copy).then_inc(qrT_copied, 1)

        @block.scalar
        def _(act):
            cursor = [0]

            def hi_part(s, width, loaded, freed):
                act.wait_ge(w_loaded[s], loaded)
                if freed is not None:
                    act.wait_ge(w_used, freed)
                nc.scalar.activation(whi[:, s, 0:width], raw[:, s, 0:width], ACT.Copy).then_inc(hi_ready, 1)

            def hi_before(c):
                while cursor[0] < NCH and PREV[cursor[0]] < c:
                    q = cursor[0]
                    hi_part(SLOT[q], CHUNKS[q][2], 16 * NTH[q], PREV[q] + 1 if PREV[q] >= 0 else None)
                    cursor[0] += 1

            def sum_squares(name, t, src, width, col=0):
                nc.scalar.activation(junk[:, col * HALF:col * HALF + width], src, ACT.Square,
                                     accum_out=norm_stat(name, t, 0, col, col + 1)).then_inc(squares, 1)

            def root(name, t, width=1):
                act.wait_ge(var_ready, 2 * NORM[name] + t + 1)
                nc.scalar.activation(norm_stat(name, t, 2, 0, width), norm_stat(name, t, 1, 0, width),
                                     ACT.Sqrt).then_inc(root_ready, 1)

            def stats(name):
                for t in range(TT):
                    act.wait_ge(x_ready, 2 * XR[name] + t + 1)
                    sum_squares(name, t, x[:, t, :], D)
                    root(name, t)

            def copy_turned(name):
                for t in range(TT):
                    for b in range(2):
                        act.wait_ge(turned, 4 * TURN[name] + 2 * t + b + 1)
                        nc.scalar.activation(act_hi[:, 4 * b:4 * b + 4, t * P:(t + 1) * P],
                                             bank(4 + 2 * t + b).rearrange("p (k t) -> p k t", t=P),
                                             ACT.Copy).then_inc(act_hi_ready, 1)

            def attention(at):
                pairs = at.heads == 16
                for h in range(at.heads + 3):
                    if h < at.heads:
                        act.wait_ge(at.maxed, h + 1)
                        for t in range(TT):
                            lo, hi = (0, P) if t == 0 else (P, 3 * P)
                            c = at.col + 2 * h + t
                            nc.scalar.activation(probs[:, h % 3, lo:hi], probs[:, h % 3, lo:hi], ACT.Exp,
                                                 bias=soft[:, 1, c:c + 1], scale=at.scale,
                                                 accum_out=soft[:, 2, c:c + 1])\
                                .then_inc(at.exped, 1)
                    g = h - 2
                    if 0 <= g < at.heads:
                        act.wait_ge(at.p_turned, g + 1)
                        nc.scalar.activation(probsT[:, g % 2, :], bank(6, 0, 3 * P), ACT.Copy)\
                            .then_inc(at.p_copied, 1)
                    g = h - 3
                    if 0 <= g < at.heads and (not pairs or g % 2):
                        act.wait_ge(at.mixed, g + 1)
                        k = g // 2 if pairs else g
                        nc.scalar.activation(act_hi[:, k, :], bank(7, 0, T), ACT.Copy).then_inc(at.o_hi, 1)

            def mlp_layer(f, layer):
                n0 = f.first

                def head(i, first):
                    act.wait_ge(w_used, n0 + 1 if first else i * 2 + n0)
                    if not first:
                        act.wait_ge(f.h_done, i)
                    nc.scalar.activation(relu, bank(4), ACT.Relu).then_inc(f.act_done, 1)

                def tail(i, first):
                    act.wait_ge(f.h_done, i + 1)
                    if not first:
                        act.wait_ge(w_used, i * 2 + (n0 + 1))
                    nc.scalar.activation(hhi[:, :, :].rearrange("p k t -> p (k t)"), hf, ACT.Copy)\
                        .then_inc(f.hi_done, 1)

                hi_before(n0)
                head(0, True)
                tail(0, True)
                extra = cursor[0] - (n0 + 3)
                with act.Fori(0, (NM - 2) // 2) as n:
                    for u in range(2):
                        i = n * 2 + 1 + u
                        head(i, False)
                        for m in (3 + 2 * u + extra, 4 + 2 * u + extra):
                            c = n0 + m
                            hi_part(SLOT[c], W, n * 16 + 16 * NTH[c], n * 4 + (c - 3))
                        tail(i, False)
                cursor[0] = n0 + 31 + extra
                head(NM - 1, False)
                hi_before(n0 + 2 * (NM - 1))
                tail(NM - 1, False)

            def ffn_layer(f):
                n0 = f.first

                def head(i, first):
                    act.wait_ge(w_used, n0 + 2 if first else i * 3 + (n0 + 1))
                    if not first:
                        act.wait_ge(f.h_done, i)
                    nc.scalar.activation(relu, bank(4), ACT.Silu).then_inc(f.act_done, 1)

                def tail(i, first):
                    act.wait_ge(f.h_done, i + 1)
                    if not first:
                        act.wait_ge(w_used, i * 3 + (n0 + 2))
                    nc.scalar.activation(hhi[:, :, :].rearrange("p k t -> p (k t)"), hf, ACT.Copy)\
                        .then_inc(f.hi_done, 1)

                def part(c, n):
                    hi_part(SLOT[c], W, n * 16 + 16 * (NTH[c] - 1), n * 3 + (c - 2 - 3))

                hi_before(n0 + 1)
                assert cursor[0] == n0 + 4, (cursor[0], n0)
                head(0, True)
                tail(0, True)
                with act.Fori(1, NF - 1) as i:
                    part(n0 + 4, i)
                    head(i, False)
                    part(n0 + 5, i)
                    part(n0 + 6, i)
                    tail(i, False)
                cursor[0] = n0 + 31
                hi_before(n0 + 3 * (NF - 1))
                head(NF - 1, False)
                hi_before(n0 + 3 * (NF - 1) + 1)
                tail(NF - 1, False)

            act.wait_ge(angle_ready, 1)
            nc.scalar.activation(sin[:, :, :], red[:, :, :], ACT.Sin).then_inc(trig_ready, 1)
            act.wait_ge(angle_ready, 2)
            nc.scalar.activation(cos[:, :, :], red2[:, :, :], ACT.Sin).then_inc(trig_ready, 1)
            stats("mix0")
            hi_before(0)
            copy_turned("mix0")
            for n in range(6):
                hi_before(2 * n + 1)
                act.wait_ge(w_used, 2 * n + 2)
                dst = qk_tok[:, 0, n * HALF:(n + 1) * HALF] if n < 4 else V[:, 0, (n - 4) * HALF:(n - 3) * HALF]
                nc.scalar.activation(dst, bank(2 * (n % 2)), ACT.Copy).then_inc(qkv_a, 1)
                if n >= 3:
                    copy_heads(act, n - 3)
            copy_heads(act, 3)
            hi_before(AT["wo"])
            attention(moba)
            hi_before(AT["wo"] + 3)
            stats("mlp0")
            copy_turned("mlp0")
            mlp_layer(mlp[0], 0)
            hi_before(mlp[0].first + 31)
            stats("mix1")
            for b in range(4):
                act.wait_ge(pooled, b + 1)
                nc.scalar.activation(act_hi[:, 2 * b:2 * b + 2, :].rearrange("p k t -> p (k t)"), bank(4 + b),
                                     ACT.Copy).then_inc(act_hi_ready, 1)
            hi_before(AT["pool"])
            stats("mlp1")
            copy_turned("mlp1")
            mlp_layer(mlp[1], 1)
            hi_before(mlp[1].first + 31)
            stats("final")
            stats("pre0")
            copy_turned("pre0")
            hi_before(AT["wa"] + 3)
            act.wait_ge(acc_wa, 1)
            nc.scalar.activation(lora[:, 0, :], ps[:, 0:704], ACT.Copy).then_inc(lora_a, 1)
            for t in range(TT):
                if t == 0:
                    act.wait_ge(lora_a, 1)
                else:
                    act.wait_ge(lora_v, 1)
                sum_squares("lora", t, lora[:, t, 0:QL], QL, 0)
                sum_squares("lora", t, lora[:, t, QL:QL + KVL], KVL, 1)
                root("lora", t, 2)
            for t in range(TT):
                act.wait_ge(turned, 4 * TURN["lora"] + 2 * t + 1)
                nc.scalar.activation(act_hi[:, 0:4, t * P:(t + 1) * P],
                                     bank(4 + 2 * t).rearrange("p (k t) -> p k t", t=P), ACT.Copy)\
                    .then_inc(act_hi_ready, 1)
                act.wait_ge(turned, 4 * TURN["lora"] + 2 * t + 2)
                nc.scalar.activation(act_hi[:, 4, t * P:(t + 1) * P], bank(5 + 2 * t, 0, P), ACT.Copy)\
                    .then_inc(act_hi_ready, 1)
                nc.scalar.activation(krT[:, t * P:(t + 1) * P], bank(5 + 2 * t, P, 2 * P), ACT.Copy)\
                    .then_inc(kr_copied, 1)
            for j in range(4):
                c = AT["uq"] + j
                hi_before(c)
                act.wait_ge(w_used, c + 1)
                nc.scalar.activation(qT[:, 2 * j:2 * j + 2, :].rearrange("p h t -> p (h t)"), bank(j % 2),
                                     ACT.Copy).then_inc(qn_copied, 1)
                if j >= 1:
                    copy_qr(act, j - 1)
            for j in range(2):
                c = AT["ukv"] + j
                hi_before(c)
                act.wait_ge(w_used, c + 1)
                for b in range(2):
                    nc.scalar.activation(kT[:, 4 * j + 2 * b:4 * j + 2 * b + 2, :].rearrange("p h t -> p (h t)"),
                                         bank(b), ACT.Copy).then_inc(kn_copied, 1)
                if j == 0:
                    copy_qr(act, 3)
            hi_before(AT["mwo"])
            attention(mla)
            hi_before(AT["mwo"] + 3)
            post_stats(act, sum_squares, root, "post0", AT["mwo"] + 4, ACC["mwo"])
            stats("fpre0")
            copy_turned("fpre0")
            ffn_layer(ffn[0])
            hi_before(ffn[0].first + 32)
            post_stats(act, sum_squares, root, "fpost0", ffn[0].first + 33, ACC["ffn0"])
            stats("kvsrc")
            copy_turned("kvsrc")
            for j in range(4):
                c = AT["kvk"] + j
                hi_before(c)
                act.wait_ge(w_used, c + 1)
                nc.scalar.activation(kT[:, 2 * j:2 * j + 2, :].rearrange("p h t -> p (h t)"), bank(4 + j % 2),
                                     ACT.Copy).then_inc(kT_copied, 1)
            for n in range(2):
                c = AT["kvv"] + 2 * n
                hi_before(c + 1)
                act.wait_ge(w_used, c + 2)
                nc.scalar.activation(V2[:, 0, n * HALF:(n + 1) * HALF], bank(2 * n), ACT.Copy)\
                    .then_inc(vs_copied, 1)
            copy_turned("pre1")
            for j in range(4):
                c = AT["bq"] + j
                hi_before(c)
                act.wait_ge(w_used, c + 1)
                nc.scalar.activation(qT[:, 2 * j:2 * j + 2, :].rearrange("p h t -> p (h t)"), bank(4 + j % 2),
                                     ACT.Copy).then_inc(qT_copied, 1)
            hi_before(AT["bwo"])
            attention(chk)
            hi_before(AT["bwo"] + 3)
            post_stats(act, sum_squares, root, "post1", AT["bwo"] + 4, ACC["bwo"])
            stats("fpre1")
            copy_turned("fpre1")
            ffn_layer(ffn[1])
            post_stats(act, sum_squares, root, "fpost1", ffn[1].first + 33, ACC["ffn1"])

        @block.vector
        def _(dve):
            cursor = [0]
            links = [0]

            def link(ins):
                links[0] += 1
                ins.then_inc(chain, 1)
                dve.wait_ge(chain, links[0])

            def lo_part(s, width, value):
                dve.wait_ge(hi_ready, value)
                w = cut(width)
                nc.vector.tensor_tensor(wlo[:, s, 0:w], raw[:, s, 0:w], whi[:, s, 0:w].bitcast(F32),
                                        ALU.subtract).then_inc(lo_ready_v, 1)

            def lo_before(c):
                while cursor[0] < NCH and PREV[cursor[0]] < c:
                    q = cursor[0]
                    lo_part(SLOT[q], CHUNKS[q][2], q + 1)
                    cursor[0] += 1

            def inverse_root(name, t, widths=(D,)):
                n = len(widths)

                def st(k, lo=0, hi=n):
                    return norm_stat(name, t, k, lo, hi)

                dve.wait_ge(squares, squares_after(name, t))
                for i, w in enumerate(widths):
                    ins = nc.vector.tensor_scalar(st(1, i, i + 1), st(0, i, i + 1), 1.0 / w, EPS, ALU.mult, ALU.add)
                ins.then_inc(var_ready, 1)
                dve.wait_ge(root_ready, 2 * NORM[name] + t + 1)
                link(nc.vector.reciprocal(st(3), st(2)))
                link(nc.vector.tensor_tensor(st(4), st(3), st(3), ALU.mult))
                link(nc.vector.tensor_tensor(st(5), st(4), st(1), ALU.mult))
                link(nc.vector.tensor_scalar(st(5), st(5), -0.5, 1.5, ALU.mult, ALU.add))
                link(nc.vector.tensor_tensor(st(6), st(5), st(3), ALU.mult))

            def scaled(dst, src, name, t, gain, col=0):
                return nc.vector.scalar_tensor_tensor(out=dst, in0=src, scalar=norm_stat(name, t, 6, col, col + 1),
                                                      in1=gain, op0=ALU.mult, op1=ALU.mult)

            def norm(name, rowname=None):
                rowname = rowname or name
                for t in range(TT):
                    if t == 0:
                        wait_row(dve, rowname)
                    if rowname == name:
                        inverse_root(name, t)
                    if rowname == "pre1":
                        dve.wait_ge(turned, 4 * TURN["kvsrc"] + 4)
                    ins = scaled(xs[:, t, :], x[:, t, :], name, t, row(rowname))
                    ins.then_inc(xs_ready, 1)
                    if t == 1:
                        dve.wait_ge(xs_ready, 2 * XSR[rowname] + 2)
                        release_row()

            def release_row():
                dve.sem_inc(row_used, 1)

            def split_turned(name):
                for t in range(TT):
                    for b in range(2):
                        dve.wait_ge(act_hi_ready, 4 * ACTN[name] + 2 * t + b + 1)
                        nc.vector.tensor_tensor(
                            act_lo[:, 4 * b:4 * b + 4, t * P:(t + 1) * P],
                            bank(4 + 2 * t + b).rearrange("p (k t) -> p k t", t=P),
                            act_hi[:, 4 * b:4 * b + 4, t * P:(t + 1) * P].bitcast(F32), ALU.subtract)\
                            .then_inc(act_lo_ready, 1)

            def residual(done, acc):
                for t in range(TT):
                    dve.wait_ge(*((acc_t0, acc + 1) if t == 0 else (w_used, done)))
                    nc.vector.tensor_tensor(x[:, t, :], x[:, t, :], ps[:, t * D:(t + 1) * D], ALU.add)\
                        .then_inc(x_ready, 1)

            def post(name):
                wait_row(dve, name)
                for t in range(TT):
                    inverse_root(name, t)
                    link(scaled(xs[:, t, :], ps[:, t * D:(t + 1) * D], name, t, row(name)))
                    nc.vector.tensor_tensor(x[:, t, :], x[:, t, :], xs[:, t, :], ALU.add).then_inc(x_ready, 1)
                release_row()

            def rope(src, dst, c, s, n, tmp):
                x1, x2 = src
                y1, y2 = dst
                nc.vector.tensor_tensor(tmp[0], x1, c, ALU.mult)
                nc.vector.tensor_tensor(tmp[1], x2, s, ALU.mult)
                nc.vector.tensor_tensor(tmp[2], x2, c, ALU.mult)
                link(nc.vector.tensor_tensor(tmp[3], x1, s, ALU.mult))
                nc.vector.tensor_tensor(y1, tmp[0], tmp[1], ALU.subtract)
                return nc.vector.tensor_tensor(y2, tmp[2], tmp[3], ALU.add)

            def attention(at, masks):
                pairs = at.heads == 16
                for h in range(at.heads + 3):
                    if h < at.heads:
                        mask = masks(h)
                        dve.wait_ge(at.scored, h + 1)
                        c = at.col + 2 * h
                        for t in range(TT):
                            lo, hi = (0, P) if t == 0 else (P, 3 * P)
                            ins = nc.vector.tensor_tensor_reduce(
                                probs[:, h % 3, lo:hi], bank(4 + h % 2, lo, hi), mask[t],
                                1.0, MIN32, ALU.add, ALU.max, soft[:, 0, c + t:c + t + 1])
                        link(ins)
                        nc.vector.tensor_scalar(soft[:, 1, c:c + 2], soft[:, 0, c:c + 2], -at.scale, None,
                                                ALU.mult).then_inc(at.maxed, 1)
                    g = h - 1
                    if 0 <= g < at.heads:
                        dve.wait_ge(at.exped, 2 * g + 2)
                        c = at.col + 2 * g
                        link(nc.vector.reciprocal(soft[:, 3, c:c + 2], soft[:, 2, c:c + 2]))
                        for t in range(TT):
                            lo, hi = (0, P) if t == 0 else (P, 3 * P)
                            ins = nc.vector.tensor_scalar(probs[:, g % 3, lo:hi], probs[:, g % 3, lo:hi],
                                                          soft[:, 3, c + t:c + t + 1], None, ALU.mult)
                        ins.then_inc(at.normed, 1)
                    g = h - 3
                    if 0 <= g < at.heads and (not pairs or g % 2):
                        k = g // 2 if pairs else g
                        dve.wait_ge(at.o_hi, k + 1)
                        nc.vector.tensor_tensor(act_lo[:, k, :], bank(7, 0, T), act_hi[:, k, :].bitcast(F32),
                                                ALU.subtract).then_inc(at.o_lo, 1)

            def hidden_lo(f, i):
                dve.wait_ge(f.hi_done, i + 1)
                nc.vector.tensor_tensor(hlo[:, :, :].rearrange("p k t -> p (k t)"), hf,
                                        hhi[:, :, :].rearrange("p k t -> p (k t)").bitcast(F32),
                                        ALU.subtract).then_inc(f.lo_done, 1)

            def mlp_layer(f):
                n0 = f.first

                def square(i, first=False):
                    dve.wait_ge(f.act_done, i + 1)
                    if not first:
                        dve.wait_ge(f.lo_done, i)
                    nc.vector.tensor_tensor(hf, relu, relu, ALU.mult).then_inc(f.h_done, 1)

                lo_before(n0)
                extra = cursor[0] - (n0 + 3)
                square(0, True)
                hidden_lo(f, 0)
                with dve.Fori(0, (NM - 2) // 2) as n:
                    for u in range(2):
                        i = n * 2 + 1 + u
                        square(i)
                        for m in (3 + 2 * u + extra, 4 + 2 * u + extra):
                            lo_part(SLOT[n0 + m], W, n * 4 + (n0 + m + 1))
                        hidden_lo(f, i)
                cursor[0] = n0 + 31 + extra
                square(NM - 1)
                lo_before(n0 + 2 * (NM - 1))
                hidden_lo(f, NM - 1)

            def ffn_layer(f):
                n0 = f.first

                def gated(i, first=False):
                    dve.wait_ge(f.act_done, i + 1)
                    if not first:
                        dve.wait_ge(f.lo_done, i)
                    nc.vector.tensor_tensor(hf, relu, bank(5), ALU.mult).then_inc(f.h_done, 1)

                lo_before(n0 + 1)
                gated(0, True)
                hidden_lo(f, 0)
                with dve.Fori(1, NF - 1) as i:
                    lo_part(SLOT[n0 + 4], W, i * 3 + (n0 + 2))
                    gated(i)
                    lo_part(SLOT[n0 + 5], W, i * 3 + (n0 + 3))
                    lo_part(SLOT[n0 + 6], W, i * 3 + (n0 + 4))
                    hidden_lo(f, i)
                cursor[0] = n0 + 31
                lo_before(n0 + 3 * (NF - 1))
                gated(NF - 1)
                lo_before(n0 + 3 * (NF - 1) + 1)
                hidden_lo(f, NF - 1)

            dve.wait_ge(x_loaded, 16)
            dve.sem_inc(x_ready, 2)
            dve.wait_ge(pos_loaded, 32)
            link(nc.vector.tensor_copy(pos_f[:, :, :], pos_i[:, :, :]))
            dve.wait_ge(const_loaded, 16)
            for t in range(TT):
                nc.vector.tensor_scalar(ang[:, t, 0:ROT1], inv[:, 0:ROT1], pos_f[:, 0, t:t + 1], None, ALU.mult)
                ins = nc.vector.tensor_scalar(ang[:, t, ROT1:NA], inv[:, ROT1:NA], pos_f[:, 1, t:t + 1], None,
                                              ALU.mult)
            link(ins)
            link(nc.vector.tensor_scalar(turns[:, :, :], ang[:, :, :], INV_2PI, MAGIC, ALU.mult, ALU.add))
            link(nc.vector.tensor_scalar(turns[:, :, :], turns[:, :, :], -MAGIC, None, ALU.add))
            src = ang
            for n, part in enumerate((PI_A, PI_B, PI_C)):
                dst = red2 if n % 2 else red
                link(nc.vector.scalar_tensor_tensor(out=dst[:, :, :], in0=turns[:, :, :], scalar=-part,
                                                    in1=src[:, :, :], op0=ALU.mult, op1=ALU.add))
                src = dst
            link(nc.vector.tensor_scalar(red[:, :, :], red[:, :, :], PI_SAFE, -PI_SAFE, ALU.min, ALU.max))
            dve.sem_inc(angle_ready, 1)
            link(nc.vector.scalar_tensor_tensor(out=red2[:, :, :], in0=red[:, :, :], scalar=-1.0,
                                                in1=red[:, :, :], op0=ALU.mult, op1=ALU.max))
            nc.vector.tensor_scalar(red2[:, :, :], red2[:, :, :], -1.0, HALF_PI, ALU.mult, ALU.add)\
                .then_inc(angle_ready, 1)
            norm("mix0")
            lo_before(0)
            split_turned("mix0")

            def trig(table, lo, hi, heads):
                return table[:, :, lo:hi].unsqueeze(2).broadcast_to([P, TT, heads, hi - lo])

            dve.wait_ge(trig_ready, 2)
            for n in range(6):
                lo_before(2 * n + 1)
                dve.wait_ge(w_used, 2 * n + 2)
                dst = qk_tok[:, 1, n * HALF:(n + 1) * HALF] if n < 4 else V[:, 1, (n - 4) * HALF:(n - 3) * HALF]
                nc.vector.tensor_copy(dst, bank(2 * (n % 2) + 1)).then_inc(qkv_v, 1)
                if n < 4:
                    dve.wait_ge(qkv_v, n + 1)
                    dve.wait_ge(qkv_a, n + 1)
                    v4 = qk_tok[:, :, n * HALF:(n + 1) * HALF].rearrange("p t (h d) -> p t h d", d=HD1)
                    halves = (v4[:, :, :, 0:ROT1], v4[:, :, :, ROT1:2 * ROT1])
                    tmp = [rope_tmp[:, q, 0:TT * 4 * ROT1].rearrange("p (t h d) -> p t h d", t=TT, d=ROT1)
                           for q in range(4)]
                    rope(halves, halves, trig(cos, 0, ROT1, 4), trig(sin, 0, ROT1, 4), ROT1, tmp)\
                        .then_inc(roped, 1)
            lo_before(AT["wo"])
            attention(moba, lambda h: (causal[:, P:T], causal))
            lo_before(AT["wo"] + 3)
            residual(AT["wo"] + 4, ACC["wo"])
            norm("mlp0")
            split_turned("mlp0")
            mlp_layer(mlp[0])
            lo_before(mlp[0].first + 31)
            residual(mlp[0].first + 32, ACC["mlp0"])
            norm("mix1")
            for b in range(4):
                dve.wait_ge(act_hi_ready, 4 * ACTN["mix1"] + b + 1)
                nc.vector.tensor_tensor(act_lo[:, 2 * b:2 * b + 2, :].rearrange("p k t -> p (k t)"), bank(4 + b),
                                        act_hi[:, 2 * b:2 * b + 2, :].rearrange("p k t -> p (k t)").bitcast(F32),
                                        ALU.subtract).then_inc(act_lo_ready, 1)
            lo_before(AT["pool"])
            wait_row(dve, "pool_scale")
            dve.wait_ge(w_used, AT["pool"] + 1)
            for t in range(TT):
                link(nc.vector.tensor_tensor(xs[:, t, :], ps[:, t * D:(t + 1) * D], row("pool_scale"), ALU.mult))
                nc.vector.tensor_tensor(x[:, t, :], x[:, t, :], xs[:, t, :], ALU.add).then_inc(x_ready, 1)
            release_row()
            norm("mlp1")
            split_turned("mlp1")
            mlp_layer(mlp[1])
            lo_before(mlp[1].first + 31)
            residual(mlp[1].first + 32, ACC["mlp1"])
            wait_row(dve, "final")
            for t in range(TT):
                inverse_root("final", t)
                link(scaled(x[:, t, :], x[:, t, :], "final", t, row("final")))
                dve.sem_inc(x_ready, 1)
            release_row()
            norm("pre0")
            split_turned("pre0")
            lo_before(AT["wa"] + 3)
            dve.wait_ge(w_used, AT["wa"] + 4)
            nc.vector.tensor_copy(lora[:, 1, :], ps[:, D:D + 704]).then_inc(lora_v, 1)
            wait_row(dve, "lora")
            for t in range(TT):
                inverse_root("lora", t, (QL, KVL))
                scaled(xs[:, t, 0:QL], lora[:, t, 0:QL], "lora", t, row("lora", 0, QL), 0)
                link(scaled(xs[:, t, QL:QL + KVL], lora[:, t, QL:QL + KVL], "lora", t, row("lora", QL, QL + KVL), 1))
                k0 = QL + KVL
                tmp = [rope_tmp[:, q, 0:ROT2] for q in range(4)]
                dve.wait_ge(squares, squares_after("lora", 1))
                link(rope((lora[:, t, k0:k0 + ROT2], lora[:, t, k0 + ROT2:k0 + 2 * ROT2]),
                          (xs[:, t, k0:k0 + ROT2], xs[:, t, k0 + ROT2:k0 + 2 * ROT2]),
                          cos[:, t, ROT1:NA], sin[:, t, ROT1:NA], ROT2, tmp))
                nc.vector.tensor_copy(xs[:, t, k0 + 64:k0 + 128], xs[:, t, k0:k0 + 64]).then_inc(xs_ready, 1)
            release_row()
            for t in range(TT):
                for b, (k0, k1) in enumerate(((0, 4), (4, 5))):
                    dve.wait_ge(act_hi_ready, 4 * ACTN["lora"] + 2 * t + b + 1)
                    if b:
                        dve.wait_ge(kr_copied, t + 1)
                    nc.vector.tensor_tensor(
                        act_lo[:, k0:k1, t * P:(t + 1) * P],
                        bank(4 + 2 * t + b, 0, (k1 - k0) * P).rearrange("p (k t) -> p k t", t=P),
                        act_hi[:, k0:k1, t * P:(t + 1) * P].bitcast(F32), ALU.subtract)\
                        .then_inc(act_lo_ready, 1)
            for j in range(4):
                c = AT["uq"] + j
                lo_before(c)
                dve.wait_ge(w_used, c + 1)
                cols = qr_tok[:, :, 2 * j * 64:(2 * j + 2) * 64]
                nc.vector.tensor_copy(cols, bank(2 + j % 2, 0, T).rearrange("p (t n) -> p t n", t=TT))\
                    .then_inc(qr_copied, 1)
                dve.wait_ge(qr_copied, j + 1)
                v4 = cols.rearrange("p t (h d) -> p t h d", d=64)
                halves = (v4[:, :, :, 0:ROT2], v4[:, :, :, ROT2:64])
                tmp = [rope_tmp[:, q, 0:TT * 2 * ROT2].rearrange("p (t h d) -> p t h d", t=TT, d=ROT2)
                       for q in range(4)]
                rope(halves, halves, trig(cos, ROT1, NA, 2), trig(sin, ROT1, NA, 2), ROT2, tmp)\
                    .then_inc(qr_roped, 1)
            for j in range(2):
                c = AT["ukv"] + j
                lo_before(c)
                dve.wait_ge(w_used, c + 1)
                for t in range(TT):
                    nc.vector.tensor_copy(V[:, t, j * HALF:(j + 1) * HALF], bank(2 + t)).then_inc(v_copied, 1)
            lo_before(AT["mwo"])
            attention(mla, lambda h: (chunked[:, P:T], chunked))
            lo_before(AT["mwo"] + 3)
            post("post0")
            norm("fpre0")
            split_turned("fpre0")
            ffn_layer(ffn[0])
            lo_before(ffn[0].first + 32)
            post("fpost0")
            norm("kvsrc")
            split_turned("kvsrc")
            norm("kvsrc", "pre1")
            for j in range(4):
                lo_before(AT["kvk"] + j)
            for n in range(2):
                c = AT["kvv"] + 2 * n
                lo_before(c + 1)
                dve.wait_ge(w_used, c + 2)
                nc.vector.tensor_copy(V2[:, 1, n * HALF:(n + 1) * HALF], bank(2 * n + 1)).then_inc(v_copied, 1)
            split_turned("pre1")
            lo_before(AT["bwo"])

            def biases(h):
                dve.wait_ge(bias_ready, h + 1)
                return (bias[:, h % 8, P - 1::-1], bias[:, h % 8, ::-1])

            attention(chk, biases)
            lo_before(AT["bwo"] + 3)
            post("post1")
            norm("fpre1")
            split_turned("fpre1")
            ffn_layer(ffn[1])
            post("fpost1")

        @block.tensor
        def _(pe):
            def wait_chunk(value):
                pe.wait_ge(lo_ready_v, value)
                pe.wait_ge(lo_ready_g, value)

            def product(dst, left, right, start, stop, **kw):
                nc.tensor.matmul(dst, lhsT=left[0], rhs=right[0], start=start, stop=False, **kw)
                nc.tensor.matmul(dst, lhsT=left[0], rhs=right[1], start=False, stop=False, **kw)
                return nc.tensor.matmul(dst, lhsT=left[1], rhs=right[0], start=False, stop=stop, **kw)

            def slot(c):
                s = SLOT[c]
                return (whi[:, s, :], wlo[:, s, :])

            def cols(w, lo, hi):
                return (w[0][:, lo:hi], w[1][:, lo:hi])

            def acts(k, lo=0, hi=T):
                return (act_hi[:, k, lo:hi], act_lo[:, k, lo:hi])

            def turn(name, blocks=((0, 4), (4, 8))):
                if name == "mix0":
                    pe.wait_ge(const_loaded, 16)
                for t in range(TT):
                    pe.wait_ge(xs_ready, 2 * XSR[name] + t + 1)
                    for b, (k0, k1) in enumerate(blocks):
                        for k in range(k0, k1):
                            ins = nc.tensor.transpose(bank(4 + 2 * t + b, (k - k0) * P, (k - k0 + 1) * P),
                                                      xs[:, t, k * P:(k + 1) * P], ident)
                        ins.then_inc(turned, 1)

            def wait_acts(name, count=4):
                pe.wait_ge(act_lo_ready, 4 * ACTN[name] + count)

            def rows_out(w, k0, left, first, last, final=False):
                for t in range(TT):
                    for k in range(2):
                        for half in range(2):
                            ins = product(bank(2 * t + half), left(k0 + k, t),
                                          cols(w, k * D + half * HALF, k * D + (half + 1) * HALF),
                                          start=first and k == 0, stop=last and k == 1,
                                          skip_group_check=True)
                    if final and t == 0:
                        ins.then_inc(acc_t0, 1)
                return ins

            def tiles_out(w, b):
                for f in range(2):
                    for k in range(KT):
                        ins = product(bank(b, f * T, (f + 1) * T),
                                      cols(w, k * FC + f * P, k * FC + (f + 1) * P), acts(k),
                                      start=k == 0, stop=k == KT - 1)
                return ins

            def projection(first, name):
                for j in range(4):
                    c = first + j
                    wait_chunk(c + 1)
                    rows_out(slot(c), 2 * j, lambda k, t: acts(k, t * P, (t + 1) * P), j == 0, j == 3,
                             j == 3).then_inc(w_used, 1)

            def attention(at, score, value):
                pairs = at.heads == 16
                for h in range(at.heads + 3):
                    if h < at.heads:
                        if h >= 2:
                            pe.wait_ge(at.maxed, h - 1)
                        for t in range(TT):
                            lo, hi = (0, P) if t == 0 else (P, 3 * P)
                            ins = score(h, t, bank(4 + h % 2, lo, hi))
                        ins.then_inc(at.scored, 1)
                    g = h - 2
                    if 0 <= g < at.heads:
                        pe.wait_ge(at.normed, g + 1)
                        if g >= 1:
                            pe.wait_ge(at.p_copied, g)
                        for b in range(3):
                            ins = nc.tensor.transpose(bank(6, b * P, (b + 1) * P),
                                                      probs[:, g % 3, b * P:(b + 1) * P], ident)
                        ins.then_inc(at.p_turned, 1)
                    g = h - 3
                    if 0 <= g < at.heads:
                        pe.wait_ge(at.p_copied, g + 1)
                        if pairs:
                            if g >= 2:
                                pe.wait_ge(at.o_lo, g // 2)
                            lo = 64 * (g % 2)
                            o = ps[lo:lo + 64, 7 * HALF:7 * HALF + T]
                        else:
                            if g >= 1:
                                pe.wait_ge(at.o_lo, g)
                            o = bank(7, 0, T)
                        nc.tensor.matmul(o, lhsT=value(g, 0), rhs=probsT[:, g % 2, 0:T], start=True, stop=False)
                        nc.tensor.matmul(o[:, P:T], lhsT=value(g, 1), rhs=probsT[:, g % 2, T:3 * P],
                                         start=False, stop=True).then_inc(at.mixed, 1)
                pe.wait_ge(at.o_lo, KT)

            def mlp_layer(f):
                n0 = f.first

                def up(c, i, value, first=False):
                    wait_chunk(value)
                    if not first:
                        pe.wait_ge(f.act_done, i)
                    tiles_out(slot(c), 4).then_inc(w_used, 1)

                def down(c, i, value, first=False, last=False):
                    wait_chunk(value)
                    pe.wait_ge(f.lo_done, i + 1)
                    rows_out(slot(c), 0, lambda k, t: (hhi[:, k, t * P:(t + 1) * P], hlo[:, k, t * P:(t + 1) * P]),
                             first, last, last).then_inc(w_used, 1)

                up(n0, 0, n0 + 1, True)
                up(n0 + 1, 1, n0 + 2)
                down(n0 + 2, 0, n0 + 3, first=True)
                with pe.Fori(0, (NM - 2) // 2) as n:
                    for u in range(2):
                        c = n0 + 3 + 2 * u
                        up(c, n * 2 + 2 + u, n * 4 + (c + 1))
                        down(c + 1, n * 2 + 1 + u, n * 4 + (c + 2))
                down(n0 + 31, NM - 1, n0 + 32, last=True)

            def ffn_layer(f):
                n0 = f.first

                def gate_up(c, i, value, first=False):
                    wait_chunk(value)
                    if not first:
                        pe.wait_ge(f.act_done, i)
                    tiles_out(slot(c), 4).then_inc(w_used, 1)
                    wait_chunk(value + 1)
                    if not first:
                        pe.wait_ge(f.h_done, i)
                    tiles_out(slot(c + 1), 5).then_inc(w_used, 1)

                def down(c, i, value, first=False, last=False):
                    wait_chunk(value)
                    pe.wait_ge(f.lo_done, i + 1)
                    rows_out(slot(c), 0, lambda k, t: (hhi[:, k, t * P:(t + 1) * P], hlo[:, k, t * P:(t + 1) * P]),
                             first, last, last).then_inc(w_used, 1)

                gate_up(n0, 0, n0 + 1, True)
                gate_up(n0 + 2, 1, n0 + 3)
                down(n0 + 4, 0, n0 + 5, first=True)
                with pe.Fori(2, NF) as i:
                    gate_up(n0 + 5, i, i * 3 + (n0 + 6 - 6))
                    down(n0 + 7, i - 1, i * 3 + (n0 + 8 - 6))
                down(n0 + 32, NF - 1, n0 + 33, last=True)

            turn("mix0")
            for n in range(6):
                for kh in range(2):
                    c = 2 * n + kh
                    wait_chunk(c + 1)
                    if c == 0:
                        wait_acts("mix0")
                    if n >= 2 and kh == 0:
                        pe.wait_ge(qkv_a, n - 1)
                        pe.wait_ge(qkv_v, n - 1)
                    for t in range(TT):
                        for k in range(4):
                            ins = product(bank(2 * (n % 2) + t), acts(4 * kh + k, t * P, (t + 1) * P),
                                          cols(slot(c), k * HALF, (k + 1) * HALF),
                                          start=kh == 0 and k == 0, stop=kh == 1 and k == 3)
                    ins.then_inc(w_used, 1)
                if n >= 2:
                    g = n - 2
                    pe.wait_ge(roped, g + 1)
                    if g == 0:
                        wait_acts("mix0")
                    if g >= 2:
                        pe.wait_ge(heads_copied, 2 * (g - 1))
                    for b in range(2):
                        for h in range(2):
                            for t in range(TT):
                                col = g * HALF + (2 * b + h) * HD1
                                ins = nc.tensor.transpose(
                                    bank(4 + 2 * (g % 2) + b, h * T + t * P, h * T + (t + 1) * P),
                                    qk_tok[:, t, col:col + HD1], ident)
                        ins.then_inc(heads_turned, 1)
            pe.wait_ge(heads_copied, 8)
            pe.wait_ge(qkv_a, 6)
            pe.wait_ge(qkv_v, 6)

            def keys(t):
                return slice(0, (t + 1) * P)

            attention(moba,
                      lambda h, t, o: nc.tensor.matmul(o, lhsT=qT[:, h, t * P:(t + 1) * P], rhs=kT[:, h, keys(t)],
                                                       start=True, stop=True),
                      lambda h, k: V[:, k, h * HD1:(h + 1) * HD1])
            projection(AT["wo"], "wo")
            turn("mlp0")
            wait_acts("mlp0")
            mlp_layer(mlp[0])

            for t in range(TT):
                pe.wait_ge(xs_ready, 2 * XSR["mix1"] + t + 1)
            for kk in range(KT):
                g = kk // 2
                o = bank(4 + kk // 2, (kk % 2) * T, (kk % 2 + 1) * T)
                band = C_BAND + g * 3 * P
                nc.tensor.matmul(o, lhsT=xs[:, 0, kk * P:(kk + 1) * P], rhs=const[:, band:band + T],
                                 start=True, stop=False)
                ins = nc.tensor.matmul(o[:, P:T], lhsT=xs[:, 1, kk * P:(kk + 1) * P],
                                       rhs=const[:, band + T:band + T + P], start=False, stop=True)
                if kk % 2:
                    ins.then_inc(pooled, 1)
            c = AT["pool"]
            wait_chunk(c + 1)
            wait_acts("mix1")
            for t in range(TT):
                for g in range(4):
                    for k in range(2):
                        ins = product(bank(2 * t + g // 2, (g % 2) * FC, (g % 2 + 1) * FC),
                                      acts(2 * g + k, t * P, (t + 1) * P),
                                      cols(slot(c), (2 * g + k) * FC, (2 * g + k + 1) * FC),
                                      start=k == 0, stop=k == 1)
            ins.then_inc(w_used, 1)
            turn("mlp1")
            wait_acts("mlp1")
            mlp_layer(mlp[1])

            turn("pre0")
            wait_acts("pre0")
            for j in range(4):
                c = AT["wa"] + j
                wait_chunk(c + 1)
                for t in range(TT):
                    for k in range(2):
                        for b, (lo, hi) in enumerate(((0, HALF), (HALF, 704))):
                            ins = product(bank(2 * t + b, 0, hi - lo), acts(2 * j + k, t * P, (t + 1) * P),
                                          cols(slot(c), k * 704 + lo, k * 704 + hi),
                                          start=j == 0 and k == 0, stop=j == 3 and k == 1, skip_group_check=True)
                    if j == 3 and t == 0:
                        ins.then_inc(acc_wa, 1)
                ins.then_inc(w_used, 1)
            turn("lora", blocks=((0, 4), (4, 6)))
            wait_acts("lora")
            pe.wait_ge(kr_copied, 2)

            def turn_qr(j):
                pe.wait_ge(qr_roped, j + 1)
                if j >= 2:
                    pe.wait_ge(qrT_copied, j - 1)
                for t in range(TT):
                    ins = nc.tensor.transpose(bank(4 + j % 2, t * P, (t + 1) * P),
                                              qr_tok[:, t, 2 * j * 64:(2 * j + 2) * 64], ident)
                ins.then_inc(qr_turned, 1)

            for j in range(4):
                c = AT["uq"] + j
                wait_chunk(c + 1)
                if j >= 2:
                    pe.wait_ge(qn_copied, j - 1)
                    pe.wait_ge(qr_copied, j - 1)
                if j == 0:
                    pe.wait_ge(lora_a, 1)
                    pe.wait_ge(lora_v, 1)
                for h in range(2):
                    for k in range(3):
                        product(bank(j % 2, h * T, (h + 1) * T),
                                cols(slot(c), k * 384 + h * 192, k * 384 + h * 192 + 128), acts(k),
                                start=k == 0, stop=k == 2)
                for t in range(TT):
                    for k in range(3):
                        ropes = tuple(w[:, k * 384:(k + 1) * 384].rearrange("p (h d) -> p h d", d=192)[:, :, 128:192]
                                      for w in slot(c))
                        ins = product(bank(2 + j % 2, t * P, (t + 1) * P), acts(k, t * P, (t + 1) * P), ropes,
                                      start=k == 0, stop=k == 2)
                ins.then_inc(w_used, 1)
                if j >= 1:
                    turn_qr(j - 1)
            for j in range(2):
                c = AT["ukv"] + j
                wait_chunk(c + 1)
                pe.wait_ge(qn_copied, 4)
                pe.wait_ge(qr_copied, 4)
                if j:
                    pe.wait_ge(kn_copied, 2)
                    pe.wait_ge(v_copied, 2)
                for h in range(4):
                    for k in range(2):
                        product(bank(h // 2, (h % 2) * T, (h % 2 + 1) * T),
                                cols(slot(c), k * D + h * 256, k * D + h * 256 + 128), acts(3 + k),
                                start=k == 0, stop=k == 1)
                for t in range(TT):
                    for k in range(2):
                        vals = tuple(w[:, k * D:(k + 1) * D].rearrange("p (h d) -> p h d", d=256)[:, :, 128:256]
                                     for w in slot(c))
                        ins = product(bank(2 + t), acts(3 + k, t * P, (t + 1) * P), vals, start=k == 0, stop=k == 1)
                ins.then_inc(w_used, 1)
                if j == 0:
                    turn_qr(3)
            pe.wait_ge(qrT_copied, 4)
            pe.wait_ge(kn_copied, 4)
            pe.wait_ge(v_copied, 4)

            def mla_score(h, t, o):
                nc.tensor.matmul(o, lhsT=qT[:, h, t * P:(t + 1) * P], rhs=kT[:, h, keys(t)], start=True, stop=False)
                lo = 64 * (h % 2)
                return nc.tensor.matmul(o, lhsT=qrT[lo:lo + 64, h // 2, t * P:(t + 1) * P],
                                        rhs=krT[lo:lo + 64, keys(t)], start=False, stop=True)

            attention(mla, mla_score, lambda h, k: V[:, k, h * HD1:(h + 1) * HD1])
            projection(AT["mwo"], "mwo")
            turn("fpre0")
            wait_acts("fpre0")
            ffn_layer(ffn[0])

            turn("kvsrc")
            wait_acts("kvsrc")
            for j in range(4):
                c = AT["kvk"] + j
                wait_chunk(c + 1)
                if j >= 2:
                    pe.wait_ge(kT_copied, j - 1)
                tiles_out(slot(c), 4 + j % 2).then_inc(w_used, 1)
            for n in range(2):
                for kh in range(2):
                    c = AT["kvv"] + 2 * n + kh
                    wait_chunk(c + 1)
                    for t in range(TT):
                        for k in range(4):
                            ins = product(bank(2 * n + t), acts(4 * kh + k, t * P, (t + 1) * P),
                                          cols(slot(c), k * HALF, (k + 1) * HALF),
                                          start=kh == 0 and k == 0, stop=kh == 1 and k == 3)
                    ins.then_inc(w_used, 1)
            pe.wait_ge(kT_copied, 4)
            turn("pre1")
            wait_acts("pre1")
            for j in range(4):
                c = AT["bq"] + j
                wait_chunk(c + 1)
                if j >= 2:
                    pe.wait_ge(qT_copied, j - 1)
                tiles_out(slot(c), 4 + j % 2).then_inc(w_used, 1)
            pe.wait_ge(qT_copied, 4)
            pe.wait_ge(vs_copied, 2)
            pe.wait_ge(v_copied, 6)

            def chunk_score(h, t, o):
                lo = 64 * (h % 2)
                return nc.tensor.matmul(o, lhsT=qT[lo:lo + 64, h // 2, t * P:(t + 1) * P],
                                        rhs=kT[lo:lo + 64, h // 2, keys(t)], start=True, stop=True)

            attention(chk, chunk_score, lambda h, k: V2[:, k, h * 64:(h + 1) * 64])
            projection(AT["bwo"], "bwo")
            turn("fpre1")
            wait_acts("fpre1")
            ffn_layer(ffn[1])


NAMES = ["x", "positions", "norm_mix", "norm_mlp", "attn_w_qkv", "attn_w_o", "pool_w", "pool_scale",
         "mlp_w_up", "mlp_w_down", "norm_final", "positions_2", "attn_pre_g_2", "attn_post_g_2",
         "ffn_pre_g_2", "ffn_post_g_2", "ffn_w_gate_2", "ffn_w_up_2", "ffn_w_down_2", "mla_w_a_2",
         "mla_g_q_2", "mla_w_uq_2", "mla_g_kv_2", "mla_w_ukv_2", "mla_w_o_2", "kv_src_g_2",
         "w_kv_shared_2", "b_w_q_2", "b_rel_table_2", "b_w_o_2"]


def constants():
    import numpy as np

    c = np.zeros((P, NCONST), np.float32)
    c[:, C_IDENT:C_IDENT + P] = np.eye(P)
    q = np.arange(P)[:, None]
    k = np.arange(P)[None, :]
    c[:, C_CAUSAL + P:C_CAUSAL + T] = np.where(k <= q, 0.0, NEG)
    c[:, C_CHUNKED + P:C_CHUNKED + T] = np.where(k // 64 <= q // 64, 0.0, NEG)
    s = np.arange(T)[:, None]
    t = np.arange(T)[None, :]
    for g, w in enumerate((2, 4, 8, 16)):
        band = np.where((s <= t) & (s > t - w), 1.0 / np.minimum(t + 1, w), 0.0) - (s == t)
        at = C_BAND + g * 3 * P
        c[:, at:at + T] = band[0:P]
        c[:, at + T:at + T + P] = band[P:T, P:T]
    c[:, C_INV:C_INV + ROT1] = np.float32(500000.0) ** (-np.arange(0, 32, 2, dtype=np.float32) / np.float32(32))
    c[:, C_INV + ROT1:] = 1.0 / (np.float32(10000.0) ** (np.arange(0, 64, 2, dtype=np.float32) / np.float32(64)))
    return c


def kernel(**inputs):
    import numpy as np
    import concourse.bacc as bacc
    from concourse.bass_utils import run_bass_kernel_spmd

    nc = bacc.Bacc("TRN2", target_bir_lowering=False, num_devices=1)
    arrays, aps = {}, {}

    def give(name, array):
        arrays[name + "_in"] = array
        aps[name] = nc.dram_tensor(name + "_in", array.shape, mybir.dt.from_np(array.dtype),
                                   kind="ExternalInput").ap()

    for name in NAMES:
        give(name, np.ascontiguousarray(inputs[name]))
    give("const", constants())
    out = nc.dram_tensor("y_out", (1, T, D), F32, kind="ExternalOutput").ap()
    two_blocks(nc, aps, out)
    r = run_bass_kernel_spmd(nc, [arrays], core_ids=[0])
    return r.results[0]["y_out"]
```

```python
from contextlib import ExitStack

import concourse.bass as bass
from concourse import mybir

F32 = mybir.dt.float32
F32R = mybir.dt.float32r
I32 = mybir.dt.int32
ALU = mybir.AluOpType
ACT = mybir.ActivationFunctionType

P = 128
T = 256
TT = T // P
D = 1024
KT = D // P
DFF1 = 4 * D
DFF2 = 2816
W = 2048
SLOTS = 4
HALF = 512
FC = 256
EPS = 1e-6
NEG = -1e30
MIN32 = -3.0e38
MAGIC = 12582912.0
INV_2PI = 0.15915494309189535
PI_A = 6.28125
PI_B = 0.0019350051879882812
PI_C = 2 * 3.141592653589793 - PI_A - PI_B
PI_SAFE = 3.1415925
HALF_PI = 1.5707963267948966
H1, HD1, ROT1 = 8, 128, 16
QL, KVL, ROT2 = 384, 256, 32
H2 = 16
REL = 320

C_IDENT, C_CAUSAL, C_CHUNKED, C_BAND, C_INV = 0, 128, 384, 640, 2176
NCONST = C_INV + ROT1 + ROT2

CHUNKS = []


def plan():
    def add(kind, n, width=W):
        first = len(CHUNKS)
        CHUNKS.extend((kind, i, width) for i in range(n))
        return first

    def mlp(layer):
        first = len(CHUNKS)
        n = DFF1 // FC
        CHUNKS.append(("up", (layer, 0), W))
        for i in range(1, n):
            CHUNKS.extend([("up", (layer, i), W), ("down", (layer, i - 1), W)])
        CHUNKS.append(("down", (layer, n - 1), W))
        return first

    def ffn(layer):
        first = len(CHUNKS)
        n = DFF2 // FC
        CHUNKS.extend([("gate2", (layer, 0), W), ("up2", (layer, 0), W)])
        for i in range(1, n):
            CHUNKS.extend([("gate2", (layer, i), W), ("up2", (layer, i), W), ("down2", (layer, i - 1), W)])
        CHUNKS.append(("down2", (layer, n - 1), W))
        return first

    at = {}
    at["qkv"] = add("qkv", 12)
    at["wo"] = add("wo", 4)
    at["mlp0"] = mlp(0)
    at["pool"] = add("pool", 1)
    at["mlp1"] = mlp(1)
    at["wa"] = add("wa", 4, 2 * 704)
    at["uq"] = add("uq", 4, 3 * 384)
    at["ukv"] = add("ukv", 2)
    at["mwo"] = add("mwo", 4)
    at["ffn0"] = ffn(0)
    at["kvk"] = add("kvk", 4)
    at["kvv"] = add("kvv", 4)
    at["bq"] = add("bq", 4)
    at["bwo"] = add("bwo", 4)
    at["ffn1"] = ffn(1)
    return at


AT = plan()
NCH = len(CHUNKS)
NM = DFF1 // FC
NF = DFF2 // FC


def place():
    ffn = {AT["ffn0"] + m for m in range(2, 3 * NF)} | {AT["ffn1"] + m for m in range(2, 3 * NF)}
    slot, prev, nth = [], [], []
    last = [-SLOTS + s for s in range(SLOTS)]
    count = [0] * SLOTS
    for c in range(NCH):
        s = slot[c - 3] if c in ffn else min(range(SLOTS), key=lambda q: last[q])
        slot.append(s)
        prev.append(max(last[s], -1))
        last[s] = c
        count[s] += 1
        nth.append(count[s])
    return slot, prev, nth


SLOT, PREV, NTH = place()


def due(cursor, w_o, h, heads):
    return PREV[cursor] < w_o + max(0, (h - 4) // (2 if heads == 8 else 4))

ROWS = ["mix0", "mlp0", "mix1", "pool_scale", "mlp1", "final", "pre0", "lora", "post0", "fpre0",
        "fpost0", "kvsrc", "pre1", "post1", "fpre1", "fpost1"]
ROW = {name: i for i, name in enumerate(ROWS)}
ROW_SLOTS = 3
NORMS = ["mix0", "mlp0", "mix1", "mlp1", "final", "pre0", "lora", "post0", "fpre0", "fpost0",
         "kvsrc", "post1", "fpre1", "fpost1"]
NORM = {name: i for i, name in enumerate(NORMS)}


def two_blocks(nc, a, out):
    with ExitStack() as ctx:
        def sb(name, shape, dt=F32):
            return ctx.enter_context(nc.sbuf_tensor(name, shape, dt))

        def sem(name):
            return ctx.enter_context(nc.semaphore(name))

        raw = sb("raw", [P, SLOTS, W])
        whi = sb("whi", [P, SLOTS, W], F32R)
        wlo = sb("wlo", [P, SLOTS, W], F32R)
        x = sb("x", [P, TT, D])
        xs = sb("xs", [P, TT, D])
        junk = sb("junk", [P, D])
        act_hi = sb("act_hi", [P, KT, T], F32R)
        act_lo = sb("act_lo", [P, KT, T], F32R)
        rows = sb("rows", [P, ROW_SLOTS, D])
        const = sb("const", [P, NCONST])
        arena = sb("arena", [P, 8192])
        hhi = sb("hhi", [P, 2, T], F32R)
        hlo = sb("hlo", [P, 2, T], F32R)
        pos_i = sb("pos_i", [P, 2, TT], I32)
        pos_f = sb("pos_f", [P, 2, TT])
        NA = ROT1 + ROT2
        ang = sb("ang", [P, TT, NA])
        turns = sb("turns", [P, TT, NA])
        red = sb("red", [P, TT, NA])
        red2 = sb("red2", [P, TT, NA])
        cos = sb("cos", [P, TT, NA])
        sin = sb("sin", [P, TT, NA])
        stat = sb("stat", [P, 7, 2 * len(NORMS), 2])
        soft = sb("soft", [P, 4, 2 * (8 + 8 + 16)])

        qk_tok = arena[:, 0:4096].rearrange("p (t n) -> p t n", t=TT)
        qT = arena[:, 4096:6144].rearrange("p (h t) -> p h t", t=T)
        kT = arena[:, 6144:8192].rearrange("p (h t) -> p h t", t=T)
        rope_tmp = junk[:, 0:1024].rearrange("p (a n) -> p a n", a=4)
        lora = arena[:, 0:1408].rearrange("p (t n) -> p t n", t=TT)
        qr_tok = arena[:, 1408:2432].rearrange("p (t n) -> p t n", t=TT)
        qrT = arena[:, 2432:3456].rearrange("p (h t) -> p h t", t=T)
        krT = arena[:, 3456:3712]
        relu = arena[:, 0:512]
        hf = arena[:, 512:1024]
        bias = arena[:, 0:2048].rearrange("p (a n) -> p a n", a=8)
        probs = sb("probs", [P, 3, 3 * P])
        probsT = sb("probsT", [P, 2, 3 * P])
        V = xs
        V2 = arena[:, 2048:4096].rearrange("p (t n) -> p t n", t=TT)

        ident = const[:, C_IDENT:C_IDENT + P]
        causal = const[:, C_CAUSAL:C_CAUSAL + T]
        chunked = const[:, C_CHUNKED:C_CHUNKED + T]
        inv = const[:, C_INV:C_INV + NA]

        ps = ctx.enter_context(nc.psum_tensor("ps", [P, 8 * HALF], F32))

        def bank(b, lo=0, hi=HALF):
            return ps[:, b * HALF + lo:b * HALF + hi]

        w_loaded = [sem(f"w_loaded{s}") for s in range(SLOTS)]
        hi_ready = sem("hi_ready")
        lo_ready_v = sem("lo_ready_v")
        lo_ready_g = sem("lo_ready_g")
        w_used = sem("w_used")
        row_loaded = [sem(f"row_loaded{s}") for s in range(ROW_SLOTS)]
        row_used = sem("row_used")
        x_loaded = sem("x_loaded")
        const_loaded = sem("const_loaded")
        pos_loaded = sem("pos_loaded")
        bias_loaded = [sem(f"bias_loaded{s}") for s in range(8)]
        bias_free = sem("bias_free")
        bias_edge = sem("bias_edge")
        bias_ready = sem("bias_ready")
        out_stored = sem("out_stored")
        chain = sem("chain")
        angle_ready = sem("angle_ready")
        trig_ready = sem("trig_ready")
        x_ready = sem("x_ready")
        squares = sem("squares")
        var_ready = sem("var_ready")
        root_ready = sem("root_ready")
        xs_ready = sem("xs_ready")
        turned = sem("turned")
        act_hi_ready = sem("act_hi_ready")
        act_lo_ready = sem("act_lo_ready")
        acc_part = sem("acc_part")
        pool_part = sem("pool_part")
        scale_ready = sem("scale_ready")
        qkv_a = sem("qkv_copied_act")
        qkv_v = sem("qkv_copied_dve")
        roped = sem("roped")
        heads_turned = sem("heads_turned")
        heads_copied = sem("heads_copied")
        pooled = sem("pooled")
        acc_wa = sem("acc_wa")
        lora_a = sem("lora_copied_act")
        lora_v = sem("lora_copied_dve")
        kr_copied = sem("kr_copied")
        kr_roped = sem("kr_roped")
        qn_copied = sem("qn_copied")
        qr_copied = sem("qr_copied")
        qr_turned = sem("qr_turned")
        qr_roped = sem("qr_roped")
        qrT_copied = sem("qrT_copied")
        kn_copied = sem("kn_copied")
        v_copied = sem("v_copied")
        kT_copied = sem("kT_copied")
        vs_copied = sem("vs_copied")
        qT_copied = sem("qT_copied")

        class Ffn:
            def __init__(self, name, first):
                self.first = first
                self.act_done = sem(name + "_act_done")
                self.h_done = sem(name + "_h_done")
                self.hi_done = sem(name + "_hi_done")
                self.lo_done = sem(name + "_lo_done")

        class Attn:
            def __init__(self, name, heads, scale, first_col):
                self.heads, self.scale, self.col = heads, scale, first_col
                self.scored = sem(name + "_scored")
                self.maxed = sem(name + "_maxed")
                self.exped = sem(name + "_exped")
                self.normed = sem(name + "_normed")
                self.p_turned = sem(name + "_p_turned")
                self.p_copied = sem(name + "_p_copied")
                self.mixed = sem(name + "_mixed")
                self.o_hi = sem(name + "_o_hi")
                self.o_lo = sem(name + "_o_lo")

        mlp = [Ffn("mlp0", AT["mlp0"]), Ffn("mlp1", AT["mlp1"])]
        ffn = [Ffn("ffn0", AT["ffn0"]), Ffn("ffn1", AT["ffn1"])]
        moba = Attn("moba", 8, 128.0 ** -0.5, 0)
        mla = Attn("mla", 8, 192.0 ** -0.5, 16)
        chk = Attn("chk", 16, 64.0 ** -0.5, 32)

        XR = {"mix0": 0, "mlp0": 1, "mix1": 2, "mlp1": 3, "final": 4, "pre0": 5, "fpre0": 6,
              "kvsrc": 7, "fpre1": 8}
        TURN = {"mix0": 0, "mlp0": 1, "mlp1": 2, "pre0": 3, "lora": 4, "fpre0": 5, "kvsrc": 6,
                "pre1": 7, "fpre1": 8}
        XSR = {"mix0": 0, "mlp0": 1, "mix1": 2, "mlp1": 3, "pre0": 4, "lora": 5, "fpre0": 6,
               "kvsrc": 7, "pre1": 8, "fpre1": 9}
        ACTN = {"mix0": 0, "mlp0": 1, "mix1": 2, "mlp1": 3, "pre0": 4, "lora": 5, "fpre0": 6,
                "kvsrc": 7, "pre1": 8, "fpre1": 9}
        ACC = {"wo": 0, "mlp0": 1, "mlp1": 2, "mwo": 3, "ffn0": 4, "bwo": 5, "ffn1": 6}

        BY_QUARTERS = ("mlp0", "mix1", "mlp1", "final", "pre0")

        def x_done(name, t):
            return 4 * XR[name] + (3 + t if name in BY_QUARTERS else 2 * (t + 1))

        def quarter(p):
            h, t = p // 2, p % 2
            return h, t, slice(h * HALF, (h + 1) * HALF)

        def act_quarter(acts, p):
            h, t, _ = quarter(p)
            return acts[:, 4 * h:4 * h + 4, t * P:(t + 1) * P]

        block = ctx.enter_context(nc.Block())

        w_qkv = a["attn_w_qkv"][0].rearrange("(h k p) (n f) -> h n p k f", h=2, p=P, f=HALF)
        w_up1 = a["mlp_w_up"].rearrange("l (k p) (n f) -> l n p k f", p=P, f=FC)
        w_down1 = a["mlp_w_down"].rearrange("l (n k p) f -> l n p k f", p=P, k=2)
        w_gate2 = a["ffn_w_gate_2"].rearrange("l (k p) (n f) -> l n p k f", p=P, f=FC)
        w_up2 = a["ffn_w_up_2"].rearrange("l (k p) (n f) -> l n p k f", p=P, f=FC)
        w_down2 = a["ffn_w_down_2"].rearrange("l (n k p) f -> l n p k f", p=P, k=2)

        def two_rows(w):
            return w.rearrange("(n k p) f -> n p k f", p=P, k=2)

        def source(kind, i):
            if kind == "qkv":
                return w_qkv[i % 2, i // 2]
            if kind == "wo":
                return two_rows(a["attn_w_o"][0])[i]
            if kind == "pool":
                return a["pool_w"][0].rearrange("g (k p) f -> p (g k) f", p=P)
            if kind == "wa":
                return two_rows(a["mla_w_a_2"][0])[i]
            if kind == "uq":
                return a["mla_w_uq_2"][0].rearrange("(k p) (n f) -> n p k f", p=P, f=384)[i]
            if kind == "ukv":
                return a["mla_w_ukv_2"][0].rearrange("(k p) (n f) -> n p k f", p=P, f=1024)[i]
            if kind == "mwo":
                return two_rows(a["mla_w_o_2"][0])[i]
            if kind == "kvk":
                return a["w_kv_shared_2"].rearrange("(k p) (n f) -> n p k f", p=P, f=FC)[i]
            if kind == "kvv":
                return a["w_kv_shared_2"].rearrange("(h k p) (n f) -> h n p k f", h=2, p=P, f=HALF)[i % 2, 2 + i // 2]
            if kind == "bq":
                return a["b_w_q_2"][0].rearrange("(k p) (n f) -> n p k f", p=P, f=FC)[i]
            if kind == "bwo":
                return two_rows(a["b_w_o_2"][0])[i]
            return {"up": w_up1, "down": w_down1, "gate2": w_gate2, "up2": w_up2,
                    "down2": w_down2}[kind][i[0], i[1]]

        row_source = {
            "mix0": a["norm_mix"][0:1, :], "mlp0": a["norm_mlp"][0:1, :], "mix1": a["norm_mix"][1:2, :],
            "pool_scale": a["pool_scale"][0:1, :], "mlp1": a["norm_mlp"][1:2, :],
            "final": a["norm_final"].rearrange("(a n) -> a n", a=1),
            "pre0": a["attn_pre_g_2"][0:1, :], "post0": a["attn_post_g_2"][0:1, :],
            "fpre0": a["ffn_pre_g_2"][0:1, :], "fpost0": a["ffn_post_g_2"][0:1, :],
            "kvsrc": a["kv_src_g_2"].rearrange("(a n) -> a n", a=1),
            "pre1": a["attn_pre_g_2"][1:2, :], "post1": a["attn_post_g_2"][1:2, :],
            "fpre1": a["ffn_pre_g_2"][1:2, :], "fpost1": a["ffn_post_g_2"][1:2, :],
        }
        ROW_BYTES_DONE = {}
        seen = [0] * ROW_SLOTS
        for r, name in enumerate(ROWS):
            seen[r % ROW_SLOTS] += 32 if name == "lora" else 16
            ROW_BYTES_DONE[name] = seen[r % ROW_SLOTS]

        def row(name, lo=0, hi=D):
            return rows[:, ROW[name] % ROW_SLOTS, lo:hi]

        def wait_row(eng, name):
            eng.wait_ge(row_loaded[ROW[name] % ROW_SLOTS], ROW_BYTES_DONE[name])

        @block.sync
        def _(sp):
            def load_row(name):
                r = ROW[name]
                s = r % ROW_SLOTS
                if r >= ROW_SLOTS:
                    sp.wait_ge(row_used, r - ROW_SLOTS + 1)
                if name == "lora":
                    sp.dma_start(rows[:, s, 0:QL], a["mla_g_q_2"][0:1, :].partition_broadcast(P)
                                 .rearrange("q a n -> q (a n)")).then_inc(row_loaded[s], 16)
                    sp.dma_start(rows[:, s, QL:QL + KVL], a["mla_g_kv_2"][0:1, :].partition_broadcast(P)
                                 .rearrange("q a n -> q (a n)")).then_inc(row_loaded[s], 16)
                else:
                    sp.dma_start(rows[:, s, :], row_source[name].partition_broadcast(P)
                                 .rearrange("q a n -> q (a n)")).then_inc(row_loaded[s], 16)

            def load(c, s, src, width, freed):
                if freed is not None:
                    sp.wait_ge(lo_ready_v, freed)
                    sp.wait_ge(lo_ready_g, freed)
                sp.dma_start(raw[:, s, 0:width].rearrange("p (k f) -> p k f", f=src.shape[-1]), src)\
                  .then_inc(w_loaded[s], 16)

            def load_one(c):
                kind, i, width = CHUNKS[c]
                load(c, SLOT[c], source(kind, i), width, PREV[c] + 1 if PREV[c] >= 0 else None)

            def load_bias(h):
                if h >= 8:
                    sp.wait_ge(chk.maxed, h - 7)
                table = a["b_rel_table_2"]
                sp.dma_start(bias[0:64, h % 8, 64:T],
                             bass.AP(table.tensor, h * REL, [[1, 64], [1, T - 64]]))\
                  .then_inc(bias_loaded[h % 8], 16)
                sp.dma_start(bias[64:128, h % 8, :],
                             bass.AP(table.tensor, h * REL, [[1, 64], [1, T]]))\
                  .then_inc(bias_loaded[h % 8], 16)

            sp.dma_start(x[:, :, :], a["x"][0].rearrange("(t p) n -> p t n", p=P)).then_inc(x_loaded, 16)
            load_one(0)
            sp.dma_start(const[:, :], a["const"]).then_inc(const_loaded, 16)
            for n, name in enumerate(("positions", "positions_2")):
                sp.dma_start(pos_i[:, n, :], a[name].rearrange("a (t p) -> p (a t)", p=P),
                             allow_slow_non_contiguous=True).then_inc(pos_loaded, 16)
            load_row("mix0")
            for c in range(1, AT["mlp0"]):
                load_one(c)
                if c == 4:
                    load_row("mlp0")
                    load_row("mix1")
                    load_row("pool_scale")
            for layer in range(2):
                n0 = AT[f"mlp{layer}"]
                for m in range(3):
                    load_one(n0 + m)
                if layer == 1:
                    load_row("final")
                    load_row("pre0")
                    load_row("lora")
                with sp.Fori(0, (NM - 2) // 2) as i:
                    for j in range(4):
                        c = n0 + 3 + j
                        src = w_up1[layer, i * 2 + 2 + j // 2] if j % 2 == 0 else w_down1[layer, i * 2 + 1 + j // 2]
                        sp.wait_ge(lo_ready_v, i * 4 + (c - 3))
                        sp.wait_ge(lo_ready_g, i * 4 + (c - 3))
                        sp.dma_start(raw[:, SLOT[c], :].rearrange("p (k f) -> p k f", f=src.shape[-1]), src)\
                          .then_inc(w_loaded[SLOT[c]], 16)
                load_one(n0 + 31)
                if layer == 0:
                    load_one(AT["pool"])
                    load_row("mlp1")
            for c in range(AT["wa"], AT["ffn0"]):
                load_one(c)
                if c == AT["uq"]:
                    load_row("post0")
                    load_row("fpre0")
                if c == AT["mwo"] + 1:
                    load_row("fpost0")
            for layer in range(2):
                n0 = AT[f"ffn{layer}"]
                for m in range(4):
                    load_one(n0 + m)
                if layer == 0:
                    load_row("kvsrc")
                    load_row("pre1")
                with sp.Fori(1, NF - 1) as i:
                    for j, src in enumerate((w_down2[layer, i - 1], w_gate2[layer, i + 1], w_up2[layer, i + 1])):
                        c = n0 + 4 + j
                        sp.wait_ge(lo_ready_v, i * 3 + (c - 3 + 1 - 3))
                        sp.wait_ge(lo_ready_g, i * 3 + (c - 3 + 1 - 3))
                        sp.dma_start(raw[:, SLOT[c], :].rearrange("p (k f) -> p k f", f=src.shape[-1]), src)\
                          .then_inc(w_loaded[SLOT[c]], 16)
                load_one(n0 + 31)
                load_one(n0 + 32)
                if layer == 0:
                    for c in range(AT["kvk"], AT["ffn1"]):
                        load_one(c)
                        if c == AT["kvk"] + 3:
                            load_row("post1")
                            sp.wait_ge(ffn[0].lo_done, NF)
                            sp.wait_ge(bias_edge, 1)
                            for h in range(8):
                                load_bias(h)
                            load_row("fpre1")
                        if c == AT["bwo"] + 3:
                            load_row("fpost1")
                            for h in range(8, 16):
                                load_bias(h)
            for t in range(TT):
                sp.wait_ge(x_ready, 4 * 9 + 2 * (t + 1))
                sp.dma_start(out[0, t * P:(t + 1) * P, :], x[:, t, :]).then_inc(out_stored, 16)
            sp.wait_ge(out_stored, 16 * TT)

        DV = 5

        def cut(width):
            return width * DV // 8

        def scale_bias(pool, h):
            pool.wait_ge(bias_loaded[h % 8], 32 * (h // 8 + 1))
            if h == 0:
                pool.wait_ge(bias_edge, 1)
            nc.gpsimd.tensor_scalar(bias[:, h % 8, :], bias[:, h % 8, :], 8.0, None, ALU.mult)\
                .then_inc(bias_ready, 1)

        @block.gpsimd
        def _(pool):
            def lo_part(s, width, value):
                pool.wait_ge(hi_ready, value)
                w = cut(width)
                nc.gpsimd.tensor_tensor(wlo[:, s, w:width], raw[:, s, w:width],
                                        whi[:, s, w:width].bitcast(F32), ALU.subtract)\
                    .then_inc(lo_ready_g, 1)

            def lo_one(c):
                lo_part(SLOT[c], CHUNKS[c][2], c + 1)

            for c in range(AT["mlp0"]):
                lo_one(c)
            for layer in range(2):
                n0 = AT[f"mlp{layer}"]
                for m in range(3):
                    lo_one(n0 + m)
                with pool.Fori(0, (NM - 2) // 2) as i:
                    for j in range(4):
                        lo_part(SLOT[n0 + 3 + j], W, i * 4 + (n0 + 4 + j))
                lo_one(n0 + 31)
                if layer == 0:
                    lo_one(AT["pool"])
            for c in range(AT["wa"], AT["ffn0"]):
                lo_one(c)
            for layer in range(2):
                n0 = AT[f"ffn{layer}"]
                for m in range(4):
                    lo_one(n0 + m)
                with pool.Fori(1, NF - 1) as i:
                    for j in range(3):
                        lo_part(SLOT[n0 + 4 + j], W, i * 3 + (n0 + 5 + j - 3))
                lo_one(n0 + 31)
                lo_one(n0 + 32)
                if layer == 0:
                    pool.wait_ge(ffn[0].lo_done, NF)
                    nc.gpsimd.memset(bias[:, :, 0:64], NEG).then_inc(bias_edge, 1)
                    for c in range(AT["kvk"], AT["ffn1"]):
                        lo_one(c)
                        if c == AT["bq"]:
                            for h in range(8):
                                scale_bias(pool, h)
                    for h in range(8, 16):
                        scale_bias(pool, h)

        def norm_stat(name, t, what, lo=0, hi=1):
            return stat[:, what, 2 * NORM[name] + t, lo:hi]

        def squares_after(name, t):
            n = 2 * NORM[name] + t + 1
            if NORM[name] > NORM["lora"]:
                n += 2
            elif name == "lora":
                n += t + 1
            return n

        def post_stats(act, sum_squares, root, name, done, acc):
            act.wait_ge(acc_part, 3 * acc + 2)
            sum_squares(name, 0, ps[:, 0:D], D)
            root(name, 0)
            act.wait_ge(w_used, done)
            sum_squares(name, 1, ps[:, D:2 * D], D)
            root(name, 1)

        def copy_heads(act, n):
            dst = qT if n < 2 else kT
            for b in range(2):
                act.wait_ge(heads_turned, 2 * n + b + 1)
                h = 4 * (n % 2) + 2 * b
                nc.scalar.activation(dst[:, h:h + 2, :].rearrange("p h t -> p (h t)"),
                                     bank(4 + 2 * (n % 2) + b), ACT.Copy).then_inc(heads_copied, 1)

        def copy_qr(act, j):
            act.wait_ge(qr_turned, j + 1)
            nc.scalar.activation(qrT[:, j, :], bank(4 + j % 2, 0, T), ACT.Copy).then_inc(qrT_copied, 1)

        @block.scalar
        def _(act):
            cursor = [0]

            def hi_part(s, width, loaded, freed):
                act.wait_ge(w_loaded[s], loaded)
                if freed is not None:
                    act.wait_ge(w_used, freed)
                nc.scalar.activation(whi[:, s, 0:width], raw[:, s, 0:width], ACT.Copy).then_inc(hi_ready, 1)

            def hi_before(c):
                while cursor[0] < NCH and PREV[cursor[0]] < c:
                    hi_next()

            def hi_next():
                q = cursor[0]
                hi_part(SLOT[q], CHUNKS[q][2], 16 * NTH[q], PREV[q] + 1 if PREV[q] >= 0 else None)
                cursor[0] += 1

            def sum_squares(name, t, src, width, col=0):
                nc.scalar.activation(junk[:, col * HALF:col * HALF + width], src, ACT.Square,
                                     accum_out=norm_stat(name, t, 0, col, col + 1)).then_inc(squares, 1)

            def root(name, t, width=1):
                act.wait_ge(var_ready, 2 * NORM[name] + t + 1)
                nc.scalar.activation(norm_stat(name, t, 2, 0, width), norm_stat(name, t, 1, 0, width),
                                     ACT.Sqrt).then_inc(root_ready, 1)

            def stats(name):
                for t in range(TT):
                    act.wait_ge(x_ready, x_done(name, t))
                    if t:
                        act.wait_ge(squares, squares_after(name, 0))
                    sum_squares(name, t, x[:, t, :], D)
                for t in range(TT):
                    root(name, t)

            def copy_turned(name):
                for p in range(4):
                    act.wait_ge(turned, 4 * TURN[name] + p + 1)
                    nc.scalar.activation(act_quarter(act_hi, p), bank(4 + p).rearrange("p (k t) -> p k t", t=P),
                                         ACT.Copy).then_inc(act_hi_ready, 1)

            def attention(at, w_o):
                pairs = at.heads == 16
                for h in range(at.heads + 3):
                    if h < at.heads:
                        act.wait_ge(at.maxed, h + 1)
                        for t in range(TT):
                            lo, hi = (0, P) if t == 0 else (P, 3 * P)
                            c = at.col + 2 * h + t
                            nc.scalar.activation(probs[:, h % 3, lo:hi], probs[:, h % 3, lo:hi], ACT.Exp,
                                                 bias=soft[:, 1, c:c + 1], scale=at.scale,
                                                 accum_out=soft[:, 2, c:c + 1])\
                                .then_inc(at.exped, 1)
                    g = h - 2
                    if 0 <= g < at.heads:
                        act.wait_ge(at.p_turned, g + 1)
                        nc.scalar.activation(probsT[:, g % 2, :], bank(6, 0, 3 * P), ACT.Copy)\
                            .then_inc(at.p_copied, 1)
                    g = h - 3
                    if 0 <= g < at.heads and (not pairs or g % 2):
                        act.wait_ge(at.mixed, g + 1)
                        k = g // 2 if pairs else g
                        nc.scalar.activation(act_hi[:, k, :], bank(7, 0, T), ACT.Copy).then_inc(at.o_hi, 1)
                    if due(cursor[0], w_o, h, at.heads):
                        hi_next()

            def mlp_layer(f, layer):
                n0 = f.first

                def head(i, first):
                    act.wait_ge(w_used, n0 + 1 if first else i * 2 + n0)
                    if not first:
                        act.wait_ge(f.h_done, i)
                    nc.scalar.activation(relu, bank(4), ACT.Relu).then_inc(f.act_done, 1)

                def tail(i, first):
                    act.wait_ge(f.h_done, i + 1)
                    if not first:
                        act.wait_ge(w_used, i * 2 + (n0 + 1))
                    nc.scalar.activation(hhi[:, :, :].rearrange("p k t -> p (k t)"), hf, ACT.Copy)\
                        .then_inc(f.hi_done, 1)

                hi_before(n0)
                head(0, True)
                tail(0, True)
                extra = cursor[0] - (n0 + 3)
                with act.Fori(0, (NM - 2) // 2) as n:
                    for u in range(2):
                        i = n * 2 + 1 + u
                        head(i, False)
                        for m in (3 + 2 * u + extra, 4 + 2 * u + extra):
                            c = n0 + m
                            hi_part(SLOT[c], W, n * 16 + 16 * NTH[c], n * 4 + (c - 3))
                        tail(i, False)
                cursor[0] = n0 + 31 + extra
                head(NM - 1, False)
                hi_before(n0 + 2 * (NM - 1))
                tail(NM - 1, False)

            def ffn_layer(f):
                n0 = f.first

                def head(i, first):
                    act.wait_ge(w_used, n0 + 2 if first else i * 3 + (n0 + 1))
                    if not first:
                        act.wait_ge(f.h_done, i)
                    nc.scalar.activation(relu, bank(4), ACT.Silu).then_inc(f.act_done, 1)

                def tail(i, first):
                    act.wait_ge(f.h_done, i + 1)
                    if not first:
                        act.wait_ge(w_used, i * 3 + (n0 + 2))
                    nc.scalar.activation(hhi[:, :, :].rearrange("p k t -> p (k t)"), hf, ACT.Copy)\
                        .then_inc(f.hi_done, 1)

                def part(c, n):
                    hi_part(SLOT[c], W, n * 16 + 16 * (NTH[c] - 1), n * 3 + (c - 2 - 3))

                hi_before(n0 + 1)
                assert cursor[0] == n0 + 4, (cursor[0], n0)
                head(0, True)
                tail(0, True)
                with act.Fori(1, NF - 1) as i:
                    part(n0 + 4, i)
                    head(i, False)
                    part(n0 + 5, i)
                    part(n0 + 6, i)
                    tail(i, False)
                cursor[0] = n0 + 31
                hi_before(n0 + 3 * (NF - 1))
                head(NF - 1, False)
                hi_before(n0 + 3 * (NF - 1) + 1)
                tail(NF - 1, False)

            act.wait_ge(angle_ready, 1)
            nc.scalar.activation(sin[:, :, :], red[:, :, :], ACT.Sin).then_inc(trig_ready, 1)
            act.wait_ge(angle_ready, 2)
            nc.scalar.activation(cos[:, :, :], red2[:, :, :], ACT.Sin).then_inc(trig_ready, 1)
            hi_before(0)
            copy_turned("mix0")
            stats("mix0")
            act.wait_ge(scale_ready, 2)
            for n in range(6):
                hi_before(2 * n + 1)
                act.wait_ge(w_used, 2 * n + 2)
                dst = qk_tok[:, 0, n * HALF:(n + 1) * HALF] if n < 4 else V[:, 0, (n - 4) * HALF:(n - 3) * HALF]
                nc.scalar.activation(dst, bank(2 * (n % 2)), ACT.Copy, scale=norm_stat("mix0", 0, 6))\
                    .then_inc(qkv_a, 1)
                if n >= 3:
                    copy_heads(act, n - 3)
            copy_heads(act, 3)
            attention(moba, AT["wo"])
            hi_before(AT["wo"] + 2)
            copy_turned("mlp0")
            stats("mlp0")
            mlp_layer(mlp[0], 0)
            hi_before(mlp[0].first + 31)
            stats("mix1")
            for b in range(4):
                act.wait_ge(pooled, b + 1)
                nc.scalar.activation(act_hi[:, 2 * b:2 * b + 2, :].rearrange("p k t -> p (k t)"), bank(4 + b),
                                     ACT.Copy).then_inc(act_hi_ready, 1)
            hi_before(AT["pool"])
            copy_turned("mlp1")
            stats("mlp1")
            mlp_layer(mlp[1], 1)
            hi_before(mlp[1].first + 31)
            stats("final")
            copy_turned("pre0")
            stats("pre0")
            hi_before(AT["wa"] + 3)
            act.wait_ge(scale_ready, 4)
            act.wait_ge(acc_wa, 1)
            nc.scalar.activation(lora[:, 0, :], ps[:, HALF - 352:HALF + 352], ACT.Copy, scale=norm_stat("pre0", 0, 6)).then_inc(lora_a, 1)
            for t in range(TT):
                if t == 0:
                    act.wait_ge(lora_a, 1)
                else:
                    act.wait_ge(lora_v, 1)
                sum_squares("lora", t, lora[:, t, 0:QL], QL, 0)
                sum_squares("lora", t, lora[:, t, QL:QL + KVL], KVL, 1)
                root("lora", t, 2)
            for t in range(TT):
                act.wait_ge(turned, 4 * TURN["lora"] + t + 1)
                nc.scalar.activation(act_hi[:, 0:4, t * P:(t + 1) * P],
                                     bank(4 + t).rearrange("p (k t) -> p k t", t=P), ACT.Copy)\
                    .then_inc(act_hi_ready, 1)
            for t in range(TT):
                act.wait_ge(turned, 4 * TURN["lora"] + t + 3)
                nc.scalar.activation(act_hi[:, 4, t * P:(t + 1) * P], bank(6 + t, 0, P), ACT.Copy)\
                    .then_inc(act_hi_ready, 1)
                nc.scalar.activation(krT[:, t * P:(t + 1) * P], bank(6 + t, P, 2 * P), ACT.Copy)\
                    .then_inc(kr_copied, 1)
            for j in range(4):
                c = AT["uq"] + j
                hi_before(c)
                act.wait_ge(w_used, c + 1)
                nc.scalar.activation(qT[:, 2 * j:2 * j + 2, :].rearrange("p h t -> p (h t)"), bank(j % 2),
                                     ACT.Copy).then_inc(qn_copied, 1)
                if j >= 1:
                    copy_qr(act, j - 1)
            for j in range(2):
                c = AT["ukv"] + j
                hi_before(c)
                act.wait_ge(w_used, c + 1)
                for b in range(2):
                    nc.scalar.activation(kT[:, 4 * j + 2 * b:4 * j + 2 * b + 2, :].rearrange("p h t -> p (h t)"),
                                         bank(b), ACT.Copy).then_inc(kn_copied, 1)
                if j == 0:
                    copy_qr(act, 3)
            attention(mla, AT["mwo"])
            hi_before(AT["mwo"] + 2)
            post_stats(act, sum_squares, root, "post0", AT["mwo"] + 4, ACC["mwo"])
            stats("fpre0")
            copy_turned("fpre0")
            ffn_layer(ffn[0])
            hi_before(ffn[0].first + 32)
            post_stats(act, sum_squares, root, "fpost0", ffn[0].first + 33, ACC["ffn0"])
            stats("kvsrc")
            copy_turned("kvsrc")
            for j in range(4):
                c = AT["kvk"] + j
                hi_before(c)
                act.wait_ge(w_used, c + 1)
                nc.scalar.activation(kT[:, 2 * j:2 * j + 2, :].rearrange("p h t -> p (h t)"), bank(4 + j % 2),
                                     ACT.Copy).then_inc(kT_copied, 1)
            for n in range(2):
                c = AT["kvv"] + 2 * n
                hi_before(c + 1)
                act.wait_ge(w_used, c + 2)
                nc.scalar.activation(V2[:, 0, n * HALF:(n + 1) * HALF], bank(2 * n), ACT.Copy)\
                    .then_inc(vs_copied, 1)
            copy_turned("pre1")
            for j in range(4):
                c = AT["bq"] + j
                hi_before(c)
                act.wait_ge(w_used, c + 1)
                nc.scalar.activation(qT[:, 2 * j:2 * j + 2, :].rearrange("p h t -> p (h t)"), bank(4 + j % 2),
                                     ACT.Copy).then_inc(qT_copied, 1)
            attention(chk, AT["bwo"])
            hi_before(AT["bwo"] + 2)
            post_stats(act, sum_squares, root, "post1", AT["bwo"] + 4, ACC["bwo"])
            stats("fpre1")
            copy_turned("fpre1")
            ffn_layer(ffn[1])
            post_stats(act, sum_squares, root, "fpost1", ffn[1].first + 33, ACC["ffn1"])

        @block.vector
        def _(dve):
            cursor = [0]
            links = [0]

            def link(ins):
                links[0] += 1
                ins.then_inc(chain, 1)
                dve.wait_ge(chain, links[0])

            def lo_part(s, width, value):
                dve.wait_ge(hi_ready, value)
                w = cut(width)
                nc.vector.tensor_tensor(wlo[:, s, 0:w], raw[:, s, 0:w], whi[:, s, 0:w].bitcast(F32),
                                        ALU.subtract).then_inc(lo_ready_v, 1)

            def lo_before(c):
                while cursor[0] < NCH and PREV[cursor[0]] < c:
                    lo_next()

            def lo_next():
                q = cursor[0]
                lo_part(SLOT[q], CHUNKS[q][2], q + 1)
                cursor[0] += 1

            def mean_square(name, t, widths=(D,)):
                dve.wait_ge(squares, squares_after(name, t))
                for i, w in enumerate(widths):
                    ins = nc.vector.tensor_scalar(norm_stat(name, t, 1, i, i + 1), norm_stat(name, t, 0, i, i + 1),
                                                  1.0 / w, EPS, ALU.mult, ALU.add)
                ins.then_inc(var_ready, 1)

            def inverse_root(name, t, widths=(D,), mean=True):
                n = len(widths)

                def st(k, lo=0, hi=n):
                    return norm_stat(name, t, k, lo, hi)

                if mean:
                    mean_square(name, t, widths)
                dve.wait_ge(root_ready, 2 * NORM[name] + t + 1)
                link(nc.vector.reciprocal(st(3), st(2)))
                link(nc.vector.tensor_tensor(st(4), st(3), st(3), ALU.mult))
                link(nc.vector.tensor_tensor(st(5), st(4), st(1), ALU.mult))
                link(nc.vector.tensor_scalar(st(5), st(5), -0.5, 1.5, ALU.mult, ALU.add))
                link(nc.vector.tensor_tensor(st(6), st(5), st(3), ALU.mult))

            def scaled(dst, src, name, t, gain, col=0):
                return nc.vector.scalar_tensor_tensor(out=dst, in0=src, scalar=norm_stat(name, t, 6, col, col + 1),
                                                      in1=gain, op0=ALU.mult, op1=ALU.mult)

            def norm(name, rowname=None):
                rowname = rowname or name
                if rowname == name:
                    for t in range(TT):
                        inverse_root(name, t)
                else:
                    dve.wait_ge(turned, 4 * TURN[name] + 4)
                wait_row(dve, rowname)
                for p in range(4):
                    h, t, cols = quarter(p)
                    scaled(xs[:, t, cols], x[:, t, cols], name, t, row(rowname)[:, cols]).then_inc(xs_ready, 1)
                dve.wait_ge(xs_ready, 4 * XSR[rowname] + 4)
                release_row()

            def late_roots(name, square=False):
                for t in range(TT):
                    inverse_root(name, t)
                    if square:
                        link(nc.vector.tensor_tensor(norm_stat(name, t, 4), norm_stat(name, t, 6),
                                                     norm_stat(name, t, 6), ALU.mult))
                    else:
                        dve.sem_inc(scale_ready, 1)

            def gained(name, p):
                h, t, cols = quarter(p)
                if p == 0:
                    wait_row(dve, name)
                dve.wait_ge(x_ready, 4 * XR[name] + p + 1 if name in BY_QUARTERS else x_done(name, t))
                nc.vector.tensor_tensor(xs[:, t, cols], x[:, t, cols], row(name)[:, cols], ALU.mult)\
                    .then_inc(xs_ready, 1)
                if p == 3:
                    dve.wait_ge(xs_ready, 4 * XSR[name] + 4)
                    release_row()

            def release_row():
                dve.sem_inc(row_used, 1)

            def split_turned(name):
                for p in range(4):
                    dve.wait_ge(act_hi_ready, 4 * ACTN[name] + p + 1)
                    nc.vector.tensor_tensor(act_quarter(act_lo, p), bank(4 + p).rearrange("p (k t) -> p k t", t=P),
                                            act_quarter(act_hi, p).bitcast(F32), ALU.subtract)\
                        .then_inc(act_lo_ready, 1)

            def residual(done, acc, scales=None, then=None):
                for p in range(4):
                    h, t, cols = quarter(p)
                    dve.wait_ge(*((acc_part, 3 * acc + p + 1) if p < 3 else (w_used, done)))
                    part = bank(2 * t + h)
                    if scales:
                        ins = nc.vector.scalar_tensor_tensor(out=x[:, t, cols], in0=part,
                                                             scalar=norm_stat(scales, t, 4),
                                                             in1=x[:, t, cols], op0=ALU.mult, op1=ALU.add)
                    else:
                        ins = nc.vector.tensor_tensor(x[:, t, cols], x[:, t, cols], part, ALU.add)
                    ins.then_inc(x_ready, 1)
                    if then:
                        gained(then, p)

            def post(name):
                wait_row(dve, name)
                for t in range(TT):
                    mean_square(name, t)
                    nc.vector.tensor_tensor(xs[:, t, :], ps[:, t * D:(t + 1) * D], row(name), ALU.mult)
                    inverse_root(name, t, mean=False)
                    nc.vector.scalar_tensor_tensor(out=x[:, t, :], in0=xs[:, t, :], scalar=norm_stat(name, t, 6),
                                                   in1=x[:, t, :], op0=ALU.mult, op1=ALU.add).then_inc(x_ready, 2)
                release_row()

            def rope(src, dst, c, s, n, tmp):
                x1, x2 = src
                y1, y2 = dst
                nc.vector.tensor_tensor(tmp[0], x1, c, ALU.mult)
                nc.vector.tensor_tensor(tmp[1], x2, s, ALU.mult)
                nc.vector.tensor_tensor(tmp[2], x2, c, ALU.mult)
                link(nc.vector.tensor_tensor(tmp[3], x1, s, ALU.mult))
                nc.vector.tensor_tensor(y1, tmp[0], tmp[1], ALU.subtract)
                return nc.vector.tensor_tensor(y2, tmp[2], tmp[3], ALU.add)

            def attention(at, masks, w_o):
                pairs = at.heads == 16
                for h in range(at.heads + 4):
                    g = h - 4
                    if 0 <= g < at.heads and (not pairs or g % 2):
                        k = g // 2 if pairs else g
                        dve.wait_ge(at.o_hi, k + 1)
                        nc.vector.tensor_tensor(act_lo[:, k, :], bank(7, 0, T), act_hi[:, k, :].bitcast(F32),
                                                ALU.subtract).then_inc(at.o_lo, 1)
                    if h < at.heads:
                        mask = masks(h)
                        dve.wait_ge(at.scored, h + 1)
                        c = at.col + 2 * h
                        for t in range(TT):
                            lo, hi = (0, P) if t == 0 else (P, 3 * P)
                            ins = nc.vector.tensor_tensor_reduce(
                                probs[:, h % 3, lo:hi], bank(4 + h % 2, lo, hi), mask[t],
                                1.0, MIN32, ALU.add, ALU.max, soft[:, 0, c + t:c + t + 1])
                        link(ins)
                        nc.vector.tensor_scalar(soft[:, 1, c:c + 2], soft[:, 0, c:c + 2], -at.scale, None,
                                                ALU.mult).then_inc(at.maxed, 1)
                    g = h - 1
                    if 0 <= g < at.heads:
                        dve.wait_ge(at.exped, 2 * g + 2)
                        c = at.col + 2 * g
                        link(nc.vector.reciprocal(soft[:, 3, c:c + 2], soft[:, 2, c:c + 2]))
                        for t in range(TT):
                            lo, hi = (0, P) if t == 0 else (P, 3 * P)
                            ins = nc.vector.tensor_scalar(probs[:, g % 3, lo:hi], probs[:, g % 3, lo:hi],
                                                          soft[:, 3, c + t:c + t + 1], None, ALU.mult)
                        ins.then_inc(at.normed, 1)
                    if h and due(cursor[0], w_o, h - 1, at.heads):
                        lo_next()

            def hidden_lo(f, i):
                dve.wait_ge(f.hi_done, i + 1)
                nc.vector.tensor_tensor(hlo[:, :, :].rearrange("p k t -> p (k t)"), hf,
                                        hhi[:, :, :].rearrange("p k t -> p (k t)").bitcast(F32),
                                        ALU.subtract).then_inc(f.lo_done, 1)

            def mlp_layer(f):
                n0 = f.first

                def square(i, first=False):
                    dve.wait_ge(f.act_done, i + 1)
                    if not first:
                        dve.wait_ge(f.lo_done, i)
                    nc.vector.tensor_tensor(hf, relu, relu, ALU.mult).then_inc(f.h_done, 1)

                lo_before(n0)
                extra = cursor[0] - (n0 + 3)
                square(0, True)
                hidden_lo(f, 0)
                with dve.Fori(0, (NM - 2) // 2) as n:
                    for u in range(2):
                        i = n * 2 + 1 + u
                        square(i)
                        for m in (3 + 2 * u + extra, 4 + 2 * u + extra):
                            lo_part(SLOT[n0 + m], W, n * 4 + (n0 + m + 1))
                        hidden_lo(f, i)
                cursor[0] = n0 + 31 + extra
                square(NM - 1)
                lo_before(n0 + 2 * (NM - 1))
                hidden_lo(f, NM - 1)

            def ffn_layer(f):
                n0 = f.first

                def gated(i, first=False):
                    dve.wait_ge(f.act_done, i + 1)
                    if not first:
                        dve.wait_ge(f.lo_done, i)
                    nc.vector.tensor_tensor(hf, relu, bank(5), ALU.mult).then_inc(f.h_done, 1)

                lo_before(n0 + 1)
                gated(0, True)
                hidden_lo(f, 0)
                with dve.Fori(1, NF - 1) as i:
                    lo_part(SLOT[n0 + 4], W, i * 3 + (n0 + 2))
                    gated(i)
                    lo_part(SLOT[n0 + 5], W, i * 3 + (n0 + 3))
                    lo_part(SLOT[n0 + 6], W, i * 3 + (n0 + 4))
                    hidden_lo(f, i)
                cursor[0] = n0 + 31
                lo_before(n0 + 3 * (NF - 1))
                gated(NF - 1)
                lo_before(n0 + 3 * (NF - 1) + 1)
                hidden_lo(f, NF - 1)

            dve.wait_ge(x_loaded, 16)
            dve.sem_inc(x_ready, 4)
            for p in range(4):
                gained("mix0", p)
            dve.wait_ge(pos_loaded, 32)
            link(nc.vector.tensor_copy(pos_f[:, :, :], pos_i[:, :, :]))
            dve.wait_ge(const_loaded, 16)
            for t in range(TT):
                nc.vector.tensor_scalar(ang[:, t, 0:ROT1], inv[:, 0:ROT1], pos_f[:, 0, t:t + 1], None, ALU.mult)
                ins = nc.vector.tensor_scalar(ang[:, t, ROT1:NA], inv[:, ROT1:NA], pos_f[:, 1, t:t + 1], None,
                                              ALU.mult)
            link(ins)
            link(nc.vector.tensor_scalar(turns[:, :, :], ang[:, :, :], INV_2PI, MAGIC, ALU.mult, ALU.add))
            link(nc.vector.tensor_scalar(turns[:, :, :], turns[:, :, :], -MAGIC, None, ALU.add))
            src = ang
            for n, part in enumerate((PI_A, PI_B, PI_C)):
                dst = red2 if n % 2 else red
                link(nc.vector.scalar_tensor_tensor(out=dst[:, :, :], in0=turns[:, :, :], scalar=-part,
                                                    in1=src[:, :, :], op0=ALU.mult, op1=ALU.add))
                src = dst
            link(nc.vector.tensor_scalar(red[:, :, :], red[:, :, :], PI_SAFE, -PI_SAFE, ALU.min, ALU.max))
            dve.sem_inc(angle_ready, 1)
            link(nc.vector.scalar_tensor_tensor(out=red2[:, :, :], in0=red[:, :, :], scalar=-1.0,
                                                in1=red[:, :, :], op0=ALU.mult, op1=ALU.max))
            nc.vector.tensor_scalar(red2[:, :, :], red2[:, :, :], -1.0, HALF_PI, ALU.mult, ALU.add)\
                .then_inc(angle_ready, 1)
            lo_before(0)
            split_turned("mix0")
            late_roots("mix0")

            def trig(table, lo, hi, heads):
                return table[:, :, lo:hi].unsqueeze(2).broadcast_to([P, TT, heads, hi - lo])

            dve.wait_ge(trig_ready, 2)
            for n in range(6):
                lo_before(2 * n + 1)
                dve.wait_ge(w_used, 2 * n + 2)
                dst = qk_tok[:, 1, n * HALF:(n + 1) * HALF] if n < 4 else V[:, 1, (n - 4) * HALF:(n - 3) * HALF]
                nc.vector.tensor_scalar(dst, bank(2 * (n % 2) + 1), norm_stat("mix0", 1, 6), None, ALU.mult)\
                    .then_inc(qkv_v, 1)
                if n < 4:
                    dve.wait_ge(qkv_v, n + 1)
                    dve.wait_ge(qkv_a, n + 1)
                    v4 = qk_tok[:, :, n * HALF:(n + 1) * HALF].rearrange("p t (h d) -> p t h d", d=HD1)
                    halves = (v4[:, :, :, 0:ROT1], v4[:, :, :, ROT1:2 * ROT1])
                    tmp = [rope_tmp[:, q, 0:TT * 4 * ROT1].rearrange("p (t h d) -> p t h d", t=TT, d=ROT1)
                           for q in range(4)]
                    rope(halves, halves, trig(cos, 0, ROT1, 4), trig(sin, 0, ROT1, 4), ROT1, tmp)\
                        .then_inc(roped, 1)
            attention(moba, lambda h: (causal[:, P:T], causal), AT["wo"])
            lo_before(AT["wo"] + 2)
            residual(AT["wo"] + 4, ACC["wo"], then="mlp0")
            split_turned("mlp0")
            late_roots("mlp0", square=True)
            mlp_layer(mlp[0])
            lo_before(mlp[0].first + 31)
            residual(mlp[0].first + 32, ACC["mlp0"], "mlp0")
            norm("mix1")
            for b in range(4):
                dve.wait_ge(act_hi_ready, 4 * ACTN["mix1"] + b + 1)
                nc.vector.tensor_tensor(act_lo[:, 2 * b:2 * b + 2, :].rearrange("p k t -> p (k t)"), bank(4 + b),
                                        act_hi[:, 2 * b:2 * b + 2, :].rearrange("p k t -> p (k t)").bitcast(F32),
                                        ALU.subtract).then_inc(act_lo_ready, 1)
            lo_before(AT["pool"])
            wait_row(dve, "pool_scale")
            for p in range(4):
                h, t, cols = quarter(p)
                dve.wait_ge(*((pool_part, p + 1) if p < 3 else (w_used, AT["pool"] + 1)))
                link(nc.vector.tensor_tensor(xs[:, t, cols], bank(2 * t + h), row("pool_scale")[:, cols], ALU.mult))
                nc.vector.tensor_tensor(x[:, t, cols], x[:, t, cols], xs[:, t, cols], ALU.add).then_inc(x_ready, 1)
                gained("mlp1", p)
            release_row()
            split_turned("mlp1")
            late_roots("mlp1", square=True)
            mlp_layer(mlp[1])
            lo_before(mlp[1].first + 31)
            residual(mlp[1].first + 32, ACC["mlp1"], "mlp1")
            wait_row(dve, "final")
            for t in range(TT):
                inverse_root("final", t)
            for p in range(4):
                h, t, cols = quarter(p)
                scaled(x[:, t, cols], x[:, t, cols], "final", t, row("final")[:, cols]).then_inc(x_ready, 1)
                gained("pre0", p)
            release_row()
            split_turned("pre0")
            late_roots("pre0")
            lo_before(AT["wa"] + 3)
            dve.wait_ge(w_used, AT["wa"] + 4)
            nc.vector.tensor_scalar(lora[:, 1, :], ps[:, D + HALF - 352:D + HALF + 352], norm_stat("pre0", 1, 6), None, ALU.mult)\
                .then_inc(lora_v, 1)
            wait_row(dve, "lora")
            for t in range(TT):
                inverse_root("lora", t, (QL, KVL))
                scaled(xs[:, t, 0:QL], lora[:, t, 0:QL], "lora", t, row("lora", 0, QL), 0)
                link(scaled(xs[:, t, QL:QL + KVL], lora[:, t, QL:QL + KVL], "lora", t, row("lora", QL, QL + KVL), 1))
                k0 = QL + KVL
                tmp = [rope_tmp[:, q, 0:ROT2] for q in range(4)]
                dve.wait_ge(squares, squares_after("lora", 1))
                link(rope((lora[:, t, k0:k0 + ROT2], lora[:, t, k0 + ROT2:k0 + 2 * ROT2]),
                          (xs[:, t, k0:k0 + ROT2], xs[:, t, k0 + ROT2:k0 + 2 * ROT2]),
                          cos[:, t, ROT1:NA], sin[:, t, ROT1:NA], ROT2, tmp))
                nc.vector.tensor_copy(xs[:, t, k0 + 64:k0 + 128], xs[:, t, k0:k0 + 64])\
                    .then_inc(xs_ready, 1 if t == 0 else 3)
            release_row()
            for p in range(4):
                h, t, _ = quarter(p)
                k0, k1 = (4, 5) if h else (0, 4)
                dve.wait_ge(act_hi_ready, 4 * ACTN["lora"] + p + 1)
                if h:
                    dve.wait_ge(kr_copied, t + 1)
                nc.vector.tensor_tensor(
                    act_lo[:, k0:k1, t * P:(t + 1) * P],
                    bank(4 + p, 0, (k1 - k0) * P).rearrange("p (k t) -> p k t", t=P),
                    act_hi[:, k0:k1, t * P:(t + 1) * P].bitcast(F32), ALU.subtract)\
                    .then_inc(act_lo_ready, 1)
            for j in range(4):
                c = AT["uq"] + j
                lo_before(c)
                dve.wait_ge(w_used, c + 1)
                cols = qr_tok[:, :, 2 * j * 64:(2 * j + 2) * 64]
                nc.vector.tensor_copy(cols, bank(2 + j % 2, 0, T).rearrange("p (t n) -> p t n", t=TT))\
                    .then_inc(qr_copied, 1)
                dve.wait_ge(qr_copied, j + 1)
                v4 = cols.rearrange("p t (h d) -> p t h d", d=64)
                halves = (v4[:, :, :, 0:ROT2], v4[:, :, :, ROT2:64])
                tmp = [rope_tmp[:, q, 0:TT * 2 * ROT2].rearrange("p (t h d) -> p t h d", t=TT, d=ROT2)
                       for q in range(4)]
                rope(halves, halves, trig(cos, ROT1, NA, 2), trig(sin, ROT1, NA, 2), ROT2, tmp)\
                    .then_inc(qr_roped, 1)
            for j in range(2):
                c = AT["ukv"] + j
                lo_before(c)
                dve.wait_ge(w_used, c + 1)
                for t in range(TT):
                    nc.vector.tensor_copy(V[:, t, j * HALF:(j + 1) * HALF], bank(2 + t)).then_inc(v_copied, 1)
            attention(mla, lambda h: (chunked[:, P:T], chunked), AT["mwo"])
            lo_before(AT["mwo"] + 2)
            post("post0")
            norm("fpre0")
            split_turned("fpre0")
            ffn_layer(ffn[0])
            lo_before(ffn[0].first + 32)
            post("fpost0")
            norm("kvsrc")
            split_turned("kvsrc")
            norm("kvsrc", "pre1")
            for j in range(4):
                lo_before(AT["kvk"] + j)
            for n in range(2):
                c = AT["kvv"] + 2 * n
                lo_before(c + 1)
                dve.wait_ge(w_used, c + 2)
                nc.vector.tensor_copy(V2[:, 1, n * HALF:(n + 1) * HALF], bank(2 * n + 1)).then_inc(v_copied, 1)
            split_turned("pre1")
            for j in range(4):
                lo_before(AT["bq"] + j)

            def biases(h):
                dve.wait_ge(bias_ready, h + 1)
                return (bias[:, h % 8, P - 1::-1], bias[:, h % 8, ::-1])

            attention(chk, biases, AT["bwo"])
            lo_before(AT["bwo"] + 2)
            post("post1")
            norm("fpre1")
            split_turned("fpre1")
            ffn_layer(ffn[1])
            post("fpost1")

        @block.tensor
        def _(pe):
            def wait_chunk(value):
                pe.wait_ge(lo_ready_v, value)
                pe.wait_ge(lo_ready_g, value)

            def product(dst, left, right, start, stop, **kw):
                nc.tensor.matmul(dst, lhsT=left[0], rhs=right[0], start=start, stop=False, **kw)
                nc.tensor.matmul(dst, lhsT=left[0], rhs=right[1], start=False, stop=False, **kw)
                return nc.tensor.matmul(dst, lhsT=left[1], rhs=right[0], start=False, stop=stop, **kw)

            def slot(c):
                s = SLOT[c]
                return (whi[:, s, :], wlo[:, s, :])

            def cols(w, lo, hi):
                return (w[0][:, lo:hi], w[1][:, lo:hi])

            def acts(k, lo=0, hi=T):
                return (act_hi[:, k, lo:hi], act_lo[:, k, lo:hi])

            def turn(name, blocks=((0, 4), (4, 8))):
                if name == "mix0":
                    pe.wait_ge(const_loaded, 16)
                for p in range(4):
                    h, t, _ = quarter(p)
                    pe.wait_ge(xs_ready, 4 * XSR[name] + p + 1)
                    k0, k1 = blocks[h]
                    for k in range(k0, k1):
                        ins = nc.tensor.transpose(bank(4 + p, (k - k0) * P, (k - k0 + 1) * P),
                                                  xs[:, t, k * P:(k + 1) * P], ident)
                    ins.then_inc(turned, 1)

            def wait_acts(name, count=4):
                pe.wait_ge(act_lo_ready, 4 * ACTN[name] + count)

            QUARTERS = [(h, t) for h in range(2) for t in range(TT)]
            TILES = [(h, t) for t in range(TT) for h in range(2)]

            def rows_out(w, k0, left, first, last, final=None):
                for n, (half, t) in enumerate(final or TILES):
                    for k in range(2):
                        ins = product(bank(2 * t + half), left(k0 + k, t),
                                      cols(w, k * D + half * HALF, k * D + (half + 1) * HALF),
                                      start=first and k == 0, stop=last and k == 1,
                                      skip_group_check=True)
                    if final and n < 3:
                        ins.then_inc(acc_part, 1)
                return ins

            def tiles_out(w, b, enter=None):
                for f in range(2):
                    for k in range(KT):
                        if enter and f == 0 and k % 4 == 0:
                            wait_acts(enter, 2 + 2 * (k // 4))
                        ins = product(bank(b, f * T, (f + 1) * T),
                                      cols(w, k * FC + f * P, k * FC + (f + 1) * P), acts(k),
                                      start=k == 0, stop=k == KT - 1)
                return ins

            def head_out(first, k, final):
                c = first + k // 2
                if k % 2 == 0:
                    wait_chunk(c + 1)
                if k == KT - 2:
                    rows_out(slot(c), k, lambda k, t: acts(k, t * P, (t + 1) * P), False, True, final)\
                        .then_inc(w_used, 1)
                elif k < KT - 2:
                    at = (k % 2) * D
                    for t in range(TT):
                        for half in range(2):
                            ins = product(bank(2 * t + half), acts(k, t * P, (t + 1) * P),
                                          cols(slot(c), at + half * HALF, at + (half + 1) * HALF),
                                          start=k == 0, stop=False, skip_group_check=True)
                    if k % 2:
                        ins.then_inc(w_used, 1)

            def attention(at, score, value, w_o, final):
                pairs = at.heads == 16
                for h in range(at.heads + 3):
                    if h == 2 and at is moba:
                        qkv_done()
                    if h < at.heads:
                        if h >= 2:
                            pe.wait_ge(at.maxed, h - 1)
                        for t in range(TT):
                            lo, hi = (0, P) if t == 0 else (P, 3 * P)
                            ins = score(h, t, bank(4 + h % 2, lo, hi))
                        ins.then_inc(at.scored, 1)
                    g = h - 2
                    if 0 <= g < at.heads:
                        pe.wait_ge(at.normed, g + 1)
                        if g >= 1:
                            pe.wait_ge(at.p_copied, g)
                        for b in range(3):
                            ins = nc.tensor.transpose(bank(6, b * P, (b + 1) * P),
                                                      probs[:, g % 3, b * P:(b + 1) * P], ident)
                        ins.then_inc(at.p_turned, 1)
                    g = h - 3
                    if 0 <= g < at.heads:
                        pe.wait_ge(at.p_copied, g + 1)
                        if pairs:
                            if g >= 2:
                                pe.wait_ge(at.o_lo, g // 2)
                            lo = 64 * (g % 2)
                            o = ps[lo:lo + 64, 7 * HALF:7 * HALF + T]
                        else:
                            if g >= 1:
                                pe.wait_ge(at.o_lo, g)
                            o = bank(7, 0, T)
                        nc.tensor.matmul(o, lhsT=value(g, 0), rhs=probsT[:, g % 2, 0:T], start=True, stop=False)
                        nc.tensor.matmul(o[:, P:T], lhsT=value(g, 1), rhs=probsT[:, g % 2, T:3 * P],
                                         start=False, stop=True).then_inc(at.mixed, 1)
                    k = (h - 5) // 2 if pairs else h - 4
                    if 0 <= k < KT - 2 and (not pairs or h % 2):
                        pe.wait_ge(at.o_lo, k + 1)
                        head_out(w_o, k, final)
                pe.wait_ge(at.o_lo, KT)
                head_out(w_o, KT - 2, final)

            def mlp_layer(f, norm):
                n0 = f.first

                def up(c, i, value, first=False):
                    wait_chunk(value)
                    if not first:
                        pe.wait_ge(f.act_done, i)
                    tiles_out(slot(c), 4, norm if first else None).then_inc(w_used, 1)

                def down(c, i, value, first=False, last=False):
                    wait_chunk(value)
                    pe.wait_ge(f.lo_done, i + 1)
                    rows_out(slot(c), 0, lambda k, t: (hhi[:, k, t * P:(t + 1) * P], hlo[:, k, t * P:(t + 1) * P]),
                             first, last, QUARTERS if last else None).then_inc(w_used, 1)

                up(n0, 0, n0 + 1, True)
                up(n0 + 1, 1, n0 + 2)
                down(n0 + 2, 0, n0 + 3, first=True)
                with pe.Fori(0, (NM - 2) // 2) as n:
                    for u in range(2):
                        c = n0 + 3 + 2 * u
                        up(c, n * 2 + 2 + u, n * 4 + (c + 1))
                        down(c + 1, n * 2 + 1 + u, n * 4 + (c + 2))
                down(n0 + 31, NM - 1, n0 + 32, last=True)

            def ffn_layer(f, norm):
                n0 = f.first

                def gate_up(c, i, value, first=False):
                    wait_chunk(value)
                    if not first:
                        pe.wait_ge(f.act_done, i)
                    tiles_out(slot(c), 4, norm if first else None).then_inc(w_used, 1)
                    wait_chunk(value + 1)
                    if not first:
                        pe.wait_ge(f.h_done, i)
                    tiles_out(slot(c + 1), 5).then_inc(w_used, 1)

                def down(c, i, value, first=False, last=False):
                    wait_chunk(value)
                    pe.wait_ge(f.lo_done, i + 1)
                    rows_out(slot(c), 0, lambda k, t: (hhi[:, k, t * P:(t + 1) * P], hlo[:, k, t * P:(t + 1) * P]),
                             first, last, TILES if last else None).then_inc(w_used, 1)

                gate_up(n0, 0, n0 + 1, True)
                gate_up(n0 + 2, 1, n0 + 3)
                down(n0 + 4, 0, n0 + 5, first=True)
                with pe.Fori(2, NF) as i:
                    gate_up(n0 + 5, i, i * 3 + (n0 + 6 - 6))
                    down(n0 + 7, i - 1, i * 3 + (n0 + 8 - 6))
                down(n0 + 32, NF - 1, n0 + 33, last=True)

            turn("mix0")
            for n in range(6):
                for kh in range(2):
                    c = 2 * n + kh
                    wait_chunk(c + 1)
                    if n >= 2 and kh == 0:
                        pe.wait_ge(qkv_a, n - 1)
                        pe.wait_ge(qkv_v, n - 1)
                    if n == 0:
                        wait_acts("mix0", 2 * kh + 2)
                    for t in range(TT):
                        for k in range(4):
                            ins = product(bank(2 * (n % 2) + t), acts(4 * kh + k, t * P, (t + 1) * P),
                                          cols(slot(c), k * HALF, (k + 1) * HALF),
                                          start=kh == 0 and k == 0, stop=kh == 1 and k == 3)
                    ins.then_inc(w_used, 1)
                if n >= 2:
                    g = n - 2
                    pe.wait_ge(roped, g + 1)
                    if g == 0:
                        wait_acts("mix0")
                    if g >= 2:
                        pe.wait_ge(heads_copied, 2 * (g - 1))
                    for b in range(2):
                        for h in range(2):
                            for t in range(TT):
                                col = g * HALF + (2 * b + h) * HD1
                                ins = nc.tensor.transpose(
                                    bank(4 + 2 * (g % 2) + b, h * T + t * P, h * T + (t + 1) * P),
                                    qk_tok[:, t, col:col + HD1], ident)
                        ins.then_inc(heads_turned, 1)
            pe.wait_ge(heads_copied, 6)

            def qkv_done():
                pe.wait_ge(heads_copied, 8)
                pe.wait_ge(qkv_a, 6)
                pe.wait_ge(qkv_v, 6)

            def keys(t):
                return slice(0, (t + 1) * P)

            attention(moba,
                      lambda h, t, o: nc.tensor.matmul(o, lhsT=qT[:, h, t * P:(t + 1) * P], rhs=kT[:, h, keys(t)],
                                                       start=True, stop=True),
                      lambda h, k: V[:, k, h * HD1:(h + 1) * HD1], AT["wo"], QUARTERS)
            turn("mlp0")
            mlp_layer(mlp[0], "mlp0")

            for kk in range(KT):
                if kk % 4 == 0:
                    pe.wait_ge(xs_ready, 4 * XSR["mix1"] + 2 + 2 * (kk // 4))
                g = kk // 2
                o = bank(4 + kk // 2, (kk % 2) * T, (kk % 2 + 1) * T)
                band = C_BAND + g * 3 * P
                nc.tensor.matmul(o, lhsT=xs[:, 0, kk * P:(kk + 1) * P], rhs=const[:, band:band + T],
                                 start=True, stop=False)
                ins = nc.tensor.matmul(o[:, P:T], lhsT=xs[:, 1, kk * P:(kk + 1) * P],
                                       rhs=const[:, band + T:band + T + P], start=False, stop=True)
                if kk % 2:
                    ins.then_inc(pooled, 1)
            c = AT["pool"]
            wait_chunk(c + 1)
            for n, (h, t) in enumerate(QUARTERS):
                wait_acts("mix1", 2 * h + 2)
                for g in (2 * h, 2 * h + 1):
                    for k in range(2):
                        ins = product(bank(2 * t + h, (g % 2) * FC, (g % 2 + 1) * FC),
                                      acts(2 * g + k, t * P, (t + 1) * P),
                                      cols(slot(c), (2 * g + k) * FC, (2 * g + k + 1) * FC),
                                      start=k == 0, stop=k == 1)
                ins.then_inc(pool_part if n < 3 else w_used, 1)
            turn("mlp1")
            mlp_layer(mlp[1], "mlp1")

            turn("pre0")
            for j in range(4):
                c = AT["wa"] + j
                wait_chunk(c + 1)
                if j % 2 == 0:
                    wait_acts("pre0", 2 + j)
                for t in range(TT):
                    for k in range(2):
                        for b, (lo, hi) in enumerate(((0, 352), (352, 704))):
                            at = (2 * t + 1) * HALF + (b - 1) * 352
                            ins = product(ps[:, at:at + 352], acts(2 * j + k, t * P, (t + 1) * P),
                                          cols(slot(c), k * 704 + lo, k * 704 + hi),
                                          start=j == 0 and k == 0, stop=j == 3 and k == 1, skip_group_check=True)
                    if j == 3 and t == 0:
                        ins.then_inc(acc_wa, 1)
                ins.then_inc(w_used, 1)
            turn("lora", blocks=((0, 4), (4, 6)))
            wait_acts("lora")
            pe.wait_ge(kr_copied, 2)

            def turn_qr(j):
                pe.wait_ge(qr_roped, j + 1)
                if j >= 2:
                    pe.wait_ge(qrT_copied, j - 1)
                for t in range(TT):
                    ins = nc.tensor.transpose(bank(4 + j % 2, t * P, (t + 1) * P),
                                              qr_tok[:, t, 2 * j * 64:(2 * j + 2) * 64], ident)
                ins.then_inc(qr_turned, 1)

            for j in range(4):
                c = AT["uq"] + j
                wait_chunk(c + 1)
                if j >= 2:
                    pe.wait_ge(qn_copied, j - 1)
                    pe.wait_ge(qr_copied, j - 1)
                if j == 0:
                    pe.wait_ge(lora_a, 1)
                    pe.wait_ge(lora_v, 1)
                for h in range(2):
                    for k in range(3):
                        product(bank(j % 2, h * T, (h + 1) * T),
                                cols(slot(c), k * 384 + h * 192, k * 384 + h * 192 + 128), acts(k),
                                start=k == 0, stop=k == 2)
                for t in range(TT):
                    for k in range(3):
                        ropes = tuple(w[:, k * 384:(k + 1) * 384].rearrange("p (h d) -> p h d", d=192)[:, :, 128:192]
                                      for w in slot(c))
                        ins = product(bank(2 + j % 2, t * P, (t + 1) * P), acts(k, t * P, (t + 1) * P), ropes,
                                      start=k == 0, stop=k == 2)
                ins.then_inc(w_used, 1)
                if j >= 1:
                    turn_qr(j - 1)
            for j in range(2):
                c = AT["ukv"] + j
                wait_chunk(c + 1)
                pe.wait_ge(qn_copied, 4)
                pe.wait_ge(qr_copied, 4)
                if j:
                    pe.wait_ge(kn_copied, 2)
                    pe.wait_ge(v_copied, 2)
                for h in range(4):
                    for k in range(2):
                        product(bank(h // 2, (h % 2) * T, (h % 2 + 1) * T),
                                cols(slot(c), k * D + h * 256, k * D + h * 256 + 128), acts(3 + k),
                                start=k == 0, stop=k == 1)
                for t in range(TT):
                    for k in range(2):
                        vals = tuple(w[:, k * D:(k + 1) * D].rearrange("p (h d) -> p h d", d=256)[:, :, 128:256]
                                     for w in slot(c))
                        ins = product(bank(2 + t), acts(3 + k, t * P, (t + 1) * P), vals, start=k == 0, stop=k == 1)
                ins.then_inc(w_used, 1)
                if j == 0:
                    turn_qr(3)
            pe.wait_ge(qrT_copied, 4)
            pe.wait_ge(kn_copied, 4)
            pe.wait_ge(v_copied, 4)

            def mla_score(h, t, o):
                nc.tensor.matmul(o, lhsT=qT[:, h, t * P:(t + 1) * P], rhs=kT[:, h, keys(t)], start=True, stop=False)
                lo = 64 * (h % 2)
                return nc.tensor.matmul(o, lhsT=qrT[lo:lo + 64, h // 2, t * P:(t + 1) * P],
                                        rhs=krT[lo:lo + 64, keys(t)], start=False, stop=True)

            attention(mla, mla_score, lambda h, k: V[:, k, h * HD1:(h + 1) * HD1], AT["mwo"], TILES)
            turn("fpre0")
            ffn_layer(ffn[0], "fpre0")

            turn("kvsrc")
            for j in range(4):
                c = AT["kvk"] + j
                wait_chunk(c + 1)
                if j >= 2:
                    pe.wait_ge(kT_copied, j - 1)
                tiles_out(slot(c), 4 + j % 2, "kvsrc" if j == 0 else None).then_inc(w_used, 1)
            for n in range(2):
                for kh in range(2):
                    c = AT["kvv"] + 2 * n + kh
                    wait_chunk(c + 1)
                    for t in range(TT):
                        for k in range(4):
                            ins = product(bank(2 * n + t), acts(4 * kh + k, t * P, (t + 1) * P),
                                          cols(slot(c), k * HALF, (k + 1) * HALF),
                                          start=kh == 0 and k == 0, stop=kh == 1 and k == 3)
                    ins.then_inc(w_used, 1)
            pe.wait_ge(kT_copied, 4)
            turn("pre1")
            for j in range(4):
                c = AT["bq"] + j
                wait_chunk(c + 1)
                if j >= 2:
                    pe.wait_ge(qT_copied, j - 1)
                tiles_out(slot(c), 4 + j % 2, "pre1" if j == 0 else None).then_inc(w_used, 1)
            pe.wait_ge(qT_copied, 4)
            pe.wait_ge(vs_copied, 2)
            pe.wait_ge(v_copied, 6)

            def chunk_score(h, t, o):
                lo = 64 * (h % 2)
                return nc.tensor.matmul(o, lhsT=qT[lo:lo + 64, h // 2, t * P:(t + 1) * P],
                                        rhs=kT[lo:lo + 64, h // 2, keys(t)], start=True, stop=True)

            attention(chk, chunk_score, lambda h, k: V2[:, k, h * 64:(h + 1) * 64], AT["bwo"], TILES)
            turn("fpre1")
            ffn_layer(ffn[1], "fpre1")


NAMES = ["x", "positions", "norm_mix", "norm_mlp", "attn_w_qkv", "attn_w_o", "pool_w", "pool_scale",
         "mlp_w_up", "mlp_w_down", "norm_final", "positions_2", "attn_pre_g_2", "attn_post_g_2",
         "ffn_pre_g_2", "ffn_post_g_2", "ffn_w_gate_2", "ffn_w_up_2", "ffn_w_down_2", "mla_w_a_2",
         "mla_g_q_2", "mla_w_uq_2", "mla_g_kv_2", "mla_w_ukv_2", "mla_w_o_2", "kv_src_g_2",
         "w_kv_shared_2", "b_w_q_2", "b_rel_table_2", "b_w_o_2"]


def constants():
    import numpy as np

    c = np.zeros((P, NCONST), np.float32)
    c[:, C_IDENT:C_IDENT + P] = np.eye(P)
    q = np.arange(P)[:, None]
    k = np.arange(P)[None, :]
    c[:, C_CAUSAL + P:C_CAUSAL + T] = np.where(k <= q, 0.0, NEG)
    c[:, C_CHUNKED + P:C_CHUNKED + T] = np.where(k // 64 <= q // 64, 0.0, NEG)
    s = np.arange(T)[:, None]
    t = np.arange(T)[None, :]
    for g, w in enumerate((2, 4, 8, 16)):
        band = np.where((s <= t) & (s > t - w), 1.0 / np.minimum(t + 1, w), 0.0) - (s == t)
        at = C_BAND + g * 3 * P
        c[:, at:at + T] = band[0:P]
        c[:, at + T:at + T + P] = band[P:T, P:T]
    c[:, C_INV:C_INV + ROT1] = np.float32(500000.0) ** (-np.arange(0, 32, 2, dtype=np.float32) / np.float32(32))
    c[:, C_INV + ROT1:] = 1.0 / (np.float32(10000.0) ** (np.arange(0, 64, 2, dtype=np.float32) / np.float32(64)))
    return c


def kernel(**inputs):
    import numpy as np
    import concourse.bacc as bacc
    from concourse.bass_utils import run_bass_kernel_spmd

    nc = bacc.Bacc("TRN2", target_bir_lowering=False, num_devices=1)
    arrays, aps = {}, {}

    def give(name, array):
        arrays[name + "_in"] = array
        aps[name] = nc.dram_tensor(name + "_in", array.shape, mybir.dt.from_np(array.dtype),
                                   kind="ExternalInput").ap()

    for name in NAMES:
        give(name, np.ascontiguousarray(inputs[name]))
    give("const", constants())
    out = nc.dram_tensor("y_out", (1, T, D), F32, kind="ExternalOutput").ap()
    two_blocks(nc, aps, out)
    r = run_bass_kernel_spmd(nc, [arrays], core_ids=[0])
    return r.results[0]["y_out"]
```

```python
from contextlib import ExitStack

import concourse.bass as bass
from concourse import mybir

F32 = mybir.dt.float32
F32R = mybir.dt.float32r
I32 = mybir.dt.int32
ALU = mybir.AluOpType
ACT = mybir.ActivationFunctionType

P = 128
T = 256
TT = T // P
D = 1024
KT = D // P
DFF1 = 4 * D
DFF2 = 2816
W = 2048
SLOTS = 4
HALF = 512
FC = 256
EPS = 1e-6
NEG = -1e30
MIN32 = -3.0e38
MAGIC = 12582912.0
INV_2PI = 0.15915494309189535
PI_A = 6.28125
PI_B = 0.0019350051879882812
PI_C = 2 * 3.141592653589793 - PI_A - PI_B
PI_SAFE = 3.1415925
HALF_PI = 1.5707963267948966
H1, HD1, ROT1 = 8, 128, 16
QL, KVL, ROT2 = 384, 256, 32
REL = 320

C_IDENT = 0
C_INV = C_IDENT + P
C_CAUSAL = C_INV + ROT1 + ROT2
C_CHUNKED = C_CAUSAL + T
C_BAND = C_CHUNKED + T
C_ONES = C_BAND + 4 * 3 * P
NCONST = C_ONES + P

CHUNKS = []


def plan():
    def add(kind, n, width=W):
        first = len(CHUNKS)
        CHUNKS.extend((kind, i, width) for i in range(n))
        return first

    def mlp(layer):
        first = len(CHUNKS)
        n = DFF1 // FC
        CHUNKS.append(("up", (layer, 0), W))
        for i in range(1, n):
            CHUNKS.extend([("up", (layer, i), W), ("down", (layer, i - 1), W)])
        CHUNKS.append(("down", (layer, n - 1), W))
        return first

    def ffn(layer):
        first = len(CHUNKS)
        n = DFF2 // FC
        CHUNKS.extend([("gate2", (layer, 0), W), ("up2", (layer, 0), W)])
        for i in range(1, n):
            CHUNKS.extend([("gate2", (layer, i), W), ("up2", (layer, i), W), ("down2", (layer, i - 1), W)])
        CHUNKS.append(("down2", (layer, n - 1), W))
        return first

    at = {}
    at["qkv"] = add("qkv", 12)
    at["wo"] = add("wo", 4)
    at["mlp0"] = mlp(0)
    at["pool"] = add("pool", 1)
    at["mlp1"] = mlp(1)
    at["wa"] = add("wa", 4, 2 * 704)
    at["uqr"] = add("uqr", 1, 3 * HALF)
    at["uq"] = add("uq", 2, 3 * HALF)
    at["ukv"] = add("ukv", 2)
    at["mwo"] = add("mwo", 4)
    at["ffn0"] = ffn(0)
    at["kvk"] = add("kvk", 4)
    at["kvv"] = add("kvv", 4)
    at["bq"] = add("bq", 4)
    at["bwo"] = add("bwo", 4)
    at["ffn1"] = ffn(1)
    return at


AT = plan()
NCH = len(CHUNKS)
NM = DFF1 // FC
NF = DFF2 // FC


def place():
    ffn = {AT["ffn0"] + m for m in range(2, 3 * NF)} | {AT["ffn1"] + m for m in range(2, 3 * NF)}
    slot, prev, nth = [], [], []
    last = [-SLOTS + s for s in range(SLOTS)]
    count = [0] * SLOTS
    for c in range(NCH):
        s = slot[c - 3] if c in ffn else min(range(SLOTS), key=lambda q: last[q])
        count[s] += QL // P if CHUNKS[c][0] in ("uq", "uqr") else 1
        slot.append(s)
        prev.append(max(last[s], -1))
        last[s] = c
        nth.append(count[s])
    return slot, prev, nth


SLOT, PREV, NTH = place()


def due(cursor, w_o, h, heads):
    return PREV[cursor] < w_o + max(0, (h - 4) // 2 if heads == 8 else (h - 5) // 4)

ROWS = ["mix0", "mlp0", "mix1", "pool_scale", "mlp1", "final", "pre0", "lora", "post0", "fpre0",
        "fpost0", "kvsrc", "pre1", "post1", "fpre1", "fpost1"]
ROW = {name: i for i, name in enumerate(ROWS)}
ROW_SLOTS = 3
NORMS = ["mix0", "mlp0", "mix1", "mlp1", "final", "pre0", "lora", "post0", "fpre0", "fpost0",
         "kvsrc", "post1", "fpre1", "fpost1"]
NORM = {name: i for i, name in enumerate(NORMS)}


def two_blocks(nc, a, out):
    with ExitStack() as ctx:
        def sb(name, shape, dt=F32):
            return ctx.enter_context(nc.sbuf_tensor(name, shape, dt))

        def sem(name):
            return ctx.enter_context(nc.semaphore(name))

        raw = sb("raw", [P, SLOTS, W])
        whi = sb("whi", [P, SLOTS, W], F32R)
        wlo = sb("wlo", [P, SLOTS, W], F32R)
        x = sb("x", [P, TT, D])
        xs = sb("xs", [P, TT, D])
        junk = sb("junk", [P, D])
        act_hi = sb("act_hi", [P, KT, T], F32R)
        act_lo = sb("act_lo", [P, KT, T], F32R)
        rows = sb("rows", [P, ROW_SLOTS, D])
        const = sb("const", [P, NCONST])
        arena = sb("arena", [P, 8192])
        hhi = sb("hhi", [P, 2, T], F32R)
        hlo = sb("hlo", [P, 2, T], F32R)
        last_hhi = sb("last_hhi", [P, 2, T], F32R)
        last_hlo = sb("last_hlo", [P, 2, T], F32R)
        pos_i = sb("pos_i", [P, 2, TT], I32)
        pos_f = sb("pos_f", [P, 2, TT])
        NA = ROT1 + ROT2
        ang = sb("ang", [P, TT, NA])
        turns = sb("turns", [P, TT, NA])
        red = sb("red", [P, TT, NA])
        red2 = sb("red2", [P, TT, NA])
        cos = sb("cos", [P, TT, NA])
        sin = sb("sin", [P, TT, NA])
        stat = sb("stat", [P, 7, 2 * len(NORMS), 2])
        scale_row = sb("scale_row", [P, T])
        soft = sb("soft", [P, 4, 2 * (8 + 8 + 16)])

        qk_tok = arena[:, 0:4096].rearrange("p (t n) -> p t n", t=TT)
        qT = arena[:, 4096:6144].rearrange("p (h t) -> p h t", t=T)
        kT = arena[:, 6144:8192].rearrange("p (h t) -> p h t", t=T)
        rope_tmp = junk[:, 0:1024].rearrange("p (a n) -> p a n", a=4)
        lora = arena[:, 0:1408].rearrange("p (t n) -> p t n", t=TT)
        qr_tok = arena[:, 1408:2432].rearrange("p (t n) -> p t n", t=TT)
        qrT = arena[:, 2432:3456].rearrange("p (h t) -> p h t", t=T)
        krT = arena[:, 3456:3712]
        relu = arena[:, 0:512]
        hf = arena[:, 512:1024]
        gate = arena[:, 1024:1536]
        bias = arena[:, 0:2048].rearrange("p (a n) -> p a n", a=8)
        probs = sb("probs", [P, 3, 3 * P])
        probsT = sb("probsT", [P, 2, 3 * P])
        V = xs
        V2 = arena[:, 2048:4096].rearrange("p (t n) -> p t n", t=TT)

        ident = const[:, C_IDENT:C_IDENT + P]
        causal = const[:, C_CAUSAL:C_CAUSAL + T]
        chunked = const[:, C_CHUNKED:C_CHUNKED + T]
        inv = const[:, C_INV:C_INV + NA]

        ps = ctx.enter_context(nc.psum_tensor("ps", [P, 8 * HALF], F32))

        def bank(b, lo=0, hi=HALF):
            return ps[:, b * HALF + lo:b * HALF + hi]

        w_loaded = [sem(f"w_loaded{s}") for s in range(SLOTS)]
        hi_ready = sem("hi_ready")
        lo_ready_v = sem("lo_ready_v")
        lo_ready_g = sem("lo_ready_g")
        w_used = sem("w_used")
        row_loaded = [sem(f"row_loaded{s}") for s in range(ROW_SLOTS)]
        row_used = sem("row_used")
        x_loaded = sem("x_loaded")
        const_loaded = sem("const_loaded")
        masks_loaded = sem("masks_loaded")
        pos_loaded = sem("pos_loaded")
        bias_loaded = [sem(f"bias_loaded{s}") for s in range(8)]
        bias_free = sem("bias_free")
        bias_edge = sem("bias_edge")
        bias_ready = sem("bias_ready")
        out_stored = sem("out_stored")
        chain = sem("chain")
        angle_ready = sem("angle_ready")
        trig_ready = sem("trig_ready")
        x_ready = sem("x_ready")
        squares = sem("squares")
        var_ready = sem("var_ready")
        root_ready = sem("root_ready")
        xs_ready = sem("xs_ready")
        turned = sem("turned")
        act_hi_ready = sem("act_hi_ready")
        act_lo_ready = sem("act_lo_ready")
        acc_part = sem("acc_part")
        pool_part = sem("pool_part")
        scale_ready = sem("scale_ready")
        diagonal_ready = sem("diagonal_ready")
        scale_row_made = sem("scale_row_made")
        qkv_a = sem("qkv_copied_act")
        qkv_v = sem("qkv_copied_dve")
        roped = sem("roped")
        heads_turned = sem("heads_turned")
        heads_copied = sem("heads_copied")
        pooled = sem("pooled")
        acc_wa = sem("acc_wa")
        lora_a = sem("lora_copied_act")
        lora_v = sem("lora_copied_dve")
        kr_copied = sem("kr_copied")
        kr_roped = sem("kr_roped")
        qn_copied = sem("qn_copied")
        qr_copied = sem("qr_copied")
        qr_turned = sem("qr_turned")
        qr_roped = sem("qr_roped")
        qrT_copied = sem("qrT_copied")
        kn_copied = sem("kn_copied")
        v_copied = sem("v_copied")
        kT_copied = sem("kT_copied")
        vs_copied = sem("vs_copied")
        qT_copied = sem("qT_copied")

        class Ffn:
            def __init__(self, name, first):
                self.first = first
                self.scaled = sem(name + "_scaled")
                self.act_done = sem(name + "_act_done")
                self.h_done = sem(name + "_h_done")
                self.hi_done = sem(name + "_hi_done")
                self.lo_done = sem(name + "_lo_done")

        class Attn:
            def __init__(self, name, heads, scale, first_col):
                self.heads, self.scale, self.col = heads, scale, first_col
                self.scored = sem(name + "_scored")
                self.maxed = sem(name + "_maxed")
                self.exped = sem(name + "_exped")
                self.normed = sem(name + "_normed")
                self.p_turned = sem(name + "_p_turned")
                self.p_copied = sem(name + "_p_copied")
                self.mixed = sem(name + "_mixed")
                self.o_hi = sem(name + "_o_hi")
                self.o_lo = sem(name + "_o_lo")

        mlp = [Ffn("mlp0", AT["mlp0"]), Ffn("mlp1", AT["mlp1"])]
        ffn = [Ffn("ffn0", AT["ffn0"]), Ffn("ffn1", AT["ffn1"])]
        moba = Attn("moba", 8, 128.0 ** -0.5, 0)
        mla = Attn("mla", 8, 192.0 ** -0.5, 16)
        chk = Attn("chk", 16, 64.0 ** -0.5, 32)

        XR = {"mix0": 0, "mlp0": 1, "mix1": 2, "mlp1": 3, "final": 4, "pre0": 5, "fpre0": 6,
              "kvsrc": 7, "pre1": 7, "fpre1": 8}
        TURN = {"mix0": 0, "mlp0": 1, "mlp1": 2, "pre0": 3, "lora": 4, "fpre0": 5, "kvsrc": 6,
                "pre1": 7, "fpre1": 8}
        XSR = {"mix0": 0, "mlp0": 1, "mix1": 2, "mlp1": 3, "pre0": 4, "lora": 5, "fpre0": 6,
               "kvsrc": 7, "pre1": 8, "fpre1": 9}
        ACTN = {"mix0": 0, "mlp0": 1, "mix1": 2, "mlp1": 3, "pre0": 4, "lora": 5, "fpre0": 6,
                "kvsrc": 7, "pre1": 8, "fpre1": 9}
        ACC = {"wo": 0, "mlp0": 1, "mlp1": 2, "mwo": 3, "ffn0": 4, "bwo": 5, "ffn1": 6}


        BY_QUARTERS = ("mlp0", "mix1", "mlp1", "final", "pre0")

        def x_done(name, t):
            return 4 * XR[name] + (3 + t if name in BY_QUARTERS else 2 * (t + 1))

        BY_TILES = ("fpre0", "kvsrc", "pre1", "fpre1")
        SPREAD = {"fpre0": 0, "kvsrc": 1, "fpre1": 2}

        def quarter(name, p):
            h, t = (p % 2, p // 2) if name in BY_TILES else (p // 2, p % 2)
            return h, t, slice(h * HALF, (h + 1) * HALF)

        def act_quarter(acts, name, p):
            h, t, _ = quarter(name, p)
            return acts[:, 4 * h:4 * h + 4, t * P:(t + 1) * P]

        def by_token(ap):
            return ap.rearrange("p (f t) -> p f t", t=T)

        scales_2 = scale_row[:, :].unsqueeze(1).broadcast_to([P, 2, T])

        block = ctx.enter_context(nc.Block())

        w_qkv = a["attn_w_qkv"][0].rearrange("(h k p) (n f) -> h n p k f", h=2, p=P, f=HALF)
        w_up1 = a["mlp_w_up"].rearrange("l (k p) (n f) -> l n p k f", p=P, f=FC)
        w_down1 = a["mlp_w_down"].rearrange("l (n k p) f -> l n p k f", p=P, k=2)
        w_gate2 = a["ffn_w_gate_2"].rearrange("l (k p) (n f) -> l n p k f", p=P, f=FC)
        w_up2 = a["ffn_w_up_2"].rearrange("l (k p) (n f) -> l n p k f", p=P, f=FC)
        w_down2 = a["ffn_w_down_2"].rearrange("l (n k p) f -> l n p k f", p=P, k=2)

        def two_rows(w):
            return w.rearrange("(n k p) f -> n p k f", p=P, k=2)

        def source(kind, i):
            if kind == "qkv":
                return w_qkv[i % 2, i // 2]
            if kind == "wo":
                return two_rows(a["attn_w_o"][0])[i]
            if kind == "pool":
                return a["pool_w"][0].rearrange("g (k p) f -> p (g k) f", p=P)
            if kind == "wa":
                return two_rows(a["mla_w_a_2"][0])[i]
            if kind == "uqr":
                return a["mla_w_uq_2"][0].rearrange("(k p) (h d) -> p k h d", p=P, d=192)[:, :, :, 128:192]
            if kind == "uq":
                return a["mla_w_uq_2"][0].rearrange("(k p) (h d) -> p k h d", p=P, d=192)[:, :, 4 * i:4 * i + 4, 0:128]
            if kind == "ukv":
                return a["mla_w_ukv_2"][0].rearrange("(k p) (n f) -> n p k f", p=P, f=1024)[i]
            if kind == "mwo":
                return two_rows(a["mla_w_o_2"][0])[i]
            if kind == "kvk":
                return a["w_kv_shared_2"].rearrange("(k p) (n f) -> n p k f", p=P, f=FC)[i]
            if kind == "kvv":
                return a["w_kv_shared_2"].rearrange("(h k p) (n f) -> h n p k f", h=2, p=P, f=HALF)[i % 2, 2 + i // 2]
            if kind == "bq":
                return a["b_w_q_2"][0].rearrange("(k p) (n f) -> n p k f", p=P, f=FC)[i]
            if kind == "bwo":
                return two_rows(a["b_w_o_2"][0])[i]
            return {"up": w_up1, "down": w_down1, "gate2": w_gate2, "up2": w_up2,
                    "down2": w_down2}[kind][i[0], i[1]]

        row_source = {
            "mix0": a["norm_mix"][0:1, :], "mlp0": a["norm_mlp"][0:1, :], "mix1": a["norm_mix"][1:2, :],
            "pool_scale": a["pool_scale"][0:1, :], "mlp1": a["norm_mlp"][1:2, :],
            "final": a["norm_final"].rearrange("(a n) -> a n", a=1),
            "pre0": a["attn_pre_g_2"][0:1, :], "post0": a["attn_post_g_2"][0:1, :],
            "fpre0": a["ffn_pre_g_2"][0:1, :], "fpost0": a["ffn_post_g_2"][0:1, :],
            "kvsrc": a["kv_src_g_2"].rearrange("(a n) -> a n", a=1),
            "pre1": a["attn_pre_g_2"][1:2, :], "post1": a["attn_post_g_2"][1:2, :],
            "fpre1": a["ffn_pre_g_2"][1:2, :], "fpost1": a["ffn_post_g_2"][1:2, :],
        }
        ROW_LANDED = {}
        seen = [0] * ROW_SLOTS
        for r, name in enumerate(ROWS):
            seen[r % ROW_SLOTS] += 32 if name == "lora" else 16
            ROW_LANDED[name] = seen[r % ROW_SLOTS]

        def row(name, lo=0, hi=D):
            return rows[:, ROW[name] % ROW_SLOTS, lo:hi]

        def wait_row(eng, name):
            eng.wait_ge(row_loaded[ROW[name] % ROW_SLOTS], ROW_LANDED[name])

        @block.sync
        def _(sp):
            def load_row(name):
                r = ROW[name]
                s = r % ROW_SLOTS
                if r >= ROW_SLOTS:
                    sp.wait_ge(row_used, r - ROW_SLOTS + 1)
                if name == "lora":
                    sp.dma_start(rows[:, s, 0:QL], a["mla_g_q_2"][0:1, :].partition_broadcast(P)
                                 .rearrange("q a n -> q (a n)")).then_inc(row_loaded[s], 16)
                    sp.dma_start(rows[:, s, QL:QL + KVL], a["mla_g_kv_2"][0:1, :].partition_broadcast(P)
                                 .rearrange("q a n -> q (a n)")).then_inc(row_loaded[s], 16)
                else:
                    sp.dma_start(rows[:, s, :], row_source[name].partition_broadcast(P)
                                 .rearrange("q a n -> q (a n)")).then_inc(row_loaded[s], 16)

            def load(c, s, src, width, freed):
                if freed is not None:
                    sp.wait_ge(lo_ready_v, freed)
                    sp.wait_ge(lo_ready_g, freed)
                sp.dma_start(raw[:, s, 0:width].rearrange("p (k f) -> p k f", f=src.shape[-1]), src)\
                  .then_inc(w_loaded[s], 16)

            def load_one(c):
                kind, i, width = CHUNKS[c]
                if kind in ("uq", "uqr"):
                    s, n = SLOT[c], QL // P
                    sp.wait_ge(lo_ready_v, PREV[c] + 1)
                    sp.wait_ge(lo_ready_g, PREV[c] + 1)
                    src = source(kind, i)
                    dst = raw[:, s, 0:width].rearrange("p (k h d) -> p k h d", k=n, d=src.shape[-1])
                    for k in range(n):
                        sp.dma_start(dst[:, k], src[:, k]).then_inc(w_loaded[s], 16)
                    return
                load(c, SLOT[c], source(kind, i), width, PREV[c] + 1 if PREV[c] >= 0 else None)

            def load_bias(h):
                if h >= 8:
                    sp.wait_ge(chk.maxed, h - 7)
                table = a["b_rel_table_2"]
                sp.dma_start(bias[0:64, h % 8, 64:T],
                             bass.AP(table.tensor, h * REL, [[1, 64], [1, T - 64]]))\
                  .then_inc(bias_loaded[h % 8], 16)
                sp.dma_start(bias[64:128, h % 8, :],
                             bass.AP(table.tensor, h * REL, [[1, 64], [1, T]]))\
                  .then_inc(bias_loaded[h % 8], 16)

            sp.dma_start(x[:, :, :], a["x"][0].rearrange("(t p) n -> p t n", p=P)).then_inc(x_loaded, 16)
            load_row("mix0")
            sp.dma_start(const[:, 0:C_CAUSAL], a["const"][:, 0:C_CAUSAL]).then_inc(const_loaded, 16)
            load_one(0)
            load_one(1)
            for n, name in enumerate(("positions", "positions_2")):
                sp.dma_start(pos_i[:, n, :], a[name].rearrange("a (t p) -> p (a t)", p=P),
                             allow_slow_non_contiguous=True).then_inc(pos_loaded, 16)
            for c in range(2, AT["mlp0"]):
                load_one(c)
                if c == 5:
                    sp.dma_start(const[:, C_CAUSAL:NCONST], a["const"][:, C_CAUSAL:NCONST])\
                      .then_inc(masks_loaded, 16)
                    load_row("mlp0")
                    load_row("mix1")
                    load_row("pool_scale")
            for layer in range(2):
                n0 = AT[f"mlp{layer}"]
                for m in range(3):
                    load_one(n0 + m)
                if layer == 1:
                    load_row("final")
                    load_row("pre0")
                    load_row("lora")
                with sp.Fori(0, (NM - 2) // 2) as i:
                    for j in range(4):
                        c = n0 + 3 + j
                        src = w_up1[layer, i * 2 + 2 + j // 2] if j % 2 == 0 else w_down1[layer, i * 2 + 1 + j // 2]
                        sp.wait_ge(lo_ready_v, i * 4 + (c - 3))
                        sp.wait_ge(lo_ready_g, i * 4 + (c - 3))
                        sp.dma_start(raw[:, SLOT[c], :].rearrange("p (k f) -> p k f", f=src.shape[-1]), src)\
                          .then_inc(w_loaded[SLOT[c]], 16)
                load_one(n0 + 31)
                if layer == 0:
                    load_one(AT["pool"])
                    load_row("mlp1")
            for c in range(AT["wa"], AT["ffn0"]):
                load_one(c)
                if c == AT["uqr"]:
                    load_row("post0")
                    load_row("fpre0")
                if c == AT["mwo"] + 1:
                    load_row("fpost0")
            for layer in range(2):
                n0 = AT[f"ffn{layer}"]
                for m in range(4):
                    load_one(n0 + m)
                if layer == 0:
                    load_row("kvsrc")
                    load_row("pre1")
                with sp.Fori(1, NF - 1) as i:
                    for j, src in enumerate((w_down2[layer, i - 1], w_gate2[layer, i + 1], w_up2[layer, i + 1])):
                        c = n0 + 4 + j
                        sp.wait_ge(lo_ready_v, i * 3 + (c - 3 + 1 - 3))
                        sp.wait_ge(lo_ready_g, i * 3 + (c - 3 + 1 - 3))
                        sp.dma_start(raw[:, SLOT[c], :].rearrange("p (k f) -> p k f", f=src.shape[-1]), src)\
                          .then_inc(w_loaded[SLOT[c]], 16)
                load_one(n0 + 31)
                load_one(n0 + 32)
                if layer == 0:
                    for c in range(AT["kvk"], AT["ffn1"]):
                        load_one(c)
                        if c == AT["kvk"] + 3:
                            load_row("post1")
                            sp.wait_ge(ffn[0].lo_done, NF)
                            sp.wait_ge(bias_edge, 1)
                            for h in range(8):
                                load_bias(h)
                            load_row("fpre1")
                        if c == AT["bwo"] + 3:
                            load_row("fpost1")
                            for h in range(8, 16):
                                load_bias(h)
            for t in range(TT):
                sp.wait_ge(x_ready, 4 * 9 + 2 * (t + 1))
                sp.dma_start(out[0, t * P:(t + 1) * P, :], x[:, t, :]).then_inc(out_stored, 16)
            sp.wait_ge(out_stored, 16 * TT)

        DV = 5

        def cut(width):
            return width * DV // 8

        def scale_bias(pool, h):
            pool.wait_ge(bias_loaded[h % 8], 32 * (h // 8 + 1))
            if h == 0:
                pool.wait_ge(bias_edge, 1)
            nc.gpsimd.tensor_scalar(bias[:, h % 8, :], bias[:, h % 8, :], 8.0, None, ALU.mult)\
                .then_inc(bias_ready, 1)

        BOTH = "both token tiles"

        def norm_stat(name, t, what, lo=0, hi=1):
            n = 2 * NORM[name]
            return stat[:, what, n:n + 2, 0] if t is BOTH else stat[:, what, n + t, lo:hi]

        def squares_after(name, t):
            n = 2 * NORM[name] + t + 1
            if NORM[name] > NORM["lora"]:
                n += 2
            elif name == "lora":
                n += t + 1
            return n

        @block.gpsimd
        def _(pool):
            def lo_part(s, width, value):
                pool.wait_ge(hi_ready, value)
                w = cut(width)
                nc.gpsimd.tensor_tensor(wlo[:, s, w:width], raw[:, s, w:width],
                                        whi[:, s, w:width].bitcast(F32), ALU.subtract)\
                    .then_inc(lo_ready_g, 1)

            def lo_one(c):
                lo_part(SLOT[c], CHUNKS[c][2], c + 1)

            for c in range(AT["mlp0"]):
                lo_one(c)
            for layer in range(2):
                n0 = AT[f"mlp{layer}"]
                for m in range(3):
                    lo_one(n0 + m)
                with pool.Fori(0, (NM - 2) // 2) as i:
                    for j in range(4):
                        lo_part(SLOT[n0 + 3 + j], W, i * 4 + (n0 + 4 + j))
                lo_one(n0 + 31)
                if layer == 0:
                    lo_one(AT["pool"])
            for c in range(AT["wa"], AT["ffn0"]):
                lo_one(c)
            for layer in range(2):
                n0 = AT[f"ffn{layer}"]
                for m in range(4):
                    lo_one(n0 + m)
                with pool.Fori(1, NF - 1) as i:
                    for j in range(3):
                        lo_part(SLOT[n0 + 4 + j], W, i * 3 + (n0 + 5 + j - 3))
                lo_one(n0 + 31)
                lo_one(n0 + 32)
                if layer == 0:
                    pool.wait_ge(ffn[0].lo_done, NF)
                    nc.gpsimd.memset(bias[:, :, 0:64], NEG).then_inc(bias_edge, 1)
                    for c in range(AT["kvk"], AT["ffn1"]):
                        lo_one(c)
                        if c == AT["bq"]:
                            for h in range(8):
                                scale_bias(pool, h)
                    for h in range(8, 16):
                        scale_bias(pool, h)

        def post_stats(act, sum_squares, root, name, done, acc):
            act.wait_ge(acc_part, 3 * acc + 2)
            sum_squares(name, 0, ps[:, 0:D], D)
            root(name, 0)
            act.wait_ge(w_used, done)
            sum_squares(name, 1, ps[:, D:2 * D], D)
            root(name, 1)

        def copy_heads(act, n):
            dst = qT if n < 2 else kT
            for b in range(2):
                act.wait_ge(heads_turned, 2 * n + b + 1)
                h = 4 * (n % 2) + 2 * b
                nc.scalar.activation(dst[:, h:h + 2, :].rearrange("p h t -> p (h t)"),
                                     bank(4 + 2 * (n % 2) + b), ACT.Copy).then_inc(heads_copied, 1)

        def copy_qr(act, j):
            act.wait_ge(qr_turned, j + 1)
            nc.scalar.activation(qrT[:, 2 * j:2 * j + 2, :].rearrange("p h t -> p (h t)"), bank(4 + j), ACT.Copy)\
                .then_inc(qrT_copied, 1)

        @block.scalar
        def _(act):
            cursor = [0]

            def hi_part(s, width, loaded, freed):
                act.wait_ge(w_loaded[s], loaded)
                if freed is not None:
                    act.wait_ge(w_used, freed)
                nc.scalar.activation(whi[:, s, 0:width], raw[:, s, 0:width], ACT.Copy).then_inc(hi_ready, 1)

            def hi_before(c):
                while cursor[0] < NCH and PREV[cursor[0]] < c:
                    hi_next()

            def hi_next():
                q = cursor[0]
                hi_part(SLOT[q], CHUNKS[q][2], 16 * NTH[q], PREV[q] + 1 if PREV[q] >= 0 else None)
                cursor[0] += 1

            def sum_squares(name, t, src, width, col=0):
                nc.scalar.activation(junk[:, col * HALF:col * HALF + width], src, ACT.Square,
                                     accum_out=norm_stat(name, t, 0, col, col + 1)).then_inc(squares, 1)

            def root(name, t, width=1):
                count = 2 if t is BOTH else 1
                act.wait_ge(var_ready, 2 * NORM[name] + (2 if t is BOTH else t + 1))
                nc.scalar.activation(norm_stat(name, t, 2, 0, width), norm_stat(name, t, 1, 0, width),
                                     ACT.Sqrt).then_inc(root_ready, count)

            def stats(name):
                for t in range(TT):
                    act.wait_ge(x_ready, x_done(name, t))
                    if t:
                        act.wait_ge(squares, squares_after(name, 0))
                    sum_squares(name, t, x[:, t, :], D)
                root(name, BOTH)

            def copy_turned(name):
                for p in range(4):
                    act.wait_ge(turned, 4 * TURN[name] + p + 1)
                    nc.scalar.activation(act_quarter(act_hi, name, p), bank(4 + p).rearrange("p (k t) -> p k t", t=P),
                                         ACT.Copy).then_inc(act_hi_ready, 1)

            def attention(at, w_o):
                pairs = at.heads == 16
                for h in range(at.heads + 3):
                    g = h - 2
                    if 0 <= g < at.heads:
                        act.wait_ge(at.p_turned, g + 1)
                        nc.scalar.activation(probsT[:, g % 2, :], bank(6, 0, 3 * P), ACT.Copy)\
                            .then_inc(at.p_copied, 1)
                    g = h - 3
                    if 0 <= g < at.heads and (not pairs or g % 2):
                        act.wait_ge(at.mixed, g + 1)
                        k = g // 2 if pairs else g
                        nc.scalar.activation(act_hi[:, k, :], bank(7, 0, T), ACT.Copy).then_inc(at.o_hi, 1)
                    if h < at.heads:
                        act.wait_ge(at.maxed, h + 1)
                        for t in range(TT):
                            lo, hi = (0, P) if t == 0 else (P, 3 * P)
                            c = at.col + 2 * h + t
                            nc.scalar.activation(probs[:, h % 3, lo:hi], probs[:, h % 3, lo:hi], ACT.Exp,
                                                 bias=soft[:, 1, c:c + 1], scale=at.scale,
                                                 accum_out=soft[:, 2, c:c + 1])\
                                .then_inc(at.exped, 1)
                    if due(cursor[0], w_o, h, at.heads):
                        hi_next()

            def mlp_layer(f, layer):
                n0 = f.first

                def head(i, first):
                    act.wait_ge(w_used, n0 + 1 if first else i * 2 + n0)
                    if not first:
                        act.wait_ge(f.h_done, i)
                    nc.scalar.activation(relu, bank(4), ACT.Relu).then_inc(f.act_done, 1)

                def tail(i, first, last=False):
                    act.wait_ge(f.h_done, i + 1)
                    if not first and not last:
                        act.wait_ge(w_used, i * 2 + (n0 + 1))
                    nc.scalar.activation((last_hhi if last else hhi)[:, :, :].rearrange("p k t -> p (k t)"), hf, ACT.Copy)\
                        .then_inc(f.hi_done, 1)

                hi_before(n0)
                head(0, True)
                tail(0, True)
                extra = cursor[0] - (n0 + 3)
                with act.Fori(0, (NM - 2) // 2) as n:
                    for u in range(2):
                        i = n * 2 + 1 + u
                        head(i, False)
                        for m in (3 + 2 * u + extra, 4 + 2 * u + extra):
                            c = n0 + m
                            hi_part(SLOT[c], W, n * 16 + 16 * NTH[c], n * 4 + (c - 3))
                        tail(i, False)
                cursor[0] = n0 + 31 + extra
                head(NM - 1, False)
                hi_before(n0 + 2 * (NM - 1))
                tail(NM - 1, False, True)

            def ffn_layer(f):
                n0 = f.first

                def head(i, first):
                    act.wait_ge(f.scaled, i + 1)
                    if not first:
                        act.wait_ge(f.h_done, i)
                    nc.scalar.activation(relu, gate, ACT.Silu).then_inc(f.act_done, 1)

                def tail(i, first, last=False):
                    act.wait_ge(f.h_done, i + 1)
                    if not first and not last:
                        act.wait_ge(w_used, i * 3 + (n0 + 2))
                    nc.scalar.activation((last_hhi if last else hhi)[:, :, :].rearrange("p k t -> p (k t)"), hf, ACT.Copy)\
                        .then_inc(f.hi_done, 1)

                def part(c, n):
                    hi_part(SLOT[c], W, n * 16 + 16 * (NTH[c] - 1), n * 3 + (c - 2 - 3))

                hi_before(n0 + 1)
                assert cursor[0] == n0 + 4, (cursor[0], n0)
                head(0, True)
                tail(0, True)
                with act.Fori(1, NF - 1) as i:
                    part(n0 + 4, i)
                    head(i, False)
                    part(n0 + 5, i)
                    part(n0 + 6, i)
                    tail(i, False)
                cursor[0] = n0 + 31
                hi_before(n0 + 3 * (NF - 1))
                head(NF - 1, False)
                hi_before(n0 + 3 * (NF - 1) + 1)
                tail(NF - 1, False, True)

            hi_next()
            copy_turned("mix0")
            hi_before(0)
            stats("mix0")
            act.wait_ge(angle_ready, 1)
            nc.scalar.activation(sin[:, :, :], red[:, :, :], ACT.Sin).then_inc(trig_ready, 1)
            act.wait_ge(angle_ready, 2)
            nc.scalar.activation(cos[:, :, :], red2[:, :, :], ACT.Sin).then_inc(trig_ready, 1)
            act.wait_ge(scale_ready, 2)
            for n in range(6):
                hi_before(2 * n + 1)
                act.wait_ge(w_used, 2 * n + 2)
                dst = qk_tok[:, 0, n * HALF:(n + 1) * HALF] if n < 4 else V[:, 0, (n - 4) * HALF:(n - 3) * HALF]
                nc.scalar.activation(dst, bank(2 * (n % 2)), ACT.Copy, scale=norm_stat("mix0", 0, 6))\
                    .then_inc(qkv_a, 1)
                if n >= 3:
                    copy_heads(act, n - 3)
            copy_heads(act, 3)
            attention(moba, AT["wo"])
            hi_before(AT["wo"] + 2)
            copy_turned("mlp0")
            stats("mlp0")
            mlp_layer(mlp[0], 0)
            hi_before(mlp[0].first + 31)
            stats("mix1")
            for b in range(4):
                act.wait_ge(pooled, b + 1)
                nc.scalar.activation(act_hi[:, 2 * b:2 * b + 2, :].rearrange("p k t -> p (k t)"), bank(4 + b),
                                     ACT.Copy).then_inc(act_hi_ready, 1)
            hi_before(AT["pool"])
            copy_turned("mlp1")
            stats("mlp1")
            mlp_layer(mlp[1], 1)
            hi_before(mlp[1].first + 31)
            stats("final")
            copy_turned("pre0")
            stats("pre0")
            hi_before(AT["wa"])
            act.wait_ge(scale_ready, 4)
            act.wait_ge(acc_wa, 1)
            nc.scalar.activation(lora[:, 0, :], ps[:, HALF - 352:HALF + 352], ACT.Copy, scale=norm_stat("pre0", 0, 6)).then_inc(lora_a, 1)
            for t in range(TT):
                act.wait_ge(*((lora_v, 1) if t else (lora_a, 1)))
                sum_squares("lora", t, lora[:, t, 0:QL], QL, 0)
                sum_squares("lora", t, lora[:, t, QL:QL + KVL], KVL, 1)
                root("lora", t, 2)
                if t == 0:
                    hi_before(AT["wa"] + 2)
            for t in range(TT):
                act.wait_ge(turned, 4 * TURN["lora"] + t + 1)
                nc.scalar.activation(act_hi[:, 0:4, t * P:(t + 1) * P],
                                     bank(4 + t).rearrange("p (k t) -> p k t", t=P), ACT.Copy)\
                    .then_inc(act_hi_ready, 1)
            for t in range(TT):
                act.wait_ge(turned, 4 * TURN["lora"] + t + 3)
                nc.scalar.activation(act_hi[:, 4, t * P:(t + 1) * P], bank(6 + t, 0, P), ACT.Copy)\
                    .then_inc(act_hi_ready, 1)
                nc.scalar.activation(krT[:, t * P:(t + 1) * P], bank(6 + t, P, 2 * P), ACT.Copy)\
                    .then_inc(kr_copied, 1)
            for j in range(2):
                c = AT["uq"] + j
                hi_before(c)
                act.wait_ge(w_used, c + 1)
                for b in range(2):
                    h = 4 * j + 2 * b
                    nc.scalar.activation(qT[:, h:h + 2, :].rearrange("p h t -> p (h t)"), bank((0, 6)[j] + b),
                                         ACT.Copy).then_inc(qn_copied, 1)
            copy_qr(act, 0)
            copy_qr(act, 1)
            for j in range(2):
                c = AT["ukv"] + j
                hi_before(c)
                act.wait_ge(w_used, c + 1)
                for b in range(2):
                    nc.scalar.activation(kT[:, 4 * j + 2 * b:4 * j + 2 * b + 2, :].rearrange("p h t -> p (h t)"),
                                         bank(b), ACT.Copy).then_inc(kn_copied, 1)
            attention(mla, AT["mwo"])
            hi_before(AT["mwo"] + 2)
            post_stats(act, sum_squares, root, "post0", AT["mwo"] + 4, ACC["mwo"])
            copy_turned("fpre0")
            stats("fpre0")
            ffn_layer(ffn[0])
            hi_before(ffn[0].first + 32)
            post_stats(act, sum_squares, root, "fpost0", ffn[0].first + 33, ACC["ffn0"])
            copy_turned("kvsrc")
            stats("kvsrc")
            act.wait_ge(diagonal_ready, 2 * SPREAD["kvsrc"] + 2)
            for n in range(2):
                c = AT["kvv"] + 2 * n
                hi_before(c + 1)
                act.wait_ge(w_used, c + 2)
                nc.scalar.activation(V2[:, 0, n * HALF:(n + 1) * HALF], bank(2 * n), ACT.Copy,
                                     scale=norm_stat("kvsrc", 0, 6)).then_inc(vs_copied, 1)
            copy_turned("pre1")
            hi_before(AT["bq"] + 3)
            attention(chk, AT["bwo"])
            hi_before(AT["bwo"] + 2)
            post_stats(act, sum_squares, root, "post1", AT["bwo"] + 4, ACC["bwo"])
            copy_turned("fpre1")
            stats("fpre1")
            ffn_layer(ffn[1])
            post_stats(act, sum_squares, root, "fpost1", ffn[1].first + 33, ACC["ffn1"])

        @block.vector
        def _(dve):
            cursor = [0]
            links = [0]

            def link(ins):
                links[0] += 1
                ins.then_inc(chain, 1)
                dve.wait_ge(chain, links[0])

            def lo_part(s, width, value):
                dve.wait_ge(hi_ready, value)
                w = cut(width)
                nc.vector.tensor_tensor(wlo[:, s, 0:w], raw[:, s, 0:w], whi[:, s, 0:w].bitcast(F32),
                                        ALU.subtract).then_inc(lo_ready_v, 1)

            def lo_before(c):
                while cursor[0] < NCH and PREV[cursor[0]] < c:
                    lo_next()

            def lo_next():
                q = cursor[0]
                lo_part(SLOT[q], CHUNKS[q][2], q + 1)
                cursor[0] += 1

            def mean_square(name, t, widths=(D,), before=None):
                dve.wait_ge(squares, squares_after(name, 1 if t is BOTH else t))
                for i, w in enumerate(widths):
                    ins = nc.vector.tensor_scalar(norm_stat(name, t, 1, i, i + 1), norm_stat(name, t, 0, i, i + 1),
                                                  norm_stat(before, t, 4) if before else 1.0 / w, EPS,
                                                  ALU.mult, ALU.add)
                ins.then_inc(var_ready, 2 if t is BOTH else 1)

            def inverse_root(name, t, widths=(D,), mean=True, before=None):
                n = len(widths)

                def st(k, lo=0, hi=n):
                    return norm_stat(name, t, k, lo, hi)

                if mean:
                    mean_square(name, t, widths)
                dve.wait_ge(root_ready, 2 * NORM[name] + (2 if t is BOTH else t + 1))
                link(nc.vector.reciprocal(st(3), st(2)))
                link(nc.vector.tensor_tensor(st(4), st(3), st(3), ALU.mult))
                link(nc.vector.tensor_tensor(st(5), st(4), st(1), ALU.mult))
                link(nc.vector.tensor_scalar(st(5), st(5), -0.5, 1.5, ALU.mult, ALU.add))
                if before:
                    link(nc.vector.scalar_tensor_tensor(out=st(6), in0=st(5), scalar=norm_stat(before, t, 6),
                                                        in1=st(3), op0=ALU.mult, op1=ALU.mult))
                else:
                    link(nc.vector.tensor_tensor(st(6), st(5), st(3), ALU.mult))

            def scaled(dst, src, name, t, gain, col=0):
                return nc.vector.scalar_tensor_tensor(out=dst, in0=src, scalar=norm_stat(name, t, 6, col, col + 1),
                                                      in1=gain, op0=ALU.mult, op1=ALU.mult)

            def norm(name):
                inverse_root(name, BOTH)
                wait_row(dve, name)
                for p in range(4):
                    h, t, cols = quarter(name, p)
                    scaled(xs[:, t, cols], x[:, t, cols], name, t, row(name)[:, cols]).then_inc(xs_ready, 1)
                dve.wait_ge(xs_ready, 4 * XSR[name] + 4)
                release_row()

            def diagonals(name):
                inverse_root(name, BOTH)
                link(nc.vector.tensor_tensor(norm_stat(name, BOTH, 4), norm_stat(name, BOTH, 6),
                                             norm_stat(name, BOTH, 6), ALU.mult))
                nc.vector.tensor_scalar(norm_stat(name, BOTH, 4), norm_stat(name, BOTH, 4), 1.0 / D, None, ALU.mult)
                for t in range(TT):
                    nc.vector.tensor_scalar(probs[:, t, 0:P], ident, norm_stat(name, t, 6), None, ALU.mult)\
                        .then_inc(diagonal_ready, 1)

            def copy_scales(name):
                dve.wait_ge(scale_row_made, SPREAD[name] + 1)
                link(nc.vector.tensor_copy(scale_row[:, :], bank(7, 0, T)))

            def late_roots(name, square=False):
                inverse_root(name, BOTH)
                if square:
                    link(nc.vector.tensor_tensor(norm_stat(name, BOTH, 4), norm_stat(name, BOTH, 6),
                                                 norm_stat(name, BOTH, 6), ALU.mult))
                else:
                    dve.sem_inc(scale_ready, 2)

            def gained(name, p):
                h, t, cols = quarter(name, p)
                if p == 0:
                    wait_row(dve, name)
                dve.wait_ge(x_ready, 4 * XR[name] + p + 1 if name in BY_QUARTERS + BY_TILES else x_done(name, t))
                nc.vector.tensor_tensor(xs[:, t, cols], x[:, t, cols], row(name)[:, cols], ALU.mult)\
                    .then_inc(xs_ready, 1)
                if p == 3:
                    dve.wait_ge(xs_ready, 4 * XSR[name] + 4)
                    release_row()

            def release_row():
                dve.sem_inc(row_used, 1)

            def split_turned(name):
                for p in range(4):
                    dve.wait_ge(act_hi_ready, 4 * ACTN[name] + p + 1)
                    nc.vector.tensor_tensor(act_quarter(act_lo, name, p), bank(4 + p).rearrange("p (k t) -> p k t", t=P),
                                            act_quarter(act_hi, name, p).bitcast(F32), ALU.subtract)\
                        .then_inc(act_lo_ready, 1)

            def residual(done, acc, scales=None, then=None):
                for p in range(4):
                    h, t, cols = quarter(then, p)
                    dve.wait_ge(*((acc_part, 3 * acc + p + 1) if p < 3 else (w_used, done)))
                    part = bank(2 * t + h)
                    if scales:
                        ins = nc.vector.scalar_tensor_tensor(out=x[:, t, cols], in0=part,
                                                             scalar=norm_stat(scales, t, 4),
                                                             in1=x[:, t, cols], op0=ALU.mult, op1=ALU.add)
                    else:
                        ins = nc.vector.tensor_tensor(x[:, t, cols], x[:, t, cols], part, ALU.add)
                    ins.then_inc(x_ready, 1)
                    if then:
                        gained(then, p)

            def post(name, before=None, then=None):
                wait_row(dve, name)
                for t in range(TT):
                    mean_square(name, t, before=before)
                    nc.vector.tensor_tensor(xs[:, t, :], ps[:, t * D:(t + 1) * D], row(name), ALU.mult)
                    inverse_root(name, t, mean=False, before=before)
                    for h in range(2):
                        cols = slice(h * HALF, (h + 1) * HALF)
                        nc.vector.scalar_tensor_tensor(out=x[:, t, cols], in0=xs[:, t, cols],
                                                       scalar=norm_stat(name, t, 6), in1=x[:, t, cols],
                                                       op0=ALU.mult, op1=ALU.add).then_inc(x_ready, 1)
                        if then:
                            gained(then, 2 * t + h)
                release_row()

            def rope(src, dst, c, s, n, tmp):
                x1, x2 = src
                y1, y2 = dst
                nc.vector.tensor_tensor(tmp[0], x1, c, ALU.mult)
                nc.vector.tensor_tensor(tmp[1], x2, s, ALU.mult)
                nc.vector.tensor_tensor(tmp[2], x2, c, ALU.mult)
                link(nc.vector.tensor_tensor(tmp[3], x1, s, ALU.mult))
                nc.vector.tensor_tensor(y1, tmp[0], tmp[1], ALU.subtract)
                return nc.vector.tensor_tensor(y2, tmp[2], tmp[3], ALU.add)

            def attention(at, masks, w_o):
                pairs = at.heads == 16
                for h in range(at.heads + 4):
                    if h < at.heads:
                        mask = masks(h)
                        dve.wait_ge(at.scored, h + 1)
                        c = at.col + 2 * h
                        for t in range(TT):
                            lo, hi = (0, P) if t == 0 else (P, 3 * P)
                            ins = nc.vector.tensor_tensor_reduce(
                                probs[:, h % 3, lo:hi], bank(4 + h % 2, lo, hi), mask[t],
                                1.0, MIN32, ALU.add, ALU.max, soft[:, 0, c + t:c + t + 1])
                        link(ins)
                        nc.vector.tensor_scalar(soft[:, 1, c:c + 2], soft[:, 0, c:c + 2], -at.scale, None,
                                                ALU.mult).then_inc(at.maxed, 1)
                    g = h - 1
                    if 0 <= g < at.heads:
                        dve.wait_ge(at.exped, 2 * g + 2)
                        c = at.col + 2 * g
                        link(nc.vector.reciprocal(soft[:, 3, c:c + 2], soft[:, 2, c:c + 2]))
                        for t in range(TT):
                            lo, hi = (0, P) if t == 0 else (P, 3 * P)
                            ins = nc.vector.tensor_scalar(probs[:, g % 3, lo:hi], probs[:, g % 3, lo:hi],
                                                          soft[:, 3, c + t:c + t + 1], None, ALU.mult)
                        ins.then_inc(at.normed, 1)
                    g = h - 3
                    if 0 <= g < at.heads and (not pairs or g % 2):
                        k = g // 2 if pairs else g
                        dve.wait_ge(at.o_hi, k + 1)
                        nc.vector.tensor_tensor(act_lo[:, k, :], bank(7, 0, T), act_hi[:, k, :].bitcast(F32),
                                                ALU.subtract).then_inc(at.o_lo, 1)
                    if h and due(cursor[0], w_o, h - 1, at.heads):
                        lo_next()

            def hidden_lo(f, i, last=False):
                hi, lo = (last_hhi, last_hlo) if last else (hhi, hlo)
                dve.wait_ge(f.hi_done, i + 1)
                nc.vector.tensor_tensor(lo[:, :, :].rearrange("p k t -> p (k t)"), hf,
                                        hi[:, :, :].rearrange("p k t -> p (k t)").bitcast(F32),
                                        ALU.subtract).then_inc(f.lo_done, 1)

            def mlp_layer(f):
                n0 = f.first

                def square(i, first=False):
                    dve.wait_ge(f.act_done, i + 1)
                    if not first:
                        dve.wait_ge(f.lo_done, i)
                    nc.vector.tensor_tensor(hf, relu, relu, ALU.mult).then_inc(f.h_done, 1)

                lo_before(n0)
                extra = cursor[0] - (n0 + 3)
                square(0, True)
                hidden_lo(f, 0)
                with dve.Fori(0, (NM - 2) // 2) as n:
                    for u in range(2):
                        i = n * 2 + 1 + u
                        square(i)
                        for m in (3 + 2 * u + extra, 4 + 2 * u + extra):
                            lo_part(SLOT[n0 + m], W, n * 4 + (n0 + m + 1))
                        hidden_lo(f, i)
                cursor[0] = n0 + 31 + extra
                square(NM - 1)
                lo_before(n0 + 2 * (NM - 1))
                hidden_lo(f, NM - 1, True)

            def ffn_layer(f, name):
                n0 = f.first

                def scale_gate(i, value, first=False):
                    dve.wait_ge(w_used, value)
                    if not first:
                        dve.wait_ge(f.act_done, i)
                    nc.vector.tensor_tensor(by_token(gate), by_token(bank(4)), scales_2, ALU.mult)\
                        .then_inc(f.scaled, 1)

                def gated(i, value, first=False):
                    dve.wait_ge(f.act_done, i + 1)
                    dve.wait_ge(w_used, value)
                    if not first:
                        dve.wait_ge(f.lo_done, i)
                    nc.vector.tensor_tensor(hf, relu, bank(5), ALU.mult).then_inc(f.h_done, 1)

                lo_before(n0)
                copy_scales(name)
                scale_gate(0, n0 + 1, True)
                lo_before(n0 + 1)
                gated(0, n0 + 2, True)
                hidden_lo(f, 0)
                with dve.Fori(1, NF - 1) as i:
                    lo_part(SLOT[n0 + 4], W, i * 3 + (n0 + 2))
                    scale_gate(i, i * 3 + n0)
                    lo_part(SLOT[n0 + 5], W, i * 3 + (n0 + 3))
                    gated(i, i * 3 + (n0 + 1))
                    lo_part(SLOT[n0 + 6], W, i * 3 + (n0 + 4))
                    hidden_lo(f, i)
                cursor[0] = n0 + 31
                lo_before(n0 + 3 * (NF - 1))
                scale_gate(NF - 1, n0 + 3 * (NF - 1))
                gated(NF - 1, n0 + 3 * (NF - 1) + 1)
                lo_before(n0 + 3 * (NF - 1) + 1)
                hidden_lo(f, NF - 1, True)

            dve.wait_ge(x_loaded, 16)
            dve.sem_inc(x_ready, 4)
            for p in range(4):
                gained("mix0", p)
            lo_next()
            split_turned("mix0")
            lo_before(0)
            late_roots("mix0")
            dve.wait_ge(pos_loaded, 32)
            link(nc.vector.tensor_copy(pos_f[:, :, :], pos_i[:, :, :]))
            dve.wait_ge(const_loaded, 16)
            for t in range(TT):
                nc.vector.tensor_scalar(ang[:, t, 0:ROT1], inv[:, 0:ROT1], pos_f[:, 0, t:t + 1], None, ALU.mult)
                ins = nc.vector.tensor_scalar(ang[:, t, ROT1:NA], inv[:, ROT1:NA], pos_f[:, 1, t:t + 1], None,
                                              ALU.mult)
            link(ins)
            link(nc.vector.tensor_scalar(turns[:, :, :], ang[:, :, :], INV_2PI, MAGIC, ALU.mult, ALU.add))
            link(nc.vector.tensor_scalar(turns[:, :, :], turns[:, :, :], -MAGIC, None, ALU.add))
            src = ang
            for n, part in enumerate((PI_A, PI_B, PI_C)):
                dst = red2 if n % 2 else red
                link(nc.vector.scalar_tensor_tensor(out=dst[:, :, :], in0=turns[:, :, :], scalar=-part,
                                                    in1=src[:, :, :], op0=ALU.mult, op1=ALU.add))
                src = dst
            link(nc.vector.tensor_scalar(red[:, :, :], red[:, :, :], PI_SAFE, -PI_SAFE, ALU.min, ALU.max))
            dve.sem_inc(angle_ready, 1)
            link(nc.vector.scalar_tensor_tensor(out=red2[:, :, :], in0=red[:, :, :], scalar=-1.0,
                                                in1=red[:, :, :], op0=ALU.mult, op1=ALU.max))
            nc.vector.tensor_scalar(red2[:, :, :], red2[:, :, :], -1.0, HALF_PI, ALU.mult, ALU.add)\
                .then_inc(angle_ready, 1)

            def trig(table, lo, hi, heads):
                return table[:, :, lo:hi].unsqueeze(2).broadcast_to([P, TT, heads, hi - lo])

            dve.wait_ge(trig_ready, 2)
            for n in range(6):
                lo_before(2 * n + 1)
                dve.wait_ge(w_used, 2 * n + 2)
                dst = qk_tok[:, 1, n * HALF:(n + 1) * HALF] if n < 4 else V[:, 1, (n - 4) * HALF:(n - 3) * HALF]
                nc.vector.tensor_scalar(dst, bank(2 * (n % 2) + 1), norm_stat("mix0", 1, 6), None, ALU.mult)\
                    .then_inc(qkv_v, 1)
                if n < 4:
                    dve.wait_ge(qkv_v, n + 1)
                    dve.wait_ge(qkv_a, n + 1)
                    v4 = qk_tok[:, :, n * HALF:(n + 1) * HALF].rearrange("p t (h d) -> p t h d", d=HD1)
                    halves = (v4[:, :, :, 0:ROT1], v4[:, :, :, ROT1:2 * ROT1])
                    tmp = [rope_tmp[:, q, 0:TT * 4 * ROT1].rearrange("p (t h d) -> p t h d", t=TT, d=ROT1)
                           for q in range(4)]
                    rope(halves, halves, trig(cos, 0, ROT1, 4), trig(sin, 0, ROT1, 4), ROT1, tmp)\
                        .then_inc(roped, 1)
            dve.wait_ge(masks_loaded, 16)
            attention(moba, lambda h: (causal[:, P:T], causal), AT["wo"])
            lo_before(AT["wo"] + 2)
            residual(AT["wo"] + 4, ACC["wo"], then="mlp0")
            split_turned("mlp0")
            late_roots("mlp0", square=True)
            mlp_layer(mlp[0])
            lo_before(mlp[0].first + 31)
            residual(mlp[0].first + 32, ACC["mlp0"], "mlp0")
            norm("mix1")
            for b in range(4):
                dve.wait_ge(act_hi_ready, 4 * ACTN["mix1"] + b + 1)
                nc.vector.tensor_tensor(act_lo[:, 2 * b:2 * b + 2, :].rearrange("p k t -> p (k t)"), bank(4 + b),
                                        act_hi[:, 2 * b:2 * b + 2, :].rearrange("p k t -> p (k t)").bitcast(F32),
                                        ALU.subtract).then_inc(act_lo_ready, 1)
            lo_before(AT["pool"])
            wait_row(dve, "pool_scale")
            for p in range(4):
                h, t, cols = quarter("mlp1", p)
                dve.wait_ge(*((pool_part, p + 1) if p < 3 else (w_used, AT["pool"] + 1)))
                link(nc.vector.tensor_tensor(xs[:, t, cols], bank(2 * t + h), row("pool_scale")[:, cols], ALU.mult))
                nc.vector.tensor_tensor(x[:, t, cols], x[:, t, cols], xs[:, t, cols], ALU.add).then_inc(x_ready, 1)
                gained("mlp1", p)
            release_row()
            split_turned("mlp1")
            late_roots("mlp1", square=True)
            mlp_layer(mlp[1])
            lo_before(mlp[1].first + 31)
            residual(mlp[1].first + 32, ACC["mlp1"], "mlp1")
            wait_row(dve, "final")
            inverse_root("final", BOTH)
            for p in range(4):
                h, t, cols = quarter("pre0", p)
                scaled(x[:, t, cols], x[:, t, cols], "final", t, row("final")[:, cols]).then_inc(x_ready, 1)
                gained("pre0", p)
            release_row()
            split_turned("pre0")
            late_roots("pre0")
            lo_before(AT["wa"])
            wait_row(dve, "lora")
            for t in range(TT):
                if t == 1:
                    lo_before(AT["wa"] + 2)
                    dve.wait_ge(w_used, AT["wa"] + 4)
                    nc.vector.tensor_scalar(lora[:, 1, :], ps[:, D + HALF - 352:D + HALF + 352],
                                            norm_stat("pre0", 1, 6), None, ALU.mult).then_inc(lora_v, 1)
                dve.wait_ge(*((lora_v, 1) if t else (lora_a, 1)))
                inverse_root("lora", t, (QL, KVL))
                scaled(xs[:, t, 0:QL], lora[:, t, 0:QL], "lora", t, row("lora", 0, QL), 0)
                link(scaled(xs[:, t, QL:QL + KVL], lora[:, t, QL:QL + KVL], "lora", t, row("lora", QL, QL + KVL), 1))
                if t == 1:
                    dve.sem_inc(xs_ready, 1)
                k0 = QL + KVL
                tmp = [junk[:, D - (q + 1) * ROT2:D - q * ROT2] for q in range(4)]
                link(rope((lora[:, t, k0:k0 + ROT2], lora[:, t, k0 + ROT2:k0 + 2 * ROT2]),
                          (xs[:, t, k0:k0 + ROT2], xs[:, t, k0 + ROT2:k0 + 2 * ROT2]),
                          cos[:, t, ROT1:NA], sin[:, t, ROT1:NA], ROT2, tmp))
                nc.vector.tensor_copy(xs[:, t, k0 + 64:k0 + 128], xs[:, t, k0:k0 + 64])\
                    .then_inc(xs_ready, 1 if t == 0 else 2)
            release_row()
            for p in range(4):
                h, t, _ = quarter("lora", p)
                k0, k1 = (4, 5) if h else (0, 4)
                dve.wait_ge(act_hi_ready, 4 * ACTN["lora"] + p + 1)
                if h:
                    dve.wait_ge(kr_copied, t + 1)
                nc.vector.tensor_tensor(
                    act_lo[:, k0:k1, t * P:(t + 1) * P],
                    bank(4 + p, 0, (k1 - k0) * P).rearrange("p (k t) -> p k t", t=P),
                    act_hi[:, k0:k1, t * P:(t + 1) * P].bitcast(F32), ALU.subtract)\
                    .then_inc(act_lo_ready, 1)
            lo_before(AT["uqr"])
            dve.wait_ge(w_used, AT["uqr"] + 1)
            for t in range(TT):
                link(nc.vector.tensor_copy(qr_tok[:, t, :], bank(2 + t)))
            dve.sem_inc(qr_copied, 1)
            lo_before(AT["uq"])
            for t in range(TT):
                v4 = qr_tok[:, t, :].rearrange("p (h d) -> p h d", d=64)
                halves = (v4[:, :, 0:ROT2], v4[:, :, ROT2:64])
                tmp = [rope_tmp[:, q, :].rearrange("p (h d) -> p h d", d=ROT2) for q in range(4)]
                link(rope(halves, halves, cos[:, t, ROT1:NA].unsqueeze(1).broadcast_to([P, 8, ROT2]),
                          sin[:, t, ROT1:NA].unsqueeze(1).broadcast_to([P, 8, ROT2]), ROT2, tmp))
            dve.sem_inc(qr_roped, 1)
            lo_before(AT["uq"] + 1)
            for j in range(2):
                c = AT["ukv"] + j
                lo_before(c)
                dve.wait_ge(w_used, c + 1)
                for t in range(TT):
                    nc.vector.tensor_copy(V[:, t, j * HALF:(j + 1) * HALF], bank(2 + t)).then_inc(v_copied, 1)
            attention(mla, lambda h: (chunked[:, P:T], chunked), AT["mwo"])
            lo_before(AT["mwo"] + 2)
            post("post0", None, "fpre0")
            split_turned("fpre0")
            diagonals("fpre0")
            ffn_layer(ffn[0], "fpre0")
            lo_before(ffn[0].first + 32)
            post("fpost0", "fpre0", "kvsrc")
            split_turned("kvsrc")
            diagonals("kvsrc")
            dve.wait_ge(turned, 4 * TURN["kvsrc"] + 4)
            for p in range(4):
                gained("pre1", p)
            copy_scales("kvsrc")
            for j in range(4):
                lo_before(AT["kvk"] + j)
                dve.wait_ge(w_used, AT["kvk"] + j + 1)
                nc.vector.tensor_tensor(kT[:, 2 * j:2 * j + 2, :], by_token(bank(4 + j % 2)), scales_2, ALU.mult)\
                    .then_inc(kT_copied, 1)
            for n in range(2):
                c = AT["kvv"] + 2 * n
                lo_before(c + 1)
                dve.wait_ge(w_used, c + 2)
                nc.vector.tensor_scalar(V2[:, 1, n * HALF:(n + 1) * HALF], bank(2 * n + 1),
                                        norm_stat("kvsrc", 1, 6), None, ALU.mult).then_inc(v_copied, 1)
            split_turned("pre1")
            for j in range(4):
                lo_before(AT["bq"] + j)
                dve.wait_ge(w_used, AT["bq"] + j + 1)
                nc.vector.tensor_tensor(qT[:, 2 * j:2 * j + 2, :], by_token(bank(4 + j % 2)), scales_2, ALU.mult)\
                    .then_inc(qT_copied, 1)

            def biases(h):
                dve.wait_ge(bias_ready, h + 1)
                return (bias[:, h % 8, P - 1::-1], bias[:, h % 8, ::-1])

            attention(chk, biases, AT["bwo"])
            lo_before(AT["bwo"] + 2)
            post("post1", None, "fpre1")
            split_turned("fpre1")
            diagonals("fpre1")
            ffn_layer(ffn[1], "fpre1")
            post("fpost1", "fpre1")

        @block.tensor
        def _(pe):
            def wait_chunk(value):
                pe.wait_ge(lo_ready_v, value)
                pe.wait_ge(lo_ready_g, value)

            def product(dst, left, right, start, stop, **kw):
                nc.tensor.matmul(dst, lhsT=left[0], rhs=right[0], start=start, stop=False, **kw)
                nc.tensor.matmul(dst, lhsT=left[0], rhs=right[1], start=False, stop=False, **kw)
                return nc.tensor.matmul(dst, lhsT=left[1], rhs=right[0], start=False, stop=stop, **kw)

            def slot(c):
                s = SLOT[c]
                return (whi[:, s, :], wlo[:, s, :])

            def cols(w, lo, hi):
                return (w[0][:, lo:hi], w[1][:, lo:hi])

            def acts(k, lo=0, hi=T):
                return (act_hi[:, k, lo:hi], act_lo[:, k, lo:hi])

            def turn(name, blocks=((0, 4), (4, 8))):
                if name == "mix0":
                    pe.wait_ge(const_loaded, 16)
                for p in range(4):
                    h, t, _ = quarter(name, p)
                    pe.wait_ge(xs_ready, 4 * XSR[name] + p + 1)
                    k0, k1 = blocks[h]
                    for k in range(k0, k1):
                        ins = nc.tensor.transpose(bank(4 + p, (k - k0) * P, (k - k0 + 1) * P),
                                                  xs[:, t, k * P:(k + 1) * P], ident)
                    ins.then_inc(turned, 1)

            def wait_acts(name, count=4):
                pe.wait_ge(act_lo_ready, 4 * ACTN[name] + count)

            QUARTERS = [(h, t) for h in range(2) for t in range(TT)]
            TILES = [(h, t) for t in range(TT) for h in range(2)]

            def rows_out(w, k0, left, first, last, final=None):
                for n, (half, t) in enumerate(final or TILES):
                    for k in range(2):
                        ins = product(bank(2 * t + half), left(k0 + k, t),
                                      cols(w, k * D + half * HALF, k * D + (half + 1) * HALF),
                                      start=first and k == 0, stop=last and k == 1,
                                      skip_group_check=True)
                    if final and n < 3:
                        ins.then_inc(acc_part, 1)
                return ins

            def tiles_out(w, b, enter=None):
                for f in range(2):
                    for k in range(KT):
                        if enter and f == 0 and k % 4 == 0:
                            wait_acts(enter, 3 + k // 4 if enter in BY_TILES else 2 + 2 * (k // 4))
                        ins = product(bank(b, f * T, (f + 1) * T),
                                      cols(w, k * FC + f * P, k * FC + (f + 1) * P), acts(k),
                                      start=k == 0, stop=k == KT - 1)
                return ins

            def spread_scales(name):
                pe.wait_ge(masks_loaded, 16)
                pe.wait_ge(diagonal_ready, 2 * SPREAD[name] + 2)
                for t in range(TT):
                    ins = nc.tensor.matmul(bank(7, t * P, (t + 1) * P), lhsT=const[:, C_ONES:C_ONES + P],
                                           rhs=probs[:, t, 0:P], start=True, stop=True)
                ins.then_inc(scale_row_made, 1)

            def head_out(first, k, final, tiles=range(TT)):
                c = first + k // 2
                if k % 2 == 0 and tiles[0] == 0:
                    wait_chunk(c + 1)
                if k == KT - 2:
                    rows_out(slot(c), k, lambda k, t: acts(k, t * P, (t + 1) * P), False, True, final)\
                        .then_inc(w_used, 1)
                elif k < KT - 2:
                    at = (k % 2) * D
                    for t in tiles:
                        for half in range(2):
                            ins = product(bank(2 * t + half), acts(k, t * P, (t + 1) * P),
                                          cols(slot(c), at + half * HALF, at + (half + 1) * HALF),
                                          start=k == 0, stop=False, skip_group_check=True)
                    if k % 2 and tiles[-1] == TT - 1:
                        ins.then_inc(w_used, 1)

            def attention(at, score, value, w_o, final):
                pairs = at.heads == 16
                for h in range(at.heads + 3):
                    if h == 2 and at is moba:
                        qkv_done()
                    if h < at.heads:
                        if h >= 2:
                            pe.wait_ge(at.maxed, h - 1)
                        for t in range(TT):
                            lo, hi = (0, P) if t == 0 else (P, 3 * P)
                            ins = score(h, t, bank(4 + h % 2, lo, hi))
                        ins.then_inc(at.scored, 1)
                    g = h - 2
                    if 0 <= g < at.heads:
                        pe.wait_ge(at.normed, g + 1)
                        if g >= 1:
                            pe.wait_ge(at.p_copied, g)
                        for b in range(3):
                            ins = nc.tensor.transpose(bank(6, b * P, (b + 1) * P),
                                                      probs[:, g % 3, b * P:(b + 1) * P], ident)
                        ins.then_inc(at.p_turned, 1)
                    g = h - 3
                    if 0 <= g < at.heads:
                        pe.wait_ge(at.p_copied, g + 1)
                        if pairs:
                            if g >= 2:
                                pe.wait_ge(at.o_lo, g // 2)
                            lo = 64 * (g % 2)
                            o = ps[lo:lo + 64, 7 * HALF:7 * HALF + T]
                        else:
                            if g >= 1:
                                pe.wait_ge(at.o_lo, g)
                            o = bank(7, 0, T)
                        nc.tensor.matmul(o, lhsT=value(g, 0), rhs=probsT[:, g % 2, 0:T], start=True, stop=False)
                        nc.tensor.matmul(o[:, P:T], lhsT=value(g, 1), rhs=probsT[:, g % 2, T:3 * P],
                                         start=False, stop=True).then_inc(at.mixed, 1)
                    k = (h - 5) // 2 if pairs else h - 4
                    if 0 <= k < KT - 2:
                        pe.wait_ge(at.o_lo, k + 1)
                        if pairs:
                            head_out(w_o, k, final, ((h - 5) % 2,))
                        else:
                            head_out(w_o, k, final)
                pe.wait_ge(at.o_lo, KT)
                head_out(w_o, KT - 2, final)

            def mlp_layer(f, norm):
                n0 = f.first

                def up(c, i, value, first=False):
                    wait_chunk(value)
                    if not first:
                        pe.wait_ge(f.act_done, i)
                    tiles_out(slot(c), 4, norm if first else None).then_inc(w_used, 1)

                def down(c, i, value, first=False, last=False):
                    wait_chunk(value)
                    pe.wait_ge(f.lo_done, i + 1)
                    hi, lo = (last_hhi, last_hlo) if last else (hhi, hlo)
                    rows_out(slot(c), 0, lambda k, t: (hi[:, k, t * P:(t + 1) * P], lo[:, k, t * P:(t + 1) * P]),
                             first, last, QUARTERS if last else None).then_inc(w_used, 1)

                up(n0, 0, n0 + 1, True)
                up(n0 + 1, 1, n0 + 2)
                down(n0 + 2, 0, n0 + 3, first=True)
                with pe.Fori(0, (NM - 2) // 2) as n:
                    for u in range(2):
                        c = n0 + 3 + 2 * u
                        up(c, n * 2 + 2 + u, n * 4 + (c + 1))
                        down(c + 1, n * 2 + 1 + u, n * 4 + (c + 2))
                down(n0 + 31, NM - 1, n0 + 32, last=True)

            def ffn_layer(f, norm):
                n0 = f.first

                def gate_up(c, i, value, first=False):
                    wait_chunk(value)
                    if not first:
                        pe.wait_ge(f.scaled, i)
                    tiles_out(slot(c), 4, norm if first else None).then_inc(w_used, 1)
                    if first:
                        spread_scales(norm)
                    wait_chunk(value + 1)
                    if not first:
                        pe.wait_ge(f.h_done, i)
                    tiles_out(slot(c + 1), 5).then_inc(w_used, 1)

                def down(c, i, value, first=False, last=False):
                    wait_chunk(value)
                    pe.wait_ge(f.lo_done, i + 1)
                    hi, lo = (last_hhi, last_hlo) if last else (hhi, hlo)
                    rows_out(slot(c), 0, lambda k, t: (hi[:, k, t * P:(t + 1) * P], lo[:, k, t * P:(t + 1) * P]),
                             first, last, TILES if last else None).then_inc(w_used, 1)

                gate_up(n0, 0, n0 + 1, True)
                gate_up(n0 + 2, 1, n0 + 3)
                down(n0 + 4, 0, n0 + 5, first=True)
                with pe.Fori(2, NF) as i:
                    gate_up(n0 + 5, i, i * 3 + (n0 + 6 - 6))
                    down(n0 + 7, i - 1, i * 3 + (n0 + 8 - 6))
                down(n0 + 32, NF - 1, n0 + 33, last=True)

            turn("mix0")
            for n in range(6):
                for kh in range(2):
                    c = 2 * n + kh
                    wait_chunk(c + 1)
                    if n >= 2 and kh == 0:
                        pe.wait_ge(qkv_a, n - 1)
                        pe.wait_ge(qkv_v, n - 1)
                    if n == 0:
                        wait_acts("mix0", 2 * kh + 2)
                    for t in range(TT):
                        for k in range(4):
                            ins = product(bank(2 * (n % 2) + t), acts(4 * kh + k, t * P, (t + 1) * P),
                                          cols(slot(c), k * HALF, (k + 1) * HALF),
                                          start=kh == 0 and k == 0, stop=kh == 1 and k == 3)
                    ins.then_inc(w_used, 1)
                if n >= 2:
                    g = n - 2
                    pe.wait_ge(roped, g + 1)
                    if g == 0:
                        wait_acts("mix0")
                    if g >= 2:
                        pe.wait_ge(heads_copied, 2 * (g - 1))
                    for b in range(2):
                        for h in range(2):
                            for t in range(TT):
                                col = g * HALF + (2 * b + h) * HD1
                                ins = nc.tensor.transpose(
                                    bank(4 + 2 * (g % 2) + b, h * T + t * P, h * T + (t + 1) * P),
                                    qk_tok[:, t, col:col + HD1], ident)
                        ins.then_inc(heads_turned, 1)
            pe.wait_ge(heads_copied, 6)

            def qkv_done():
                pe.wait_ge(heads_copied, 8)
                pe.wait_ge(qkv_a, 6)
                pe.wait_ge(qkv_v, 6)

            def keys(t):
                return slice(0, (t + 1) * P)

            attention(moba,
                      lambda h, t, o: nc.tensor.matmul(o, lhsT=qT[:, h, t * P:(t + 1) * P], rhs=kT[:, h, keys(t)],
                                                       start=True, stop=True),
                      lambda h, k: V[:, k, h * HD1:(h + 1) * HD1], AT["wo"], QUARTERS)
            turn("mlp0")
            mlp_layer(mlp[0], "mlp0")

            pe.wait_ge(masks_loaded, 16)
            for kk in range(KT):
                if kk % 4 == 0:
                    pe.wait_ge(xs_ready, 4 * XSR["mix1"] + 2 + 2 * (kk // 4))
                g = kk // 2
                o = bank(4 + kk // 2, (kk % 2) * T, (kk % 2 + 1) * T)
                band = C_BAND + g * 3 * P
                nc.tensor.matmul(o, lhsT=xs[:, 0, kk * P:(kk + 1) * P], rhs=const[:, band:band + T],
                                 start=True, stop=False)
                ins = nc.tensor.matmul(o[:, P:T], lhsT=xs[:, 1, kk * P:(kk + 1) * P],
                                       rhs=const[:, band + T:band + T + P], start=False, stop=True)
                if kk % 2:
                    ins.then_inc(pooled, 1)
            c = AT["pool"]
            wait_chunk(c + 1)
            for n, (h, t) in enumerate(QUARTERS):
                wait_acts("mix1", 2 * h + 2)
                for g in (2 * h, 2 * h + 1):
                    for k in range(2):
                        ins = product(bank(2 * t + h, (g % 2) * FC, (g % 2 + 1) * FC),
                                      acts(2 * g + k, t * P, (t + 1) * P),
                                      cols(slot(c), (2 * g + k) * FC, (2 * g + k + 1) * FC),
                                      start=k == 0, stop=k == 1)
                ins.then_inc(pool_part if n < 3 else w_used, 1)
            turn("mlp1")
            mlp_layer(mlp[1], "mlp1")

            turn("pre0")
            for t in range(TT):
                for j in range(4):
                    c = AT["wa"] + j
                    wait_chunk(c + 1)
                    if j % 2 == 0:
                        wait_acts("pre0", 2 + j)
                    for k in range(2):
                        for b, (lo, hi) in enumerate(((0, 352), (352, 704))):
                            at = (2 * t + 1) * HALF + (b - 1) * 352
                            ins = product(ps[:, at:at + 352], acts(2 * j + k, t * P, (t + 1) * P),
                                          cols(slot(c), k * 704 + lo, k * 704 + hi),
                                          start=j == 0 and k == 0, stop=j == 3 and k == 1, skip_group_check=True)
                    if t == 1:
                        ins.then_inc(w_used, 1)
                if t == 0:
                    ins.then_inc(acc_wa, 1)
            turn("lora", blocks=((0, 4), (4, 6)))
            wait_acts("lora")
            pe.wait_ge(kr_copied, 2)

            pe.wait_ge(lora_a, 1)
            pe.wait_ge(lora_v, 1)
            c = AT["uqr"]
            wait_chunk(c + 1)
            for t in range(TT):
                for k in range(3):
                    ins = product(bank(2 + t), acts(k, t * P, (t + 1) * P),
                                  cols(slot(c), k * HALF, (k + 1) * HALF), start=k == 0, stop=k == 2)
            ins.then_inc(w_used, 1)
            for j in range(2):
                c = AT["uq"] + j
                wait_chunk(c + 1)
                for h in range(4):
                    for k in range(3):
                        at = k * HALF + h * P
                        ins = product(bank((0, 6)[j] + h // 2, (h % 2) * T, (h % 2 + 1) * T),
                                      cols(slot(c), at, at + P), acts(k), start=k == 0, stop=k == 2)
                ins.then_inc(w_used, 1)
            pe.wait_ge(qr_roped, 1)
            for j in range(4):
                for t in range(TT):
                    ins = nc.tensor.transpose(bank(4 + j // 2, (j % 2) * T + t * P, (j % 2) * T + (t + 1) * P),
                                              qr_tok[:, t, j * P:(j + 1) * P], ident)
                if j % 2:
                    ins.then_inc(qr_turned, 1)
            for j in range(2):
                c = AT["ukv"] + j
                wait_chunk(c + 1)
                pe.wait_ge(qn_copied, 2)
                pe.wait_ge(qr_copied, 1)
                if j:
                    pe.wait_ge(kn_copied, 2)
                    pe.wait_ge(v_copied, 2)
                for h in range(4):
                    for k in range(2):
                        product(bank(h // 2, (h % 2) * T, (h % 2 + 1) * T),
                                cols(slot(c), k * D + h * 256, k * D + h * 256 + 128), acts(3 + k),
                                start=k == 0, stop=k == 1)
                for t in range(TT):
                    for k in range(2):
                        vals = tuple(w[:, k * D:(k + 1) * D].rearrange("p (h d) -> p h d", d=256)[:, :, 128:256]
                                     for w in slot(c))
                        ins = product(bank(2 + t), acts(3 + k, t * P, (t + 1) * P), vals, start=k == 0, stop=k == 1)
                ins.then_inc(w_used, 1)
            pe.wait_ge(qn_copied, 4)
            pe.wait_ge(qrT_copied, 2)
            pe.wait_ge(kn_copied, 4)
            pe.wait_ge(v_copied, 4)

            def mla_score(h, t, o):
                nc.tensor.matmul(o, lhsT=qT[:, h, t * P:(t + 1) * P], rhs=kT[:, h, keys(t)], start=True, stop=False)
                lo = 64 * (h % 2)
                return nc.tensor.matmul(o, lhsT=qrT[lo:lo + 64, h // 2, t * P:(t + 1) * P],
                                        rhs=krT[lo:lo + 64, keys(t)], start=False, stop=True)

            attention(mla, mla_score, lambda h, k: V[:, k, h * HD1:(h + 1) * HD1], AT["mwo"], TILES)
            turn("fpre0")
            ffn_layer(ffn[0], "fpre0")

            turn("kvsrc")
            for j in range(4):
                c = AT["kvk"] + j
                wait_chunk(c + 1)
                if j >= 2:
                    pe.wait_ge(kT_copied, j - 1)
                tiles_out(slot(c), 4 + j % 2, "kvsrc" if j == 0 else None).then_inc(w_used, 1)
                if j == 0:
                    spread_scales("kvsrc")
            for n in range(2):
                for kh in range(2):
                    c = AT["kvv"] + 2 * n + kh
                    wait_chunk(c + 1)
                    for t in range(TT):
                        for k in range(4):
                            ins = product(bank(2 * n + t), acts(4 * kh + k, t * P, (t + 1) * P),
                                          cols(slot(c), k * HALF, (k + 1) * HALF),
                                          start=kh == 0 and k == 0, stop=kh == 1 and k == 3)
                    ins.then_inc(w_used, 1)
            pe.wait_ge(kT_copied, 4)
            turn("pre1")
            for j in range(4):
                c = AT["bq"] + j
                wait_chunk(c + 1)
                if j >= 2:
                    pe.wait_ge(qT_copied, j - 1)
                tiles_out(slot(c), 4 + j % 2, "pre1" if j == 0 else None).then_inc(w_used, 1)
            pe.wait_ge(qT_copied, 4)
            pe.wait_ge(vs_copied, 2)
            pe.wait_ge(v_copied, 6)

            def chunk_score(h, t, o):
                lo = 64 * (h % 2)
                return nc.tensor.matmul(o, lhsT=qT[lo:lo + 64, h // 2, t * P:(t + 1) * P],
                                        rhs=kT[lo:lo + 64, h // 2, keys(t)], start=True, stop=True)

            attention(chk, chunk_score, lambda h, k: V2[:, k, h * 64:(h + 1) * 64], AT["bwo"], TILES)
            turn("fpre1")
            ffn_layer(ffn[1], "fpre1")


NAMES = ["x", "positions", "norm_mix", "norm_mlp", "attn_w_qkv", "attn_w_o", "pool_w", "pool_scale",
         "mlp_w_up", "mlp_w_down", "norm_final", "positions_2", "attn_pre_g_2", "attn_post_g_2",
         "ffn_pre_g_2", "ffn_post_g_2", "ffn_w_gate_2", "ffn_w_up_2", "ffn_w_down_2", "mla_w_a_2",
         "mla_g_q_2", "mla_w_uq_2", "mla_g_kv_2", "mla_w_ukv_2", "mla_w_o_2", "kv_src_g_2",
         "w_kv_shared_2", "b_w_q_2", "b_rel_table_2", "b_w_o_2"]


def constants():
    import numpy as np

    c = np.zeros((P, NCONST), np.float32)
    c[:, C_IDENT:C_IDENT + P] = np.eye(P)
    q = np.arange(P)[:, None]
    k = np.arange(P)[None, :]
    c[:, C_CAUSAL + P:C_CAUSAL + T] = np.where(k <= q, 0.0, NEG)
    c[:, C_CHUNKED + P:C_CHUNKED + T] = np.where(k // 64 <= q // 64, 0.0, NEG)
    s = np.arange(T)[:, None]
    t = np.arange(T)[None, :]
    for g, w in enumerate((2, 4, 8, 16)):
        band = np.where((s <= t) & (s > t - w), 1.0 / np.minimum(t + 1, w), 0.0) - (s == t)
        at = C_BAND + g * 3 * P
        c[:, at:at + T] = band[0:P]
        c[:, at + T:at + T + P] = band[P:T, P:T]
    c[:, C_ONES:C_ONES + P] = 1.0
    c[:, C_INV:C_INV + ROT1] = np.float32(500000.0) ** (-np.arange(0, 32, 2, dtype=np.float32) / np.float32(32))
    c[:, C_INV + ROT1:C_CAUSAL] = 1.0 / (np.float32(10000.0) ** (np.arange(0, 64, 2, dtype=np.float32) / np.float32(64)))
    return c


def kernel(**inputs):
    import numpy as np
    import concourse.bacc as bacc
    from concourse.bass_utils import run_bass_kernel_spmd

    nc = bacc.Bacc("TRN2", target_bir_lowering=False, num_devices=1)
    arrays, aps = {}, {}

    def give(name, array):
        arrays[name + "_in"] = array
        aps[name] = nc.dram_tensor(name + "_in", array.shape, mybir.dt.from_np(array.dtype),
                                   kind="ExternalInput").ap()

    for name in NAMES:
        give(name, np.ascontiguousarray(inputs[name]))
    give("const", constants())
    out = nc.dram_tensor("y_out", (1, T, D), F32, kind="ExternalOutput").ap()
    two_blocks(nc, aps, out)
    r = run_bass_kernel_spmd(nc, [arrays], core_ids=[0])
    return r.results[0]["y_out"]
```
